# Optimizing a Trainium2 kernel written in Bass

```python
import math
import jax, jax.numpy as jnp
from jax import lax
import numpy as np

D_MODEL = 1024
BATCH = 1
SEQ = 2048
DEPTH = 1

EXPAND = 2
MIX_W = EXPAND * D_MODEL
POOL_W = MIX_W // 2
POOL_WINDOWS = (2, 4, 8, 16)
N_POOL_GROUPS = len(POOL_WINDOWS)
POOL_G = POOL_W // N_POOL_GROUPS
DN_W = MIX_W - POOL_W
HEAD_DIM = 128
N_HEADS = DN_W // HEAD_DIM
N_DIRS = 2
CONV_K = 5
CHUNK = 64
EPS = 1e-6
OFF_UP = 0
OFF_ZP = OFF_UP + POOL_W
OFF_QKV = OFF_ZP + POOL_W
OFF_ZD = OFF_QKV + 3 * DN_W
OFF_B = OFF_ZD + DN_W
OFF_A = OFF_B + N_DIRS * N_HEADS
IN_W = OFF_A + N_DIRS * N_HEADS

kernel_name = "hybrid_pool_gated_deltanet_bidir"

def rmsnorm(x, w):
    xf = x.astype(jnp.float32)
    y = xf * lax.rsqrt(jnp.mean(xf * xf, axis=-1, keepdims=True) + EPS)
    return (y * w.astype(jnp.float32)).astype(x.dtype)

def l2norm(x):
    return x * lax.rsqrt(jnp.sum(x * x, axis=-1, keepdims=True) + EPS)

def pool_mixer(u, pool_w, pool_scale):
    b, s, _ = u.shape
    uf = u.astype(jnp.float32)
    cs = jnp.concatenate([jnp.zeros((b, 1, POOL_W), jnp.float32), jnp.cumsum(uf, axis=1)], axis=1)
    t = np.arange(s)
    outs = []
    for gi, w in enumerate(POOL_WINDOWS):
        left = w // 2
        right = w - 1 - left
        lo = np.maximum(t - left, 0)
        hi = np.minimum(t + right, s - 1)
        cnt = jnp.asarray((hi - lo + 1).astype(np.float32))
        csg = cs[..., gi * POOL_G:(gi + 1) * POOL_G]
        mean = (csg[:, hi + 1] - csg[:, lo]) / cnt[None, :, None]
        outs.append(mean - uf[..., gi * POOL_G:(gi + 1) * POOL_G])
    m = jnp.stack(outs, axis=2).astype(u.dtype)
    y = jnp.einsum('bsgc,gcd->bsgd', m, pool_w).reshape(b, s, POOL_W)
    return y * pool_scale

def gated_delta_chunked(q, k, v, g, beta):
    b, s, h, dk = q.shape
    dv = v.shape[-1]
    n = s // CHUNK
    q = l2norm(q) * (dk ** -0.5)
    k = l2norm(k)

    def blk(t):
        return t.reshape(b, n, CHUNK, h, -1).transpose(0, 3, 1, 2, 4)

    q, k, v = blk(q), blk(k), blk(v)
    g = g.reshape(b, n, CHUNK, h).transpose(0, 3, 1, 2)
    beta = beta.reshape(b, n, CHUNK, h).transpose(0, 3, 1, 2)
    gc = jnp.cumsum(g, axis=-1)
    tril = jnp.tril(jnp.ones((CHUNK, CHUNK), bool))
    strict = jnp.tril(jnp.ones((CHUNK, CHUNK), bool), -1)
    diff = gc[..., :, None] - gc[..., None, :]
    decay = jnp.where(tril, jnp.exp(jnp.where(tril, diff, 0.0)), 0.0)
    kb = k * beta[..., None]
    lmat = jnp.where(strict, jnp.einsum('bhncd,bhnsd->bhncs', kb, k) * decay, 0.0)
    eye = jnp.eye(CHUNK, dtype=jnp.float32)
    tinv = lax.linalg.triangular_solve(eye + lmat, jnp.broadcast_to(eye, lmat.shape),
                                       left_side=True, lower=True, unit_diagonal=True)
    u = jnp.einsum('bhncs,bhnsd->bhncd', tinv, v * beta[..., None])
    w = jnp.einsum('bhncs,bhnsd->bhncd', tinv, kb * jnp.exp(gc)[..., None])
    a_intra = jnp.einsum('bhncd,bhnsd->bhncs', q, k) * decay

    def step(state, inp):
        q_c, k_c, u_c, w_c, gc_c, a_c = inp
        v_new = u_c - jnp.einsum('bhcd,bhde->bhce', w_c, state)
        o = (jnp.einsum('bhcd,bhde->bhce', q_c * jnp.exp(gc_c)[..., None], state)
             + jnp.einsum('bhcs,bhse->bhce', a_c, v_new))
        g_last = gc_c[..., -1]
        state = (state * jnp.exp(g_last)[..., None, None]
                 + jnp.einsum('bhcd,bhce->bhde', k_c * jnp.exp(g_last[..., None] - gc_c)[..., None], v_new))
        return state, o

    mv = lambda t: jnp.moveaxis(t, 2, 0)
    xs = (mv(q), mv(k), mv(u), mv(w), mv(gc), mv(a_intra))
    s0 = jnp.zeros((b, h, dk, dv), jnp.float32)
    _, o = lax.scan(step, s0, xs)
    return o.transpose(1, 0, 3, 2, 4).reshape(b, s, h, dv)

def deltanet_mixer(qkv, b_logit, a_logit, conv_w, a_log, dt_bias, head_norm_w, z):
    bsz, s, _ = qkv.shape
    c = 3 * DN_W
    qkv = lax.conv_general_dilated(qkv, conv_w.astype(qkv.dtype).reshape(CONV_K, 1, c), window_strides=(1,),
                                   padding=[(CONV_K // 2, CONV_K // 2)],
                                   dimension_numbers=('NWC', 'WIO', 'NWC'), feature_group_count=c)
    qkv = jax.nn.silu(qkv).astype(jnp.float32)
    q, k, v = jnp.split(qkv, 3, axis=-1)
    q = q.reshape(bsz, s, N_HEADS, HEAD_DIM)
    k = k.reshape(bsz, s, N_HEADS, HEAD_DIM)
    v = v.reshape(bsz, s, N_HEADS, HEAD_DIM)
    beta = jax.nn.sigmoid(b_logit.astype(jnp.float32))
    g = -jnp.exp(a_log.astype(jnp.float32)) * jax.nn.softplus(a_logit.astype(jnp.float32) + dt_bias.astype(jnp.float32))
    o_f = gated_delta_chunked(q, k, v, g[:, :, 0], beta[:, :, 0])
    fl = lambda t: jnp.flip(t, axis=1)
    o_b = fl(gated_delta_chunked(fl(q), fl(k), fl(v), fl(g[:, :, 1]), fl(beta[:, :, 1])))
    o = (o_f + o_b).astype(z.dtype)
    o = rmsnorm(o, head_norm_w).reshape(bsz, s, DN_W)
    return o * jax.nn.silu(z)

def setup_inputs(seed: int = 0) -> dict:
    key = jax.random.key(seed)
    ks = jax.random.split(key, 12)
    f32 = jnp.float32
    x = jax.random.normal(ks[0], (BATCH, SEQ, D_MODEL), f32)
    norm_w = 1.0 + 0.1 * jax.random.normal(ks[1], (DEPTH, D_MODEL), f32)
    w_in = jax.random.normal(ks[2], (DEPTH, D_MODEL, IN_W), f32) * D_MODEL ** -0.5
    pool_w = jax.random.normal(ks[3], (DEPTH, N_POOL_GROUPS, POOL_G, POOL_G), f32) * POOL_G ** -0.5
    pool_scale = 1.0 + 0.1 * jax.random.normal(ks[4], (DEPTH, POOL_W), f32)
    conv_w = jax.random.normal(ks[5], (DEPTH, CONV_K, 3 * DN_W), f32) * CONV_K ** -0.5
    a_log = jnp.log(jax.random.uniform(ks[6], (DEPTH, N_DIRS, N_HEADS), f32, 1.0, 16.0))
    dt = jnp.exp(jax.random.uniform(ks[7], (DEPTH, N_DIRS, N_HEADS), f32, math.log(1e-3), math.log(1e-1)))
    dt_bias = dt + jnp.log(-jnp.expm1(-dt))
    head_norm_w = 1.0 + 0.1 * jax.random.normal(ks[8], (DEPTH, HEAD_DIM), f32)
    w_out = jax.random.normal(ks[9], (DEPTH, MIX_W, D_MODEL), f32) * (MIX_W ** -0.5) * 0.5
    final_norm_w = 1.0 + 0.1 * jax.random.normal(ks[10], (D_MODEL,), f32)
    return {"x": x, "norm_w": norm_w, "w_in": w_in, "pool_w": pool_w, "pool_scale": pool_scale,
            "conv_w": conv_w, "a_log": a_log, "dt_bias": dt_bias, "head_norm_w": head_norm_w,
            "w_out": w_out, "final_norm_w": final_norm_w}

def reference(x, norm_w, w_in, pool_w, pool_scale, conv_w, a_log, dt_bias, head_norm_w, w_out, final_norm_w):
    bsz, s, _ = x.shape
    for l in range(DEPTH):
        h = rmsnorm(x, norm_w[l])
        proj = jnp.einsum('bsd,de->bse', h, w_in[l])
        u_p = proj[..., OFF_UP:OFF_ZP]
        z_p = proj[..., OFF_ZP:OFF_QKV]
        qkv = proj[..., OFF_QKV:OFF_ZD]
        z_d = proj[..., OFF_ZD:OFF_B]
        b_logit = proj[..., OFF_B:OFF_A].reshape(bsz, s, N_DIRS, N_HEADS)
        a_logit = proj[..., OFF_A:IN_W].reshape(bsz, s, N_DIRS, N_HEADS)
        y_pool = pool_mixer(u_p, pool_w[l], pool_scale[l]) * jax.nn.silu(z_p)
        y_dn = deltanet_mixer(qkv, b_logit, a_logit, conv_w[l], a_log[l], dt_bias[l], head_norm_w[l], z_d)
        y = jnp.einsum('bse,ed->bsd', jnp.concatenate([y_pool, y_dn], axis=-1), w_out[l])
        x = x + y
    return rmsnorm(x, final_norm_w)


_drawn_inputs = setup_inputs


def setup_inputs(seed=0):
    import zlib

    import numpy as np

    out = dict(_drawn_inputs(seed))
    spreads = {}
    factors = {'pool_scale': 3.208, 'head_norm_w': 2.985}
    for name, (base, spread) in spreads.items():
        noise = np.random.default_rng([zlib.crc32(name.encode()), seed]).standard_normal(out[name].shape)
        drawn = base * np.exp(spread * noise) if base else spread * noise
        out[name] = __import__('jax').numpy.asarray(drawn.astype(out[name].dtype))
    for name, factor in factors.items():
        out[name] = (out[name] * factor).astype(out[name].dtype)
    return out
```

```python
from contextlib import ExitStack

import numpy as np
import concourse.bass as bass
import concourse.mybir as mybir

F32 = mybir.dt.float32
F32R = mybir.dt.float32r
ACT = mybir.ActivationFunctionType
ALU = mybir.AluOpType
AX = mybir.AxisListType

P = 128
D = 1024
SEQ = 2048
KT = D // P
NT = SEQ // P
TB = 512
NB = SEQ // TB
POOL_W = 1024
H = 8
CONV_K = 5
EPS = 1e-6
OFF_ZP = 1024
OFF_QKV = 2048
OFF_LOGITS = 6144
IN_W = 6176
MIX_W = 2048
WINDOWS = (2, 4, 8, 16)

J_QK, J_V, J_ZD, J_ZP, J_U, J_LG, J_END = 0, 16, 24, 32, 40, 48, 49
PAD = 8
CW = SEQ + 2 * PAD

LEVELS = (2, 4, 8, 16, 32, 64)
BIG = -1.0e30


def constant_layout():
    at, out = 0, {}
    for name, n in (("ident", P), ("edge", 4 * 2 * PAD), ("tri_f", P), ("tri_b", P), ("ones", P), ("mask_f", P), ("mask_b", P),
                    ("neg1_f", P), ("neg1_b", P), ("level_f", 64 * len(LEVELS)), ("level_b", 64 * len(LEVELS))):
        out[name] = (at, at + n)
        at += n
    return out, at


CL, CN = constant_layout()
CN_EARLY = CL["edge"][1]


def constant_table():
    t = np.zeros((P, CN), np.float32)

    def put(name, a):
        t[:, CL[name][0]:CL[name][1]] = a

    r, c = np.arange(P)[:, None], np.arange(P)[None, :]
    put("ident", r == c)
    put("tri_f", r <= c)
    put("tri_b", r >= c)
    put("ones", 1.0)
    put("mask_f", np.where(c >= r, 0.0, BIG))
    put("mask_b", np.where(c <= r, 0.0, BIG))
    put("neg1_f", -((r % 2 == 0) & (c == r + 1)).astype(np.float32))
    put("neg1_b", -((r % 2 == 1) & (c == r - 1)).astype(np.float32))
    f, b = [], []
    for s in LEVELS:
        even = np.array([x for x in range(P) if (x // s) % 2 == 0])[None, :]
        odd = np.array([x for x in range(P) if (x // s) % 2 == 1])[None, :]
        f.append(r // s == even // s + 1)
        b.append(r // s == odd // s - 1)
    put("level_f", np.concatenate(f, 1))
    put("level_b", np.concatenate(b, 1))
    e = np.ones((4, 2, PAD), np.float32)
    for g, w in enumerate(WINDOWS):
        for n in range(PAD):
            for side, tok in ((0, n), (1, SEQ - PAD + n)):
                lo, hi = max(tok - w // 2, 0), min(tok + w // 2 - 1, SEQ - 1)
                e[g, side, n] = w / (hi - lo + 1)
    put("edge", e.reshape(1, -1))
    return t


def stage_prepare(nc, a, sh):
    with ExitStack() as es:
        sb = lambda name, shape, dt=F32: es.enter_context(nc.sbuf_tensor("pr_" + name, shape, dt))
        sem = lambda name: sh.es.enter_context(nc.semaphore("pr_" + name))
        xin = [sb(f"xin{b}", [P, D]) for b in range(2)]
        xs = [sb(f"xs{b}", [P, D]) for b in range(2)]
        ht = [sb(f"ht{b}", [P, KT, P]) for b in range(2)]
        junk = sb("junk", [P, D])
        stat = sb("stat", [P, 2, 4])
        rows = sb("rows", [P, P])
        rows2 = sb("rows2", [16, P])
        eps = sb("eps", [P, 1])
        consts_in, rows_in = sem("consts_in"), sem("rows_in")
        x_in = [sem(f"x_in{b}") for b in range(2)]
        x_scaled, ssq, std, rstd = sem("x_scaled"), sem("ssq"), sem("std"), sem("rstd")
        x_t, ht_half, hi, lo, cols_t, cols = sem("x_t"), sem("ht_half"), sem("hi"), sem("lo"), sem("cols_t"), sem("cols")
        eps_set = sem("eps_set")
        ps = sh.ps
        ident = sh.const("ident")

        with nc.Block() as block:
            @block.sync
            def _(sp):
                sp.dma_start(sh.consts[:, :], a["consts"][:, 0:CN_EARLY]).then_inc(consts_in, 16)
                sp.dma_start(rows[0:120, :], a["conv_w"].rearrange("o k (t p) -> (o k t) p", p=P)).then_inc(rows_in, 16)
                sp.dma_start(rows[120:128, :], a["norm_w"].rearrange("o (t p) -> (o t) p", p=P)).then_inc(rows_in, 16)
                sp.dma_start(rows2[0:8, :], a["pool_scale"].rearrange("o (t p) -> (o t) p", p=P)).then_inc(rows_in, 16)
                sp.dma_start(rows2[8:9, :], a["head_norm_w"]).then_inc(rows_in, 16)

                def load(t, b, first):
                    if not first:
                        sp.wait_ge(x_scaled, t - 1)
                    sp.dma_start(xin[b][:, :], a["x"][0, bass.ds(t * P, P), :]).then_inc(x_in[b], 16)

                load(0, 0, True)
                load(1, 1, True)
                with sp.Fori(1, NT // 2) as i:
                    load(i * 2, 0, False)
                    load(i * 2 + 1, 1, False)

            @block.scalar
            def _(act):
                act.wait_ge(eps_set, 1)

                def tile(i, b, first):
                    t = i * 2 + b
                    act.wait_ge(x_in[b], (i + 1) * 16)
                    act.wait_ge(ssq, t)
                    act.activation(junk[:, :], xin[b][:, :], ACT.Square,
                                   accum_out=stat[:, b, 0:1]).then_inc(ssq, 1)
                    act.wait_ge(ssq, t + 1)
                    act.activation(stat[:, b, 1:2], stat[:, b, 0:1], ACT.Sqrt, bias=eps[:, :],
                                   scale=1.0 / D).then_inc(std, 1)
                    act.wait_ge(rstd, t + 1)
                    if not first:
                        act.wait_ge(x_t, t - 1)
                    act.activation(xs[b][:, :], xin[b][:, :], ACT.Copy,
                                   scale=stat[:, b, 2:3]).then_inc(x_scaled, 1)
                    act.wait_ge(ht_half, t * 2 + 2)
                    act.activation(sh.xh[:, :, bass.ds(t * P, P)], ht[b][:, :, :], ACT.Copy).then_inc(hi, 1)

                tile(0, 0, True)
                tile(0, 1, True)
                with act.Fori(1, NT // 2) as i:
                    tile(i, 0, False)
                    tile(i, 1, False)

            @block.tensor
            def _(pe):
                pe.wait_ge(consts_in, 16)
                pe.wait_ge(rows_in, 64)
                pe.transpose(ps[4][:, 0:P], rows[:, :], ident).then_inc(cols_t, 1)
                pe.transpose(ps[5][:, 0:9], rows2[0:9, :], ident[0:9, 0:9]).then_inc(cols_t, 1)

                def tile(t, b, first):
                    pe.wait_ge(x_scaled, t + 1)
                    if not first:
                        pe.wait_ge(ht_half, t * 2 - 2)
                    for k in range(KT):
                        last = pe.transpose(ps[2 * b + k // 4][:, (k % 4) * P:(k % 4 + 1) * P],
                                            xs[b][:, k * P:(k + 1) * P], ident)
                    last.then_inc(x_t, 1)

                tile(0, 0, True)
                tile(1, 1, True)
                with pe.Fori(1, NT // 2) as i:
                    tile(i * 2, 0, False)
                    tile(i * 2 + 1, 1, False)

            @block.vector
            def _(dve):
                dve.memset(eps[:, :], EPS).then_inc(eps_set, 1)
                dve.wait_ge(cols_t, 2)
                dve.tensor_copy(sh.cols[:, 0:P], ps[4][:, 0:P]).then_inc(cols, 1)
                dve.tensor_copy(sh.cols[:, P:P + 9], ps[5][:, 0:9]).then_inc(cols, 1)
                dve.wait_ge(cols, 2)

                def tile(t, b, first):
                    dve.wait_ge(std, t + 1)
                    dve.reciprocal(stat[:, b, 2:3], stat[:, b, 1:2]).then_inc(rstd, 1)
                    dve.wait_ge(x_t, t + 1)
                    if not first:
                        dve.wait_ge(lo, t - 1)
                    for half in range(2):
                        nw = sh.cols[:, 120 + 4 * half:124 + 4 * half].unsqueeze(2).broadcast_to((P, 4, P))
                        dve.tensor_tensor(ht[b][:, 4 * half:4 * half + 4, :],
                                          ps[2 * b + half][:, :].rearrange("p (k t) -> p k t", t=P),
                                          nw, ALU.mult).then_inc(ht_half, 1)

                tile(0, 0, True)
                tile(1, 1, True)
                with dve.Fori(1, NT // 2) as i:
                    tile(i * 2, 0, False)
                    tile(i * 2 + 1, 1, False)

            @block.gpsimd
            def _(pool):
                def tile(t, b):
                    pool.wait_ge(hi, t + 1)
                    pool.tensor_tensor(sh.xl[:, :, bass.ds(t * P, P)], ht[b][:, :, :],
                                       sh.xh[:, :, bass.ds(t * P, P)].bitcast(F32), ALU.subtract).then_inc(lo, 1)

                with pool.Fori(0, NT // 2) as i:
                    tile(i * 2, 0)
                    tile(i * 2 + 1, 1)


def held(eng, v, most):
    if isinstance(v, int):
        return v
    reg = eng.alloc_register()
    eng.reg_mov(reg, v)
    return eng.snap(reg, min_val=0, max_val=most)


def tile_columns(j):
    if isinstance(j, int):
        if j >= J_LG:
            return IN_W - P
        if j >= J_U:
            return (j - J_U) * P
        if j >= J_ZP:
            return OFF_ZP + (j - J_ZP) * P
        return OFF_QKV + j * P
    raise TypeError(j)


def stage_project(nc, a, sh):
    with ExitStack() as es:
        sb = lambda name, shape, dt=F32: es.enter_context(nc.sbuf_tensor("pj_" + name, shape, dt))
        sem = lambda name: sh.es.enter_context(nc.semaphore("pj_" + name))
        w_raw = [sb(f"w_raw{b}", [P, KT, P]) for b in range(2)]
        w_hi = [sb(f"w_hi{b}", [P, KT, P], F32R) for b in range(2)]
        w_lo = [sb(f"w_lo{b}", [P, KT, P], F32R) for b in range(2)]
        row = [sb(f"row{b}", [P, CW]) for b in range(2)]
        acc = [sb(f"acc{b}", [P, CW]) for b in range(2)]
        act_row = [sb(f"act_row{b}", [P, SEQ]) for b in range(2)]
        w_in_sem = [sem(f"w_loaded{b}") for b in range(2)]
        stored = [sem(f"stored{b}") for b in range(2)]
        hi_done, lo_done, projected, evacuated = sem("hi_done"), sem("lo_done"), sem("projected"), sem("evacuated")
        padded, tap, row_free, silu_done, sq_done = sem("padded"), sem("tap"), sem("row_free"), sem("silu_done"), sem("sq_done")
        row_done, ss_done, ss_out = sem("row_done"), sem("ss_done"), sem("ss_out")
        window = sem("window")
        lg_t, lg_out = sem("lg_t"), sem("lg_out")
        ps, ident = sh.ps, sh.const("ident")

        segments = [(J_QK, J_V, "qk", 4), (J_V, J_ZD, "v", 2), (J_ZD, J_ZP, "z", 2), (J_ZP, J_U, "z", 2),
                    (J_U, J_LG, "u", 2), (J_LG, J_END, "lg", 1)]

        def each_tile(eng, step, parts=segments):
            for j0, j1, kind, peel in parts:
                for j in range(j0, j0 + peel):
                    step(j, j // 2, j % 2, j0, kind, j < 2)
                if j1 - j0 > peel:
                    with eng.Fori((j0 + peel) // 2, j1 // 2) as n:
                        step(n * 2, n, 0, j0, kind, False)
                        step(n * 2 + 1, n, 1, j0, kind, False)

        def at(j, n):
            return isinstance(j, int) and j == n

        def columns(j, j0):
            return tile_columns(j0) + (j - j0) * P

        with nc.Block() as block:
            @block.sync
            def _(sp):
                def load(j, pair, b, j0, first):
                    if not first:
                        sp.wait_ge(lo_done, j - 1)
                    w = a["w_in"][0, :, bass.ds(columns(j, j0), P)].rearrange("(k p) n -> p k n", p=P)
                    sp.dma_start(w_raw[b][:, :, :], w).then_inc(w_in_sem[b], 16)

                def store(j, b, kind):
                    if kind in ("qk", "v"):
                        sp.wait_ge(silu_done, j + 1)
                    elif kind == "z":
                        sp.wait_ge(evacuated, (j + 1) * NB)
                    else:
                        sp.wait_ge(row_free, j - J_U + 1)
                    sp.dma_start(sh.rows[bass.ds(j, 1), :, :].rearrange("o p t -> (o p) t"),
                                 act_row[b][:, :]).then_inc(stored[b], 16)

                def step(j, pair, b, j0, kind, first):
                    load(j, pair, b, j0, first)
                    if not first:
                        before = [s[2] for s in segments if s[0] < j0][-1:] if at(j, j0) or at(j, j0 + 1) else [kind]
                        store(j - 2, b, before[0])

                each_tile(sp, step)
                store(J_LG - 1, 1, "u")
                for b in range(2):
                    sp.wait_ge(stored[b], J_LG // 2 * 16)

            @block.gpsimd
            def _(pool):
                for b in range(2):
                    pool.memset(row[b][:, 0:PAD], 0.0).then_inc(padded, 1)
                    pool.memset(row[b][:, PAD + SEQ:CW], 0.0).then_inc(padded, 1)
                pool.memset(sh.ones[:, :], 1.0).then_inc(padded, 1)

                def step(j, pair, b, j0, kind, first):
                    pool.wait_ge(hi_done, j + 1)
                    pool.tensor_tensor(w_lo[b][:, :, :], w_raw[b][:, :, :], w_hi[b][:, :, :].bitcast(F32),
                                       ALU.subtract).then_inc(lo_done, 1)

                each_tile(pool, step)

            @block.tensor
            def _(pe):
                pe.wait_ge(padded, 5)

                def sums(j, b):
                    pe.wait_ge(sq_done, j + 1)
                    if not (at(j, 0) or at(j, 1)):
                        pe.wait_ge(ss_out, j - 1)
                    for c in range(NT):
                        last = pe.matmul(ps[4 + b][:, c:c + 1], acc[b][:, c * P:(c + 1) * P], sh.ones[:, 0:1],
                                         start=True, stop=True)
                    last.then_inc(ss_done, 1)

                def step(j, pair, b, j0, kind, first):
                    pe.wait_ge(lo_done, j + 1)
                    for t in range(NB):
                        if not at(j, 0):
                            pe.wait_ge(evacuated, j * NB + (t - NB + 1))
                        for k in range(KT):
                            for w, x in ((w_hi, sh.xh), (w_hi, sh.xl), (w_lo, sh.xh)):
                                last = pe.matmul(ps[t][:, :], w[b][:, k, :], x[:, k, t * TB:(t + 1) * TB],
                                                 start=(k == 0 and x is sh.xh and w is w_hi),
                                                 stop=(k == KT - 1 and w is w_lo))
                        last.then_inc(projected, 1)
                        if t == 1:
                            if kind == "qk" and not first:
                                sums(j - 2, b)
                            if kind == "v" and isinstance(j, int):
                                sums(j - 2, b)
                    if kind == "lg":
                        pe.wait_ge(evacuated, (j + 1) * NB)
                        pe.wait_ge(ss_out, J_V)
                        for c in range(NT):
                            last = pe.transpose(ps[4 + c // 4][:, (c % 4) * P:(c % 4 + 1) * P],
                                                act_row[0][:, c * P:(c + 1) * P], ident)
                        last.then_inc(lg_t, 1)

                each_tile(pe, step)

            @block.scalar
            def _(act):
                def split(j, pair, b, first):
                    act.wait_ge(w_in_sem[b], (pair + 1) * 16)
                    if not first:
                        act.wait_ge(projected, (j - 1) * NB)
                    act.activation(w_hi[b][:, :, :], w_raw[b][:, :, :], ACT.Copy).then_inc(hi_done, 1)

                def silu(j, pair, b, kind, first):
                    act.wait_ge(tap, (j + 1) * CONV_K)
                    if not first:
                        act.wait_ge(stored[b], pair * 16)
                    act.activation(act_row[b][:, :], acc[b][:, 0:SEQ], ACT.Silu).then_inc(silu_done, 1)
                    if kind == "qk":
                        act.wait_ge(silu_done, j + 1)
                        act.activation(acc[b][:, 0:SEQ], act_row[b][:, :], ACT.Square).then_inc(sq_done, 1)

                def step(j, pair, b, j0, kind, first):
                    if first and b == 0:
                        split(j, pair, b, True)
                    if not (isinstance(j, int) and j == J_END - 1):
                        split(j + 1, pair + b, 1 - b, first and b == 0)
                    for t in range(NB):
                        act.wait_ge(projected, j * NB + t + 1)
                        if t == 0:
                            if first:
                                pass
                            elif kind in ("qk", "v"):
                                act.wait_ge(tap, (j - 1) * CONV_K)
                            elif kind == "u":
                                if not (at(j, J_U) or at(j, J_U + 1)):
                                    act.wait_ge(row_free, j - J_U - 1)
                            else:
                                act.wait_ge(stored[b], pair * 16)
                        if kind in ("qk", "v", "u"):
                            dst, fn = row[b][:, PAD + t * TB:PAD + (t + 1) * TB], ACT.Copy
                        else:
                            dst, fn = act_row[b][:, t * TB:(t + 1) * TB], ACT.Silu if kind == "z" else ACT.Copy
                        act.activation(dst, ps[t][:, :], fn).then_inc(evacuated, 1)
                    if kind in ("qk", "v") and not at(j, 0) or at(j, J_ZD):
                        prev = "v" if at(j, J_ZD) or kind == "v" and not at(j, J_V) else "qk"
                        silu(j - 1, pair - 1 + b, 1 - b, prev, at(j, 1) or at(j, 2))
                    if kind == "lg":
                        act.wait_ge(lg_t, 1)
                        for n in range(4):
                            act.activation(sh.logits[:, 4 * n:4 * n + 4, :],
                                           ps[4 + n][:, :].rearrange("p (c n) -> p c n", n=P)[:, :, 96:128],
                                           ACT.Copy).then_inc(lg_out, 1)

                each_tile(act, step)

            @block.vector
            def _(dve):
                dve.wait_ge(padded, 4)

                def conv(j, b):
                    dve.wait_ge(evacuated, (j + 1) * NB)
                    for n in range(CONV_K):
                        src = row[b][:, PAD - CONV_K // 2 + n:PAD - CONV_K // 2 + n + SEQ]
                        w = sh.cols[:, bass.ds(j + 24 * n, 1)]
                        if n:
                            dve.wait_ge(tap, j * CONV_K + n)
                            dve.scalar_tensor_tensor(acc[b][:, 0:SEQ], src, w, acc[b][:, 0:SEQ], ALU.mult,
                                                     ALU.add).then_inc(tap, 1)
                        else:
                            dve.tensor_scalar(acc[b][:, 0:SEQ], src, w, None, ALU.mult).then_inc(tap, 1)

                def sums_out(j, b):
                    dve.wait_ge(ss_done, j + 1)
                    dve.tensor_copy(sh.sumsq[:, bass.ds(j, 1), :],
                                    ps[4 + b][:, 0:NT].unsqueeze(1)).then_inc(ss_out, 1)

                n_window = [0]

                def windows(j, b, g):
                    dve.wait_ge(evacuated, (j + 1) * NB)
                    if j > J_U:
                        dve.wait_ge(row_free, j - J_U)
                    w = WINDOWS[g]
                    src, dst, m = row[b], acc[0], 1
                    n = CW - 1

                    def chained(ins):
                        n_window[0] += 1
                        ins.then_inc(window, 1)
                        dve.wait_ge(window, n_window[0])

                    while m < w:
                        chained(dve.tensor_tensor(dst[:, 0:n], src[:, 0:n], src[:, m:m + n], ALU.add))
                        m *= 2
                        n -= m
                        src, dst = dst, acc[1] if dst is acc[0] else acc[0]
                    at = PAD - w // 2
                    for side, p0 in ((0, at), (1, at + SEQ - PAD)):
                        e0 = CL["edge"][0] + (g * 2 + side) * PAD
                        chained(dve.tensor_tensor(src[:, p0:p0 + PAD], src[:, p0:p0 + PAD],
                                                  sh.consts[:, e0:e0 + PAD], ALU.mult))
                    dve.wait_ge(stored[b], (j // 2) * 16)
                    dve.scalar_tensor_tensor(act_row[b][:, :], src[:, at:at + SEQ], 1.0 / w,
                                             row[b][:, PAD:PAD + SEQ], ALU.mult, ALU.subtract).then_inc(row_free, 1)

                def step(j, pair, b, j0, kind, first):
                    if kind == "v" and not isinstance(j, int):
                        dve.wait_ge(silu_done, j - 1)
                    elif not first:
                        dve.wait_ge(ss_done, j - 1)
                    conv(j, b)
                    if kind == "qk" and not at(j, 0) or at(j, J_V):
                        sums_out(j - 1, 1 - b)

                each_tile(dve, step, segments[:2])
                dve.wait_ge(silu_done, J_ZD)
                for j in range(J_U, J_LG):
                    windows(j, j % 2, (j - J_U) // 2)

FIELDS = ("g", "neg_gc", "neg_eg", "e_last", "e_to_last", "w", "norm_k")
NF = len(FIELDS)
GROUPS = 2
HG = H // GROUPS


def stage_gates(nc, a, sh):
    with ExitStack() as es:
        sb = lambda name, shape, dt=F32: es.enter_context(nc.sbuf_tensor("gt_" + name, shape, dt))
        sem = lambda name: sh.es.enter_context(nc.semaphore("gt_" + name))
        rate = sb("rate", [P, 16])
        dt_b = sb("dt_b", [P, 16])
        half = [P, NT, 16]
        x, mag, z, z2, poly, soft, g = (sb(n, half) for n in ("x", "mag", "z", "z2", "poly", "soft", "g"))
        beta = sb("beta", half)
        nk2, nq2 = sb("nk2", [P, NT, H]), sb("nq2", [P, NT, H])
        nk, nq = sb("nk", [P, NT, H]), sb("nq", [P, NT, H])
        tmp = sb("tmp", [P, NT, H])
        gc_s, gl_s = sb("gc_s", [P, 2, NT, H]), sb("gl_s", [P, 2, NT, H])
        params_in, more_in = sem("params_in"), sem("consts_in")
        v, s, mm = sem("vector_step"), sem("scalar_step"), sem("sums")
        ps = sh.ps

        def view(dr, field):
            f = FIELDS.index(field)
            return sh.tables[:, dr, :, :, f, :]

        def by_group(ap):
            return ap.rearrange("p c (g h) -> p c g h", g=GROUPS)

        with nc.Block() as block:
            @block.sync
            def _(sp):
                sp.dma_start(sh.consts_late[:, :], a["consts"][:, CN_EARLY:CN]).then_inc(more_in, 16)
                sp.dma_start(rate[:, :], a["a_log"].rearrange("o d h -> o (d h)").broadcast_to((P, 16))).then_inc(params_in, 16)
                sp.dma_start(dt_b[:, :], a["dt_bias"].rearrange("o d h -> o (d h)").broadcast_to((P, 16))).then_inc(params_in, 16)

            @block.vector
            def _(dve):
                n = [0]

                def then(ins):
                    n[0] += 1
                    ins.then_inc(v, 1)
                    dve.wait_ge(v, n[0])

                tt, ts, stt = dve.tensor_tensor, dve.tensor_scalar, dve.scalar_tensor_tensor
                dve.wait_ge(params_in, 32)
                then(tt(x[:, :, :], sh.logits[:, :, 16:32], dt_b[:, :].unsqueeze(1).broadcast_to((P, NT, 16)), ALU.add))
                then(ts(z[:, :, :], x[:, :, :], -1.0, None, ALU.mult))
                then(tt(mag[:, :, :], x[:, :, :], z[:, :, :], ALU.max))
                then(ts(beta[:, :, :], sh.logits[:, :, 0:16], -80.0, None, ALU.max))
                dve.wait_ge(s, 2)
                then(ts(z[:, :, :], z2[:, :, :], 2.0, None, ALU.add))
                then(dve.reciprocal(z[:, :, :], z[:, :, :]))
                then(tt(z[:, :, :], z2[:, :, :], z[:, :, :], ALU.mult))
                then(tt(z2[:, :, :], z[:, :, :], z[:, :, :], ALU.mult))
                terms = [2.0 / (2 * k + 1) for k in range(8)]
                then(ts(poly[:, :, :], z2[:, :, :], terms[7], terms[6], ALU.mult, ALU.add))
                for k in range(5, -1, -1):
                    then(tt(poly[:, :, :], poly[:, :, :], z2[:, :, :], ALU.mult))
                    then(ts(poly[:, :, :], poly[:, :, :], terms[k], None, ALU.add))
                then(tt(poly[:, :, :], poly[:, :, :], z[:, :, :], ALU.mult))
                then(stt(soft[:, :, :], x[:, :, :], 0.0, poly[:, :, :], ALU.max, ALU.add))
                dve.wait_ge(s, 3)
                then(stt(g[:, :, :], soft[:, :, :], -1.0, rate[:, :].unsqueeze(1).broadcast_to((P, NT, 16)),
                         ALU.mult, ALU.mult))
                sh.g_ready = n[0]
                for dr in range(2):
                    then(dve.tensor_copy(view(dr, "g"), by_group(g[:, :, dr * H:dr * H + H])))
                then(ts(beta[:, :, :], beta[:, :, :], 1.0, None, ALU.add))
                then(dve.reciprocal(beta[:, :, :], beta[:, :, :]))
                then(ts(nk2[:, :, :], sh.sumsq[:, 8:16, :].rearrange("p h c -> p c h"), EPS, None, ALU.add))
                then(ts(nq2[:, :, :], sh.sumsq[:, 0:8, :].rearrange("p h c -> p c h"), EPS, None, ALU.add))
                sh.norms_ready = n[0]
                then(dve.reciprocal(tmp[:, :, :], nk2[:, :, :]))
                for dr in range(2):
                    then(tt(view(dr, "w"), by_group(tmp[:, :, :]), by_group(beta[:, :, dr * H:dr * H + H]), ALU.mult))
                dve.wait_ge(s, 5)
                for dr in range(2):
                    then(dve.tensor_copy(view(dr, "norm_k"), by_group(nk[:, :, :])))
                then(dve.reciprocal(sh.rq[:, :, :], nq[:, :, :]))
                dve.wait_ge(mm, 4)
                for dr in range(2):
                    then(dve.tensor_copy(gc_s[:, dr, :, :], ps[dr][:, 0:P].rearrange("p (c h) -> p c h", h=H)))
                    then(tt(gl_s[:, dr, :, :], ps[2 + dr][:, 0:P].rearrange("p (c h) -> p c h", h=H),
                            gc_s[:, dr, :, :], ALU.subtract))
                    then(ts(view(dr, "neg_gc"), by_group(gc_s[:, dr, :, :]), -1.0, None, ALU.mult))
                sh.sums_ready = n[0]
                dve.wait_ge(s, 11)
                for dr in range(2):
                    then(ts(view(dr, "neg_eg"), by_group(gc_s[:, dr, :, :]), -1.0, None, ALU.mult))
                    then(dve.tensor_copy(view(dr, "e_last"), by_group(gl_s[:, dr, :, :])))

            @block.scalar
            def _(act):
                act.wait_ge(v, 3)
                act.activation(z2[:, :, :], mag[:, :, :], ACT.Exp, scale=-1.0).then_inc(s, 1)
                act.wait_ge(v, 4)
                act.activation(beta[:, :, :], beta[:, :, :], ACT.Exp, scale=-1.0).then_inc(s, 1)
                act.activation(rate[:, :], rate[:, :], ACT.Exp).then_inc(s, 1)
                act.wait_ge(v, sh.norms_ready)
                act.activation(nk[:, :, :], nk2[:, :, :], ACT.Sqrt).then_inc(s, 1)
                act.activation(nq[:, :, :], nq2[:, :, :], ACT.Sqrt).then_inc(s, 1)
                act.wait_ge(v, sh.sums_ready)
                for dr in range(2):
                    act.activation(view(dr, "e_to_last"), by_group(gl_s[:, dr, :, :]), ACT.Exp).then_inc(s, 1)
                    act.wait_ge(s, 6 + 3 * dr)
                    act.activation(gc_s[:, dr, :, :], gc_s[:, dr, :, :], ACT.Exp).then_inc(s, 1)
                    act.activation(gl_s[:, dr, :, :], ps[2 + dr][:, 0:P].rearrange("p (c h) -> p c h", h=H),
                                   ACT.Exp).then_inc(s, 1)

            @block.tensor
            def _(pe):
                pe.wait_ge(v, sh.g_ready)
                pe.wait_ge(more_in, 16)
                for dr, tri in ((0, "tri_f"), (1, "tri_b")):
                    gd = g[:, :, dr * H:dr * H + H]
                    pe.matmul(ps[dr][:, 0:P], sh.late(tri), gd, start=True, stop=True).then_inc(mm, 1)
                    pe.matmul(ps[2 + dr][:, 0:P], sh.late("ones"), gd, start=True, stop=True).then_inc(mm, 1)


def stage_delta(nc, a, sh):
    with ExitStack() as es:
        sb = lambda name, shape, dt=F32: es.enter_context(nc.sbuf_tensor("dl_" + name, shape, dt))
        sems = lambda name: [sh.es.enter_context(nc.semaphore(f"dl_{name}_{d}")) for d in "fb"]
        quad = [P, HG, P]
        pair = lambda name, shape=quad: [sb(f"{name}_{d}", shape) for d in "fb"]
        pairs = lambda name, shape=quad: [pair(f"{name}{g}", shape) for g in range(GROUPS)]
        qkv = pairs("qkv", [P, 3, HG, P])
        cur = pairs("cur", [P, NF, HG])
        arg, dmat, eb, lt, tm = pair("arg"), pair("dmat"), pair("eb"), pair("lt"), pair("tm")
        at_, xm, kd, vp, qs, ost = pairs("at"), pairs("xm"), pairs("kd"), pairs("vp"), pairs("qs"), pairs("ost")
        state = pairs("state")
        mm = [pair(f"m{s}") for s in LEVELS]
        r, zs = pair("r"), pair("zs")

        loaded = [sems(f"loaded{g}") for g in range(GROUPS)]
        stored = [sems(f"stored{g}") for g in range(GROUPS)]
        cleared = sems("cleared")
        cur_ready, gcb_ps, arg_done, eb_done, d_done = map(sems, ("cur_ready", "gcb_ps", "arg_done", "eb_done", "d_done"))
        kk_ps, kq_ps, kt_ps, vt_ps, xt_ps = map(sems, ("kk_ps", "kq_ps", "kt_ps", "vt_ps", "xt_ps"))
        lt_done, x_masked, x_init, at_done = map(sems, ("lt_done", "x_masked", "x_init", "at_done"))
        k_out, v_out, t_out, qs_done = map(sems, ("k_out", "v_out", "t_out", "qs_done"))
        m_ps, m_out, join_ps, joined = map(sems, ("m_ps", "m_out", "join_ps", "joined"))
        ks_ps, r_done, z_ps, zs_done, o_ps, s_ps, o_out, s_done = map(
            sems, ("ks_ps", "r_done", "z_ps", "zs_done", "o_ps", "s_ps", "o_out", "s_done"))
        NL = len(LEVELS)
        ident = sh.const("ident")
        A, B, C, E = ([sh.ps[4 * d + n] for d in range(2)] for n in range(4))

        def field(g, d, name):
            return cur[g][d][:, FIELDS.index(name), :]

        def scalar(g, d, name, u):
            return cur[g][d][:, FIELDS.index(name), u:u + 1]

        def quads(bank):
            return bank[:, :].rearrange("p (u i) -> p u i", u=HG)

        def blocks(ap, s, odd):
            return ap.rearrange("p u (b two s) -> p u b two s", two=2, s=s)[:, :, :, odd, :]

        def each_step(eng, step):
            for g in range(GROUPS):
                step(g, 0, g)
            with eng.Fori(1, NT) as c:
                for g in range(GROUPS):
                    step(c * 2 + g, c, g)

        def chunks(eng, c):
            return c, held(eng, NT - 1 - c, NT - 2)

        early = lambda n: isinstance(n, int) and n < GROUPS

        with nc.Block() as block:
            @block.sync
            def _(sp):
                def load(n, at, g, d):
                    if not early(n):
                        sp.wait_ge(ks_ps[d], n - 1)
                        sp.wait_ge(qs_done[d], n - 1)
                    for kind in range(3):
                        sp.dma_start(qkv[g][d][:, kind, :, :],
                                     sh.rows[kind * H + g * HG:kind * H + (g + 1) * HG, :,
                                             bass.ds(at * P, P)].rearrange("h p t -> p h t")
                                     ).then_inc(loaded[g][d], 16)

                def store(n, at, g, d):
                    sp.wait_ge(o_out[d], n + 1)
                    sp.dma_start(sh.o_rows[d, bass.ds(at * P, P), g * HG * P:(g + 1) * HG * P],
                                 ost[g][d][:, :, :].rearrange("p u e -> p (u e)")).then_inc(stored[g][d], 16)

                def step(n, c, g):
                    here = chunks(sp, c)
                    for d in range(2):
                        load(n, here[d], g, d)
                    if not early(n):
                        before = c - 1, here[1] + 1
                        for d in range(2):
                            store(n - 2, before[d], g, d)

                each_step(sp, step)
                for g in range(GROUPS):
                    for d in range(2):
                        store((NT - 1) * 2 + g, (NT - 1, 0)[d], g, d)
                for g in range(GROUPS):
                    for d in range(2):
                        sp.wait_ge(stored[g][d], NT * 16)

            @block.gpsimd
            def _(pool):
                for d in range(2):
                    for g in range(GROUPS):
                        pool.memset(state[g][d][:, :, :], 0.0)
                    for l in range(NL):
                        last = pool.memset(mm[l][d][:, :, :], 0.0)
                    last.then_inc(cleared[d], 1)

                def step(n, c, g):
                    for d in range(2):
                        pool.wait_ge(eb_done[d], n + 1)
                        pool.wait_ge(loaded[g][d], (c + 1) * 48)
                        if not early(n):
                            pool.wait_ge(o_ps[d], n - 1)
                        pool.tensor_tensor(qs[g][d][:, :, :], qkv[g][d][:, 0, :, :], eb[d][:, :, :],
                                           ALU.mult).then_inc(qs_done[d], 1)

                each_step(pool, step)

            @block.tensor
            def _(pe):
                def prepare(n, c, g):
                    for d in range(2):
                        pe.wait_ge(cur_ready[d], n + 1)
                        for u in range(HG):
                            last = pe.matmul(quads(A[d])[:, u, :], scalar(g, d, "g", u).broadcast_to((P, P)),
                                             sh.late(("tri_f", "tri_b")[d]), start=True, stop=True)
                        last.then_inc(gcb_ps[d], 1)
                    for d in range(2):
                        pe.wait_ge(loaded[g][d], (c + 1) * 48)
                        if not (early(n) and n == 0):
                            pe.wait_ge(joined[d], n * NL)
                        for u in range(HG):
                            k = qkv[g][d][:, 1, u, :]
                            last = pe.matmul(quads(B[d])[:, u, :], k, k, start=True, stop=True)
                        last.then_inc(kk_ps[d], 1)
                    for d in range(2):
                        if not early(n):
                            pe.wait_ge(s_done[d], n - 1)
                        for u in range(HG):
                            last = pe.transpose(quads(C[d])[:, u, :], qkv[g][d][:, 1, u, :], ident)
                        last.then_inc(kt_ps[d], 1)
                        if not early(n):
                            pe.wait_ge(o_out[d], n - 1)
                        for u in range(HG):
                            last = pe.transpose(quads(E[d])[:, u, :], qkv[g][d][:, 2, u, :], ident)
                        last.then_inc(vt_ps[d], 1)
                    for d in range(2):
                        pe.wait_ge(arg_done[d], n + 1)
                        pe.wait_ge(eb_done[d], n + 1)
                        for u in range(HG):
                            last = pe.matmul(quads(A[d])[:, u, :], qkv[g][d][:, 1, u, :], qkv[g][d][:, 0, u, :],
                                             start=True, stop=True)
                        last.then_inc(kq_ps[d], 1)
                    for d in range(2):
                        pe.wait_ge(x_init[d], n + 1)
                        for u in range(HG):
                            last = pe.transpose(quads(B[d])[:, u, :], xm[g][d][:, u, :], ident)
                        last.then_inc(xt_ps[d], 1)

                def level_m(n, g, l):
                    s = LEVELS[l]
                    for d in range(2):
                        if l == 0:
                            pe.wait_ge(t_out[d], n + 1)
                            pe.wait_ge(at_done[d], n + 1)
                        else:
                            pe.wait_ge(joined[d], n * NL + l)
                        for u in range(HG):
                            last = pe.matmul(A[d][:, u * 64:(u + 1) * 64], lt[d][:, u, :],
                                             blocks(tm[d][:, :, :], s, d)[:, u], start=True, stop=True)
                        last.then_inc(m_ps[d], 1)

                def level_join(n, g, l):
                    s = LEVELS[l]
                    for d in range(2):
                        pe.wait_ge(m_out[d], n * NL + l + 1)
                        for u in range(HG):
                            if l < NL - 1:
                                pe.matmul(B[d][:, u * 64:(u + 1) * 64], xm[g][d][:, u, :],
                                          blocks(mm[l][d][:, :, :], s, d)[:, u], start=True, stop=True)
                            last = pe.matmul(B[d][:, 256 + u * 64:256 + (u + 1) * 64], mm[l][d][:, u, :],
                                             blocks(xm[g][d][:, :, :], s, 1 - d)[:, u], start=True, stop=True)
                        last.then_inc(join_ps[d], 1)

                def scan_ks(n, g, final):
                    for d in range(2):
                        if early(n):
                            pe.wait_ge(cleared[d], 1)
                        else:
                            pe.wait_ge(s_done[d], n - 1)
                        pe.wait_ge(v_out[d], n + 1 if final else n + 2)
                        if final:
                            pe.wait_ge(o_out[d], n)
                        for u in range(HG):
                            last = pe.matmul(quads(E[d])[:, u, :], qkv[g][d][:, 1, u, :], state[g][d][:, u, :],
                                             start=True, stop=True)
                        last.then_inc(ks_ps[d], 1)

                def scan_z(n, g, final):
                    for d in range(2):
                        pe.wait_ge(r_done[d], n + 1)
                        pe.wait_ge(k_out[d], n + 1 if final else n + 2)
                        if final:
                            pe.wait_ge(s_done[d], n)
                            pe.wait_ge(joined[d], (n + 1) * NL)
                        for u in range(HG):
                            last = pe.matmul(quads(C[d])[:, u, :], xm[g][d][:, u, :], r[d][:, u, :],
                                             start=True, stop=True)
                        last.then_inc(z_ps[d], 1)

                def scan_os(n, g, d):
                    pe.wait_ge(zs_done[d], n + 1)
                    pe.wait_ge(qs_done[d], n + 1)
                    for u in range(HG):
                        pe.matmul(quads(E[d])[:, u, :], qs[g][d][:, u, :], state[g][d][:, u, :],
                                  start=True, stop=False)
                        last = pe.matmul(quads(E[d])[:, u, :], at_[g][d][:, u, :], zs[d][:, u, :],
                                         start=False, stop=True)
                    last.then_inc(o_ps[d], 1)
                    for u in range(HG):
                        last = pe.matmul(quads(C[d])[:, u, :], kd[g][d][:, u, :], zs[d][:, u, :],
                                         start=True, stop=True)
                    last.then_inc(s_ps[d], 1)

                def step(n, c, g):
                    scan = not (early(n) and n == 0)
                    prepare(n, c, g)
                    level_m(n, g, 0)
                    if scan:
                        scan_ks(n - 1, 1 - g, False)
                    level_join(n, g, 0)
                    level_m(n, g, 1)
                    if scan:
                        scan_z(n - 1, 1 - g, False)
                    level_join(n, g, 1)
                    for l in (2, 3):
                        level_m(n, g, l)
                        if scan:
                            scan_os(n - 1, 1 - g, l - 2)
                        level_join(n, g, l)
                    for l in range(4, NL):
                        level_m(n, g, l)
                        level_join(n, g, l)

                each_step(pe, step)
                n = NT * GROUPS - 1
                scan_ks(n, 1, True)
                scan_z(n, 1, True)
                for d in range(2):
                    scan_os(n, 1, d)

            @block.scalar
            def _(act):
                def prepare(n, c, g):
                    for d in range(2):
                        act.wait_ge(arg_done[d], n + 1)
                        if not (early(n) and n == 0):
                            act.wait_ge(at_done[d], n)
                        for u in range(HG):
                            last = act.activation(dmat[d][:, u, :], arg[d][:, u, :], ACT.Exp,
                                                  bias=scalar(g, d, "neg_gc", u))
                        last.then_inc(d_done[d], 1)
                    for d in range(2):
                        act.wait_ge(arg_done[d], n + 1)
                        if not (early(n) and n == 0):
                            act.wait_ge(qs_done[d], n)
                        act.activation(eb[d][:, :, :], quads(A[d]), ACT.Exp).then_inc(eb_done[d], 1)
                    for d in range(2):
                        act.wait_ge(kt_ps[d], n + 1)
                        if not early(n):
                            act.wait_ge(s_ps[d], n - 1)
                        for u in range(HG):
                            last = act.activation(kd[g][d][:, u, :], quads(C[d])[:, u, :], ACT.Copy,
                                                  scale=scalar(g, d, "e_to_last", u))
                        last.then_inc(k_out[d], 1)
                        act.wait_ge(vt_ps[d], n + 1)
                        if not early(n):
                            act.wait_ge(r_done[d], n - 1)
                        for u in range(HG):
                            last = act.activation(vp[g][d][:, u, :], quads(E[d])[:, u, :], ACT.Copy,
                                                  scale=scalar(g, d, "norm_k", u))
                        last.then_inc(v_out[d], 1)
                    for d in range(2):
                        act.wait_ge(xt_ps[d], n + 1)
                        act.activation(tm[d][:, :, :], quads(B[d]), ACT.Copy).then_inc(t_out[d], 1)

                def scan(n, c, g):
                    for d in range(2):
                        act.wait_ge(z_ps[d], n + 1)
                        if not (early(n) and n == 0):
                            act.wait_ge(s_ps[d], n)
                        for u in range(HG):
                            last = act.activation(zs[d][:, u, :], quads(C[d])[:, u, :], ACT.Copy,
                                                  scale=scalar(g, d, "w", u))
                        last.then_inc(zs_done[d], 1)
                    for d in range(2):
                        act.wait_ge(o_ps[d], n + 1)
                        if not early(n):
                            act.wait_ge(stored[g][d], c * 16)
                        act.activation(ost[g][d][:, :, :], quads(E[d]), ACT.Copy).then_inc(o_out[d], 1)

                def step(n, c, g):
                    prepare(n, c, g)
                    if not (early(n) and n == 0):
                        scan(n - 1, c if g else c - 1, 1 - g)

                each_step(act, step)
                scan(NT * GROUPS - 1, NT - 1, 1)

            @block.vector
            def _(dve):
                def prepare(n, c, g):
                    here = chunks(dve, c)
                    for d in range(2):
                        if not early(n):
                            dve.wait_ge(zs_done[d], n - 1)
                            dve.wait_ge(s_done[d], n - 1)
                        dve.tensor_copy(cur[g][d][:, :, :].unsqueeze(1),
                                        sh.tables[:, d, bass.ds(here[d], 1), g, :, :]).then_inc(cur_ready[d], 1)
                    for d in range(2):
                        dve.wait_ge(gcb_ps[d], n + 1)
                        if not (early(n) and n == 0):
                            dve.wait_ge(d_done[d], n)
                        mask = sh.late(("mask_f", "mask_b")[d]).unsqueeze(1).broadcast_to((P, HG, P))
                        dve.tensor_tensor(arg[d][:, :, :], quads(A[d]), mask, ALU.add).then_inc(arg_done[d], 1)
                    for d in range(2):
                        dve.wait_ge(d_done[d], n + 1)
                        dve.wait_ge(kk_ps[d], n + 1)
                        for u in range(HG):
                            last = dve.scalar_tensor_tensor(lt[d][:, u, :], quads(B[d])[:, u, :], scalar(g, d, "w", u),
                                                            dmat[d][:, u, :], ALU.mult, ALU.mult)
                        last.then_inc(lt_done[d], 1)
                    for d in range(2):
                        dve.wait_ge(lt_done[d], n + 1)
                        if not early(n):
                            dve.wait_ge(z_ps[d], n - 1)
                        neg1 = sh.late(("neg1_f", "neg1_b")[d]).unsqueeze(1).broadcast_to((P, HG, P))
                        dve.tensor_tensor(xm[g][d][:, :, :], lt[d][:, :, :], neg1, ALU.mult).then_inc(x_masked[d], 1)
                    for d in range(2):
                        dve.wait_ge(x_masked[d], n + 1)
                        dve.tensor_tensor(xm[g][d][:, :, :], xm[g][d][:, :, :],
                                          ident.unsqueeze(1).broadcast_to((P, HG, P)), ALU.add).then_inc(x_init[d], 1)
                    for d in range(2):
                        dve.wait_ge(kq_ps[d], n + 1)
                        if not early(n):
                            dve.wait_ge(o_ps[d], n - 1)
                        dve.tensor_tensor(at_[g][d][:, :, :], quads(A[d]), dmat[d][:, :, :],
                                          ALU.mult).then_inc(at_done[d], 1)

                def level_mask(n, g, l):
                    s = LEVELS[l]
                    for d in range(2):
                        dve.wait_ge(m_ps[d], n * NL + l + 1)
                        if early(n) and n == 0 and l == 0:
                            dve.wait_ge(cleared[d], 1)
                        c0 = CL[("level_f", "level_b")[d]][0] - CN_EARLY + l * 64
                        mask = sh.consts_late[:, c0:c0 + 64].rearrange("p (b s) -> p b s", s=s)
                        dve.tensor_tensor(blocks(mm[l][d][:, :, :], s, d),
                                          A[d][:, 0:256].rearrange("p (u b s) -> p u b s", u=HG, s=s),
                                          mask.unsqueeze(1).broadcast_to((P, HG, 64 // s, s)),
                                          ALU.mult).then_inc(m_out[d], 1)

                def level_update(n, g, l):
                    s = LEVELS[l]
                    for d in range(2):
                        dve.wait_ge(join_ps[d], n * NL + l + 1)
                        if l < NL - 1:
                            t = blocks(tm[d][:, :, :], s, d)
                            dve.tensor_tensor(t, t, B[d][:, 0:256].rearrange("p (u b s) -> p u b s", u=HG, s=s),
                                              ALU.subtract)
                        x = blocks(xm[g][d][:, :, :], s, 1 - d)
                        dve.tensor_tensor(x, x, B[d][:, 256:512].rearrange("p (u b s) -> p u b s", u=HG, s=s),
                                          ALU.subtract).then_inc(joined[d], 1)

                def scan_r(n, g):
                    for d in range(2):
                        dve.wait_ge(ks_ps[d], n + 1)
                        if not (early(n) and n == 0):
                            dve.wait_ge(z_ps[d], n)
                        for u in range(HG):
                            last = dve.scalar_tensor_tensor(r[d][:, u, :], quads(E[d])[:, u, :],
                                                            scalar(g, d, "neg_eg", u), vp[g][d][:, u, :],
                                                            ALU.mult, ALU.add)
                        last.then_inc(r_done[d], 1)

                def scan_state(n, g):
                    for d in range(2):
                        dve.wait_ge(s_ps[d], n + 1)
                        for u in range(HG):
                            last = dve.scalar_tensor_tensor(state[g][d][:, u, :], state[g][d][:, u, :],
                                                            scalar(g, d, "e_last", u), quads(C[d])[:, u, :],
                                                            ALU.mult, ALU.add)
                        last.then_inc(s_done[d], 1)

                def step(n, c, g):
                    scan = not (early(n) and n == 0)
                    prepare(n, c, g)
                    for l in range(NL):
                        level_mask(n, g, l)
                        level_update(n, g, l)
                        if scan and l == 0:
                            scan_r(n - 1, 1 - g)
                        if scan and l == 3:
                            scan_state(n - 1, 1 - g)

                each_step(dve, step)
                scan_r(NT * GROUPS - 1, 1)
                scan_state(NT * GROUPS - 1, 1)

N_POOL = len(WINDOWS)
PK = POOL_W // N_POOL // P


def stage_pool(nc, a, sh):
    with ExitStack() as es:
        sb = lambda name, shape, dt=F32: es.enter_context(nc.sbuf_tensor("po_" + name, shape, dt))
        sem = lambda name: sh.es.enter_context(nc.semaphore("po_" + name))
        two = lambda name, shape, dt=F32: [sb(f"{name}{b}", shape, dt) for b in range(2)]
        m, m_hi, m_lo = two("m", [P, PK, SEQ]), two("m_hi", [P, PK, SEQ], F32R), two("m_lo", [P, PK, SEQ], F32R)
        w, w_hi, w_lo = (two("w", [P, PK, PK * P]), two("w_hi", [P, PK, PK * P], F32R),
                         two("w_lo", [P, PK, PK * P], F32R))
        gate, y = two("gate", [P, PK, SEQ]), two("y", [P, SEQ])
        loaded = [sem(f"loaded{b}") for b in range(2)]
        stored = [sem(f"stored{b}") for b in range(2)]
        hi, lo, mapped, gated = sem("hi"), sem("lo"), sem("mapped"), sem("gated")
        ps = sh.ps

        with nc.Block() as block:
            @block.sync
            def _(sp):
                for g in range(N_POOL):
                    b = g % 2
                    if g >= 2:
                        sp.wait_ge(gated, (g - 1) * PK * NB)
                    for dst, row in ((m[b], J_U + PK * g), (gate[b], J_ZP + PK * g)):
                        sp.dma_start(dst[:, :, :], sh.rows[row:row + PK, :, :].rearrange("k p t -> p k t")
                                     ).then_inc(loaded[b], 16)
                    sp.dma_start(w[b][:, :, :], a["pool_w"][0, g].rearrange("(k p) n -> p k n", p=P)
                                 ).then_inc(loaded[b], 16)
                for b in range(2):
                    sp.wait_ge(stored[b], N_POOL * PK // 2 * 16)

            @block.scalar
            def _(act):
                for g in range(N_POOL):
                    b = g % 2
                    act.wait_ge(loaded[b], (g // 2 + 1) * 48)
                    if g >= 2:
                        act.wait_ge(mapped, (g - 1) * PK * NB)
                    act.activation(w_hi[b][:, :, :], w[b][:, :, :], ACT.Copy).then_inc(hi, 1)
                    for k in range(PK):
                        act.activation(m_hi[b][:, k, :], m[b][:, k, :], ACT.Copy).then_inc(hi, 1)

            @block.gpsimd
            def _(pool):
                for g in range(N_POOL):
                    for o in range(PK):
                        n = g * PK + o
                        pool.wait_ge(gated, (n + 1) * NB)
                        pool.dma_start(sh.yp_rows[n, :, :], y[o][:, :]).then_inc(stored[o], 16)

            @block.vector
            def _(dve):
                def split(g):
                    b = g % 2
                    dve.wait_ge(hi, g * (PK + 1) + 1)
                    dve.tensor_tensor(w_lo[b][:, :, :], w[b][:, :, :], w_hi[b][:, :, :].bitcast(F32),
                                      ALU.subtract).then_inc(lo, 1)
                    for k in range(PK):
                        dve.wait_ge(hi, g * (PK + 1) + k + 2)
                        dve.tensor_tensor(m_lo[b][:, k, :], m[b][:, k, :], m_hi[b][:, k, :].bitcast(F32),
                                          ALU.subtract).then_inc(lo, 1)

                split(0)
                for g in range(N_POOL):
                    if g + 1 < N_POOL:
                        split(g + 1)
                    for o in range(PK):
                        n = g * PK + o
                        if g:
                            dve.wait_ge(stored[o], g * 16)
                        for t in range(NB):
                            dve.wait_ge(mapped, n * NB + t + 1)
                            dve.scalar_tensor_tensor(y[o][:, t * TB:(t + 1) * TB], ps[o * NB + t][:, :],
                                                     sh.cols[:, P + n:P + n + 1],
                                                     gate[g % 2][:, o, t * TB:(t + 1) * TB],
                                                     ALU.mult, ALU.mult).then_inc(gated, 1)

            @block.tensor
            def _(pe):
                for g in range(N_POOL):
                    b = g % 2
                    pe.wait_ge(lo, (g + 1) * (PK + 1))
                    for o in range(PK):
                        for t in range(NB):
                            if g:
                                pe.wait_ge(gated, ((g - 1) * PK + o) * NB + t + 1)
                            for k in range(PK):
                                for wp, mp in ((w_hi, m_hi), (w_hi, m_lo), (w_lo, m_hi)):
                                    last = pe.matmul(ps[o * NB + t][:, :], wp[b][:, k, o * P:(o + 1) * P],
                                                     mp[b][:, k, t * TB:(t + 1) * TB],
                                                     start=(k == 0 and mp is m_hi and wp is w_hi),
                                                     stop=(k == PK - 1 and wp is w_lo))
                            last.then_inc(mapped, 1)


EK = MIX_W // P


def stage_output(nc, a, sh, out):
    with ExitStack() as es:
        sb = lambda name, shape, dt=F32: es.enter_context(nc.sbuf_tensor("ou_" + name, shape, dt))
        sem = lambda name: sh.es.enter_context(nc.semaphore("ou_" + name))
        two = lambda name, shape, dt=F32: [sb(f"{name}{b}", shape, dt) for b in range(2)]
        w_hi, w_lo = sb("w_hi", [P, EK, D], F32R), sb("w_lo", [P, EK, D], F32R)
        w_raw = two("w_raw", [P, D // 2])
        o_f, o_b, x = two("o_f", [P, D]), two("o_b", [P, D]), two("x", [P, D])
        y, y_hi, y_lo = sb("y", [P, EK, P]), two("y_hi", [P, EK, P], F32R), two("y_lo", [P, EK, P], F32R)
        gate = sb("gate", [P, H, P])
        fnw = sb("fnw", [P, D])
        qf, qf2 = sb("qf", [P, NT, H]), sb("qf2", [P, NT, H])
        st = two("st", [P, 4, H])
        eps = sb("eps", [P, 1])
        w_loaded = [sem(f"w_loaded{b}") for b in range(2)]
        w_split_hi, w_split = sem("w_split_hi"), sem("w_split")
        loaded = [sem(f"loaded{b}") for b in range(2)]
        gate_in = sem("gate_in")
        stored = [sem(f"stored{b}") for b in range(2)]
        const_in, const_set = sem("const_in"), sem("const_set")
        o_sum, o_sq, o_ss, o_arg, o_std, o_rstd, o_fac, o_norm = map(
            sem, ("o_sum", "o_sq", "o_ss", "o_arg", "o_std", "o_rstd", "o_fac", "o_norm"))
        turned, gated, hi_p, hi_d, lo_p, lo_d = map(sem, ("turned", "gated", "hi_p", "hi_d", "lo_p", "lo_d"))
        out_ps, res, res_sq, res_std, res_rstd, final = map(
            sem, ("out_ps", "res", "res_sq", "res_std", "res_rstd", "final"))
        ps, ident = sh.ps, sh.const("ident")
        heads = lambda ap: ap.rearrange("p (h e) -> p h e", h=H)

        def each_tile(eng, step):
            for b in range(2):
                step(b, 0, b, True)
            with eng.Fori(1, NT // 2) as n:
                for b in range(2):
                    step(n * 2 + b, n, b, False)

        cols_of = lambda i: slice(i % 2 * TB, (i % 2 + 1) * TB)
        is0 = lambda t: isinstance(t, int) and t == 0

        with nc.Block() as block:
            @block.sync
            def _(sp):
                sp.dma_start(fnw[:, :], a["final_norm_w"].rearrange("(o n) -> o n", o=1).broadcast_to((P, D))
                             ).then_inc(const_in, 16)

                def load(t, b, first, row, res_before):
                    if not first:
                        sp.wait_ge(res, res_before)
                    for dst, src in ((o_f[b][:, :], sh.o_rows[0, bass.ds(row, P), :]),
                                     (o_b[b][:, :], sh.o_rows[1, bass.ds(row, P), :]),
                                     (x[b][:, :], a["x"][0, bass.ds(row, P), :])):
                        sp.dma_start(dst, src).then_inc(loaded[b], 16)

                def store(t, b):
                    sp.wait_ge(final, t + 1)
                    sp.dma_start(out[0, bass.ds(t * P, P), :], o_f[b][:, :]).then_inc(stored[b], 16)

                for b in range(2):
                    load(b, b, True, b * P, None)
                with sp.Fori(1, NT // 2) as n:
                    for b in range(2):
                        t = n * 2 + b
                        row, res_before = held(sp, t * P, SEQ - P), held(sp, (t - 1) * 2, NT * 2)
                        n_stored = held(sp, n * 16, NT * 8)
                        store(t - 2, b)
                        sp.wait_ge(stored[b], n_stored)
                        load(t, b, False, row, res_before)
                for b in range(2):
                    store(NT - 2 + b, b)
                for b in range(2):
                    sp.wait_ge(stored[b], NT // 2 * 16)

            @block.gpsimd
            def _(pool):
                for i in range(2 * EK):
                    if i >= 2:
                        pool.wait_ge(w_split, i - 1)
                    pool.dma_start(w_raw[i % 2][:, :], a["w_out"][0, i // 2 * P:(i // 2 + 1) * P, cols_of(i)]
                                   ).then_inc(w_loaded[i % 2], 16)

                def load(t):
                    pool.dma_start(y[:, 0:H, :], sh.yp_rows[:, :, bass.ds(t * P, P)].rearrange("k p t -> p k t")
                                   ).then_inc(gate_in, 16)
                    pool.dma_start(gate[:, :, :], sh.rows[J_ZD:J_ZP, :, bass.ds(t * P, P)].rearrange("k p t -> p k t")
                                   ).then_inc(gate_in, 16)

                def step(t, n, b, first):
                    if not is0(t):
                        pool.wait_ge(lo_p, t)
                        pool.wait_ge(lo_d, t)
                    load(t)
                    pool.wait_ge(hi_p, t + 1)
                    pool.tensor_tensor(y_lo[b][:, 0:H, :], y[:, 0:H, :], y_hi[b][:, 0:H, :].bitcast(F32),
                                       ALU.subtract).then_inc(lo_p, 1)

                each_tile(pool, step)

            @block.scalar
            def _(act):
                act.wait_ge(const_set, 1)

                def front(t, n, b, first):
                    act.wait_ge(o_sum, t + 1)
                    act.activation(o_b[b][:, :], o_f[b][:, :], ACT.Square).then_inc(o_sq, 1)
                    act.wait_ge(gate_in, (t + 1) * 32)
                    if not first:
                        act.wait_ge(out_ps, (t - 1) * 2)
                    act.activation(y_hi[b][:, 0:H, :], y[:, 0:H, :], ACT.Copy).then_inc(hi_p, 1)
                    act.wait_ge(o_arg, t + 1)
                    act.activation(st[b][:, 1, :], st[b][:, 0, :], ACT.Sqrt, bias=eps[:, :],
                                   scale=1.0 / P).then_inc(o_std, 1)
                    act.wait_ge(gated, (t + 1) * 2)
                    act.activation(y_hi[b][:, H:EK, :], y[:, H:EK, :], ACT.Copy).then_inc(hi_d, 1)

                def back(t, b):
                    act.wait_ge(res, (t + 1) * 2)
                    act.activation(o_b[b][:, :], x[b][:, :], ACT.Square,
                                   accum_out=st[b][:, 2, 0:1]).then_inc(res_sq, 1)
                    act.wait_ge(res_sq, t + 1)
                    act.activation(st[b][:, 2, 1:2], st[b][:, 2, 0:1], ACT.Sqrt, bias=eps[:, :],
                                   scale=1.0 / D).then_inc(res_std, 1)

                for i in range(2 * EK):
                    act.wait_ge(w_loaded[i % 2], (i // 2 + 1) * 16)
                    act.activation(w_hi[:, i // 2, cols_of(i)], w_raw[i % 2][:, :], ACT.Copy).then_inc(w_split_hi, 1)

                def step(t, n, b, first):
                    front(t, n, b, first)
                    if not is0(t):
                        back(t - 1, 1 - b)

                each_tile(act, step)
                back(NT - 1, 1)

            @block.vector
            def _(dve):
                dve.memset(eps[:, :], EPS).then_inc(const_set, 1)
                dve.tensor_scalar(qf[:, :, :], sh.rq[:, :, :], float(P) ** -0.5, None, ALU.mult).then_inc(const_set, 1)
                dve.wait_ge(const_set, 2)
                dve.tensor_tensor(qf2[:, :, :], qf[:, :, :], qf[:, :, :], ALU.mult).then_inc(const_set, 1)
                dve.wait_ge(const_set, 3)
                dve.wait_ge(const_in, 16)

                def front(t, n, b, first):
                    dve.wait_ge(loaded[b], (n + 1) * 48)
                    dve.tensor_tensor(o_f[b][:, :], o_f[b][:, :], o_b[b][:, :], ALU.add).then_inc(o_sum, 1)
                    dve.wait_ge(o_sq, t + 1)
                    dve.tensor_reduce(st[b][:, 3, :], heads(o_b[b][:, :]), AX.X, ALU.add).then_inc(o_ss, 1)
                    dve.wait_ge(o_ss, t + 1)
                    dve.tensor_tensor(st[b][:, 0, :].unsqueeze(1), st[b][:, 3, :].unsqueeze(1), qf2[:, bass.ds(t, 1), :],
                                      ALU.mult).then_inc(o_arg, 1)
                    dve.wait_ge(o_std, t + 1)
                    dve.reciprocal(st[b][:, 0, :], st[b][:, 1, :]).then_inc(o_rstd, 1)
                    dve.wait_ge(o_rstd, t + 1)
                    dve.tensor_tensor(st[b][:, 3, :].unsqueeze(1), st[b][:, 0, :].unsqueeze(1), qf[:, bass.ds(t, 1), :],
                                      ALU.mult).then_inc(o_fac, 1)
                    dve.wait_ge(o_fac, t + 1)
                    dve.tensor_tensor(heads(o_f[b][:, :]), heads(o_f[b][:, :]),
                                      st[b][:, 3, :].unsqueeze(2).broadcast_to((P, H, P)), ALU.mult).then_inc(o_norm, 1)
                    dve.wait_ge(turned, t + 1)
                    dve.wait_ge(gate_in, (t + 1) * 32)
                    for n2 in range(2):
                        h = slice(n2 * 4, n2 * 4 + 4)
                        dve.scalar_tensor_tensor(y[:, H + n2 * 4:H + n2 * 4 + 4, :],
                                                 ps[n2][:, :].rearrange("p (h t) -> p h t", h=4),
                                                 sh.cols[:, P + 8:P + 9], gate[:, h, :],
                                                 ALU.mult, ALU.mult).then_inc(gated, 1)
                    dve.wait_ge(hi_d, t + 1)
                    dve.tensor_tensor(y_lo[b][:, H:EK, :], y[:, H:EK, :], y_hi[b][:, H:EK, :].bitcast(F32),
                                      ALU.subtract).then_inc(lo_d, 1)

                def back(t, b):
                    for n2 in range(2):
                        dve.wait_ge(out_ps, t * 2 + n2 + 1)
                        c = slice(n2 * TB, (n2 + 1) * TB)
                        dve.tensor_tensor(x[b][:, c], ps[2 + 2 * b + n2][:, :], x[b][:, c], ALU.add).then_inc(res, 1)
                    dve.wait_ge(res_std, t + 1)
                    dve.reciprocal(st[b][:, 2, 2:3], st[b][:, 2, 1:2]).then_inc(res_rstd, 1)
                    dve.wait_ge(res_rstd, t + 1)
                    dve.scalar_tensor_tensor(o_f[b][:, :], x[b][:, :], st[b][:, 2, 2:3], fnw[:, :],
                                             ALU.mult, ALU.mult).then_inc(final, 1)

                for i in range(2 * EK):
                    dve.wait_ge(w_split_hi, i + 1)
                    dve.tensor_tensor(w_lo[:, i // 2, cols_of(i)], w_raw[i % 2][:, :],
                                      w_hi[:, i // 2, cols_of(i)].bitcast(F32), ALU.subtract).then_inc(w_split, 1)

                def step(t, n, b, first):
                    front(t, n, b, first)
                    if not is0(t):
                        back(t - 1, 1 - b)

                each_tile(dve, step)
                back(NT - 1, 1)

            @block.tensor
            def _(pe):
                def turn(t, b):
                    pe.wait_ge(o_norm, t + 1)
                    if not is0(t):
                        pe.wait_ge(gated, t * 2)
                    for h in range(H):
                        last = pe.transpose(ps[h // 4][:, (h % 4) * P:(h % 4 + 1) * P],
                                            o_f[b][:, h * P:(h + 1) * P], ident)
                    last.then_inc(turned, 1)

                def multiply(t, b, half, early):
                    if half == 0:
                        pe.wait_ge(lo_p, t + 1)
                        pe.wait_ge(lo_d, t + 1)
                        if not early:
                            pe.wait_ge(res, (t - 1) * 2)
                    for k in range(EK):
                        if is0(t) and half == 0:
                            pe.wait_ge(w_split, 2 * k + 2)
                        for yp, wp in ((y_hi, w_hi), (y_lo, w_hi), (y_hi, w_lo)):
                            last = pe.matmul(ps[2 + 2 * b + half][:, :], yp[b][:, k, :],
                                             wp[:, k, half * TB:(half + 1) * TB],
                                             start=(k == 0 and yp is y_hi and wp is w_hi),
                                             stop=(k == EK - 1 and wp is w_lo))
                    last.then_inc(out_ps, 1)

                def step(t, n, b, first):
                    if not is0(t):
                        early = first or b == 0 and isinstance(t, int)
                        multiply(t - 1, 1 - b, 0, early)
                    turn(t, b)
                    if not is0(t):
                        multiply(t - 1, 1 - b, 1, True)

                step(0, 0, 0, True)
                step(1, 0, 1, True)
                step(2, 1, 0, False)
                step(3, 1, 1, False)
                with pe.Fori(2, NT // 2) as n:
                    for b in range(2):
                        step(n * 2 + b, n, b, False)
                multiply(NT - 1, 1, 0, False)
                multiply(NT - 1, 1, 1, True)


class Shared:

    def const(self, name):
        return self.consts[:, CL[name][0]:CL[name][1]]

    def late(self, name):
        return self.consts_late[:, CL[name][0] - CN_EARLY:CL[name][1] - CN_EARLY]


def build(nc, a, out):
    with ExitStack() as es:
        sh = Shared()
        sh.es = es
        sb = lambda name, shape, dt=F32: es.enter_context(nc.sbuf_tensor(name, shape, dt))
        sh.ps = [es.enter_context(nc.psum_tensor(f"bank{n}", [P, TB], F32)) for n in range(8)]
        sh.consts = sb("consts_sb", [P, CN_EARLY])
        sh.cols = sb("cols", [P, P + 16])
        sh.ones = sb("ones_col", [P, 1])
        sh.rows = nc.dram_tensor("rows", (J_LG, P, SEQ), F32, kind="Internal").ap()
        sh.rq = sb("rq", [P, NT, H])
        sh.o_rows = nc.dram_tensor("o_rows", (2, SEQ, H * P), F32, kind="Internal").ap()
        sh.yp_rows = nc.dram_tensor("yp_rows", (POOL_W // P, P, SEQ), F32, kind="Internal").ap()
        with ExitStack() as scope:
            sh.sumsq = scope.enter_context(nc.sbuf_tensor("sumsq", [P, J_V, NT], F32))
            sh.logits = scope.enter_context(nc.sbuf_tensor("logits", [P, NT, 32], F32))
            with ExitStack() as early:
                sh.xh = early.enter_context(nc.sbuf_tensor("xh", [P, KT, SEQ], F32R))
                sh.xl = early.enter_context(nc.sbuf_tensor("xl", [P, KT, SEQ], F32R))
                stage_prepare(nc, a, sh)
                stage_project(nc, a, sh)
            stage_pool(nc, a, sh)
            sh.consts_late = scope.enter_context(nc.sbuf_tensor("consts_late", [P, CN - CN_EARLY], F32))
            sh.tables = scope.enter_context(nc.sbuf_tensor("tables", [P, 2, NT, GROUPS, NF, HG], F32))
            stage_gates(nc, a, sh)
            stage_delta(nc, a, sh)
        stage_output(nc, a, sh, out)


_INS = ["x", "norm_w", "w_in", "pool_w", "pool_scale", "conv_w", "a_log", "dt_bias", "head_norm_w", "w_out",
        "final_norm_w"]


def kernel(**inputs):
    import concourse.bacc as bacc
    from concourse.bass_utils import run_bass_kernel_spmd

    nc = bacc.Bacc("TRN2", target_bir_lowering=False, num_devices=1)
    arrays = {"in_" + name: np.ascontiguousarray(inputs[name]) for name in _INS}
    arrays["in_consts"] = constant_table()
    args = {name[3:]: nc.dram_tensor(name, v.shape, mybir.dt.from_np(v.dtype), kind="ExternalInput").ap()
            for name, v in arrays.items()}
    out = nc.dram_tensor("out_0", (1, SEQ, D), F32, kind="ExternalOutput").ap()
    build(nc, args, out)
    r = run_bass_kernel_spmd(nc, [arrays], core_ids=[0])
    return r.results[0]["out_0"]
```

```python
from contextlib import ExitStack

import numpy as np
import concourse.bass as bass
import concourse.mybir as mybir

F32 = mybir.dt.float32
F32R = mybir.dt.float32r
ACT = mybir.ActivationFunctionType
ALU = mybir.AluOpType
AX = mybir.AxisListType

P = 128
D = 1024
SEQ = 2048
KT = D // P
NT = SEQ // P
TB = 512
NB = SEQ // TB
POOL_W = 1024
H = 8
CONV_K = 5
EPS = 1e-6
OFF_ZP = 1024
OFF_QKV = 2048
OFF_LOGITS = 6144
IN_W = 6176
MIX_W = 2048
WINDOWS = (2, 4, 8, 16)

J_QK, J_V, J_U, J_LG, J_END = 0, 16, 24, 32, 33
R_ZD, R_ZP, R_END = 32, 40, 48
OFF_ZD = 5120
PAD = 8
CW = SEQ + 2 * PAD

LEVELS = (2, 4, 8, 16, 32, 64)
BIG = -1.0e30


def constant_layout():
    at, out = 0, {}
    for name, n in (("ident", P), ("edge", 4 * 2 * PAD), ("tri_f", P), ("tri_b", P), ("ones", P), ("mask_f", P), ("mask_b", P),
                    ("neg1_f", P), ("neg1_b", P), ("level_f", 64 * len(LEVELS)), ("level_b", 64 * len(LEVELS))):
        out[name] = (at, at + n)
        at += n
    return out, at


CL, CN = constant_layout()
CN_EARLY = CL["edge"][1]


def constant_table():
    t = np.zeros((P, CN), np.float32)

    def put(name, a):
        t[:, CL[name][0]:CL[name][1]] = a

    r, c = np.arange(P)[:, None], np.arange(P)[None, :]
    put("ident", r == c)
    put("tri_f", r <= c)
    put("tri_b", r >= c)
    put("ones", 1.0)
    put("mask_f", np.where(c >= r, 0.0, BIG))
    put("mask_b", np.where(c <= r, 0.0, BIG))
    put("neg1_f", -((r % 2 == 0) & (c == r + 1)).astype(np.float32))
    put("neg1_b", -((r % 2 == 1) & (c == r - 1)).astype(np.float32))
    f, b = [], []
    for s in LEVELS:
        even = np.array([x for x in range(P) if (x // s) % 2 == 0])[None, :]
        odd = np.array([x for x in range(P) if (x // s) % 2 == 1])[None, :]
        f.append(r // s == even // s + 1)
        b.append(r // s == odd // s - 1)
    put("level_f", np.concatenate(f, 1))
    put("level_b", np.concatenate(b, 1))
    e = np.ones((4, 2, PAD), np.float32)
    for g, w in enumerate(WINDOWS):
        for n in range(PAD):
            for side, tok in ((0, n), (1, SEQ - PAD + n)):
                lo, hi = max(tok - w // 2, 0), min(tok + w // 2 - 1, SEQ - 1)
                e[g, side, n] = w / (hi - lo + 1)
    put("edge", e.reshape(1, -1))
    return t


def stage_prepare(nc, a, sh):
    with ExitStack() as es:
        sb = lambda name, shape, dt=F32: es.enter_context(nc.sbuf_tensor("pr_" + name, shape, dt))
        sem = lambda name: sh.es.enter_context(nc.semaphore("pr_" + name))
        xin = [sb(f"xin{q}", [P, D]) for q in range(4)]
        xs = [sb(f"xs{b}", [P, D]) for b in range(2)]
        ht = [sb(f"ht{b}", [P, KT, P]) for b in range(2)]
        junk = sb("junk", [P, D])
        stat = sb("stat", [P, 2, 4])
        rows = sb("rows", [P, P])
        rows2 = sb("rows2", [16, P])
        eps = sb("eps", [P, 1])
        consts_in, rows_in = sem("consts_in"), sem("rows_in")
        x_in = [sem(f"x_in{q}") for q in range(4)]
        h_out = [sem(f"h_out{b}") for b in range(2)]
        x_scaled, norms, rstd = sem("x_scaled"), sem("norms"), sem("rstd")
        x_t, ht_half, hi, lo, cols_t, cols = sem("x_t"), sem("ht_half"), sem("hi"), sem("lo"), sem("cols_t"), sem("cols")
        ps = sh.ps
        ident = sh.const("ident")
        is0 = lambda t: isinstance(t, int) and t == 0

        with nc.Block() as block:
            @block.sync
            def _(sp):
                sp.dma_start(sh.consts[:, :], a["consts"][:, 0:CN_EARLY]).then_inc(consts_in, 16)
                sp.dma_start(rows[0:120, :], a["conv_w"].rearrange("o k (t p) -> (o k t) p", p=P)).then_inc(rows_in, 16)
                sp.dma_start(rows[120:128, :], a["norm_w"].rearrange("o (t p) -> (o t) p", p=P)).then_inc(rows_in, 16)
                sp.dma_start(rows2[0:8, :], a["pool_scale"].rearrange("o (t p) -> (o t) p", p=P)).then_inc(rows_in, 16)
                sp.dma_start(rows2[8:9, :], a["head_norm_w"]).then_inc(rows_in, 16)

                def store(t, b):
                    sp.wait_ge(ht_half, t * 2 + 2)
                    sp.dma_start(sh.h_tiles[bass.ds(t, 1), :, :, :].rearrange("o p k n -> (o p) k n"),
                                 ht[b][:, :, :]).then_inc(h_out[b], 16)

                for t in range(4):
                    sp.dma_start(xin[t][:, :], a["x"][0, t * P:(t + 1) * P, :]).then_inc(x_in[t], 16)
                with sp.Fori(1, NT // 4) as i:
                    for q in range(4):
                        t = i * 4 + q
                        row, scaled = held(sp, t * P, SEQ - P), held(sp, t - 3, NT)
                        sp.wait_ge(x_scaled, scaled)
                        sp.dma_start(xin[q][:, :], a["x"][0, bass.ds(row, P), :]).then_inc(x_in[q], 16)
                        store(held(sp, t - 4, NT - 5), q % 2)
                for t in range(NT - 4, NT):
                    store(t, t % 2)
                for b in range(2):
                    sp.wait_ge(h_out[b], NT // 2 * 16)

            @block.scalar
            def _(act):
                act.wait_ge(cols, 1)

                def front(t, i, q):
                    b = q % 2
                    act.wait_ge(x_in[q], (i + 1) * 16)
                    if not is0(t):
                        act.wait_ge(norms, t * 2)
                    act.activation(junk[:, :], xin[q][:, :], ACT.Square,
                                   accum_out=stat[:, b, 0:1]).then_inc(norms, 1)
                    act.wait_ge(norms, t * 2 + 1)
                    act.activation(stat[:, b, 1:2], stat[:, b, 0:1], ACT.Sqrt, bias=eps[:, :],
                                   scale=1.0 / D).then_inc(norms, 1)

                def scale(t, q, first):
                    act.wait_ge(rstd, t + 1)
                    if not first:
                        act.wait_ge(x_t, t - 1)
                    act.activation(xs[q % 2][:, :], xin[q][:, :], ACT.Copy,
                                   scale=stat[:, q % 2, 2:3]).then_inc(x_scaled, 1)

                def high(t, q):
                    act.wait_ge(ht_half, t * 2 + 2)
                    act.activation(sh.xh[:, :, bass.ds(t * P, P)], ht[q % 2][:, :, :], ACT.Copy).then_inc(hi, 1)

                for t in range(4):
                    front(t, 0, t)
                    if t >= 1:
                        scale(t - 1, t - 1, t < 3)
                    if t >= 2:
                        high(t - 2, t - 2)
                with act.Fori(1, NT // 4) as i:
                    for q in range(4):
                        front(i * 4 + q, i, q)
                        scale(i * 4 + q - 1, (q - 1) % 4, False)
                        high(i * 4 + q - 2, (q - 2) % 4)
                scale(NT - 1, 3, False)
                high(NT - 2, 2)
                high(NT - 1, 3)

            @block.tensor
            def _(pe):
                pe.wait_ge(consts_in, 16)
                pe.wait_ge(rows_in, 64)
                pe.transpose(ps[4][:, 0:P], rows[:, :], ident).then_inc(cols_t, 1)
                pe.transpose(ps[5][:, 0:9], rows2[0:9, :], ident[0:9, 0:9]).then_inc(cols_t, 1)

                def tile(t, b, first):
                    pe.wait_ge(x_scaled, t + 1)
                    if not first:
                        pe.wait_ge(ht_half, t * 2 - 2)
                    for k in range(KT):
                        last = pe.transpose(ps[2 * b + k // 4][:, (k % 4) * P:(k % 4 + 1) * P],
                                            xs[b][:, k * P:(k + 1) * P], ident)
                    last.then_inc(x_t, 1)

                tile(0, 0, True)
                tile(1, 1, True)
                with pe.Fori(1, NT // 2) as i:
                    tile(i * 2, 0, False)
                    tile(i * 2 + 1, 1, False)

            @block.vector
            def _(dve):
                dve.memset(eps[:, :], EPS).then_inc(cols, 1)
                dve.wait_ge(cols_t, 2)
                dve.tensor_copy(sh.cols[:, 0:P], ps[4][:, 0:P]).then_inc(cols, 1)
                dve.tensor_copy(sh.cols[:, P:P + 9], ps[5][:, 0:9]).then_inc(cols, 1)
                dve.wait_ge(cols, 3)

                def root(t, b):
                    dve.wait_ge(norms, t * 2 + 2)
                    dve.reciprocal(stat[:, b, 2:3], stat[:, b, 1:2]).then_inc(rstd, 1)

                def tile(t, i, b, first):
                    dve.wait_ge(x_t, t + 1)
                    if not first:
                        dve.wait_ge(lo, t - 1)
                        dve.wait_ge(h_out[b], i * 16)
                    for half in range(2):
                        nw = sh.cols[:, 120 + 4 * half:124 + 4 * half].unsqueeze(2).broadcast_to((P, 4, P))
                        dve.tensor_tensor(ht[b][:, 4 * half:4 * half + 4, :],
                                          ps[2 * b + half][:, :].rearrange("p (k t) -> p k t", t=P),
                                          nw, ALU.mult).then_inc(ht_half, 1)

                root(0, 0)
                root(1, 1)
                tile(0, 0, 0, True)
                root(2, 0)
                tile(1, 0, 1, True)
                with dve.Fori(1, NT // 2 - 1) as i:
                    root(i * 2 + 1, 1)
                    tile(i * 2, i, 0, False)
                    root(i * 2 + 2, 0)
                    tile(i * 2 + 1, i, 1, False)
                root(NT - 1, 1)
                tile(NT - 2, NT // 2 - 1, 0, False)
                tile(NT - 1, NT // 2 - 1, 1, False)

            @block.gpsimd
            def _(pool):
                def tile(t, b):
                    pool.wait_ge(hi, t + 1)
                    pool.tensor_tensor(sh.xl[:, :, bass.ds(t * P, P)], ht[b][:, :, :],
                                       sh.xh[:, :, bass.ds(t * P, P)].bitcast(F32), ALU.subtract).then_inc(lo, 1)

                with pool.Fori(0, NT // 2) as i:
                    tile(i * 2, 0)
                    tile(i * 2 + 1, 1)


def held(eng, v, most):
    if isinstance(v, int):
        return v
    reg = eng.alloc_register()
    eng.reg_mov(reg, v)
    return eng.snap(reg, min_val=0, max_val=most)


def tile_columns(j):
    if isinstance(j, int):
        if j >= J_LG:
            return IN_W - P
        if j >= J_U:
            return (j - J_U) * P
        return OFF_QKV + j * P
    raise TypeError(j)


def stage_project(nc, a, sh):
    with ExitStack() as es:
        sb = lambda name, shape, dt=F32: es.enter_context(nc.sbuf_tensor("pj_" + name, shape, dt))
        sem = lambda name: sh.es.enter_context(nc.semaphore("pj_" + name))
        w_raw = [sb(f"w_raw{b}", [P, KT, P]) for b in range(2)]
        w_hi = [sb(f"w_hi{b}", [P, KT, P], F32R) for b in range(2)]
        w_lo = [sb(f"w_lo{b}", [P, KT, P], F32R) for b in range(2)]
        row = [sb(f"row{b}", [P, CW]) for b in range(2)]
        acc = [sb(f"acc{b}", [P, CW]) for b in range(2)]
        act_row = [sb(f"act_row{b}", [P, SEQ]) for b in range(2)]
        w_in_sem = [sem(f"w_loaded{b}") for b in range(2)]
        stored = [sem(f"stored{b}") for b in range(2)]
        hi_done, lo_done, projected, evacuated = sem("hi_done"), sem("lo_done"), sem("projected"), sem("evacuated")
        padded, tap, row_free, silu_done, sq_done = sem("padded"), sem("tap"), sem("row_free"), sem("silu_done"), sem("sq_done")
        row_done, ss_done, ss_out = sem("row_done"), sem("ss_done"), sem("ss_out")
        window = sem("window")
        lg_t, lg_out = sem("lg_t"), sem("lg_out")
        ps, ident = sh.ps, sh.const("ident")

        segments = [(J_QK, J_V, "qk", 4), (J_V, J_U, "v", 2), (J_U, J_LG, "u", 2), (J_LG, J_END, "lg", 1)]

        def each_tile(eng, step, parts=segments):
            for j0, j1, kind, peel in parts:
                for j in range(j0, j0 + peel):
                    step(j, j // 2, j % 2, j0, kind, j < 2)
                if j1 - j0 > peel:
                    with eng.Fori((j0 + peel) // 2, j1 // 2) as n:
                        step(n * 2, n, 0, j0, kind, False)
                        step(n * 2 + 1, n, 1, j0, kind, False)

        def at(j, n):
            return isinstance(j, int) and j == n

        def columns(j, j0):
            return tile_columns(j0) + (j - j0) * P

        with nc.Block() as block:
            @block.sync
            def _(sp):
                def load(j, pair, b, j0, first):
                    if not first:
                        sp.wait_ge(lo_done, j - 1)
                    w = a["w_in"][0, :, bass.ds(columns(j, j0), P)].rearrange("(k p) n -> p k n", p=P)
                    sp.dma_start(w_raw[b][:, :, :], w).then_inc(w_in_sem[b], 16)

                def store(j, b, kind):
                    if kind in ("qk", "v"):
                        sp.wait_ge(silu_done, j + 1)
                    else:
                        sp.wait_ge(row_free, j - J_U + 1)
                    sp.dma_start(sh.rows[bass.ds(j, 1), :, :].rearrange("o p t -> (o p) t"),
                                 act_row[b][:, :]).then_inc(stored[b], 16)

                def step(j, pair, b, j0, kind, first):
                    load(j, pair, b, j0, first)
                    if not first:
                        before = [s[2] for s in segments if s[0] < j0][-1:] if at(j, j0) or at(j, j0 + 1) else [kind]
                        store(j - 2, b, before[0])

                each_tile(sp, step)
                store(J_LG - 1, 1, "u")
                for b in range(2):
                    sp.wait_ge(stored[b], J_LG // 2 * 16)

            @block.gpsimd
            def _(pool):
                for b in range(2):
                    pool.memset(row[b][:, 0:PAD], 0.0).then_inc(padded, 1)
                    pool.memset(row[b][:, PAD + SEQ:CW], 0.0).then_inc(padded, 1)
                pool.memset(sh.ones[:, :], 1.0).then_inc(padded, 1)

                def step(j, pair, b, j0, kind, first):
                    pool.wait_ge(hi_done, j + 1)
                    pool.tensor_tensor(w_lo[b][:, :, :], w_raw[b][:, :, :], w_hi[b][:, :, :].bitcast(F32),
                                       ALU.subtract).then_inc(lo_done, 1)

                each_tile(pool, step)

            @block.tensor
            def _(pe):
                pe.wait_ge(padded, 5)

                def sums(j, b):
                    pe.wait_ge(sq_done, j + 1)
                    if not (at(j, 0) or at(j, 1)):
                        pe.wait_ge(ss_out, j - 1)
                    for c in range(NT):
                        last = pe.matmul(ps[4 + b][:, c:c + 1], acc[b][:, c * P:(c + 1) * P], sh.ones[:, 0:1],
                                         start=True, stop=True)
                    last.then_inc(ss_done, 1)

                def step(j, pair, b, j0, kind, first):
                    pe.wait_ge(lo_done, j + 1)
                    for t in range(NB):
                        if not at(j, 0):
                            pe.wait_ge(evacuated, j * NB + (t - NB + 1))
                        for k in range(KT):
                            for w, x in ((w_hi, sh.xh), (w_hi, sh.xl), (w_lo, sh.xh)):
                                last = pe.matmul(ps[t][:, :], w[b][:, k, :], x[:, k, t * TB:(t + 1) * TB],
                                                 start=(k == 0 and x is sh.xh and w is w_hi),
                                                 stop=(k == KT - 1 and w is w_lo))
                        last.then_inc(projected, 1)
                        if t == 1:
                            if kind == "qk" and not first:
                                sums(j - 2, b)
                            if kind == "v" and isinstance(j, int):
                                sums(j - 2, b)
                    if kind == "lg":
                        pe.wait_ge(evacuated, (j + 1) * NB)
                        pe.wait_ge(ss_out, J_V)
                        for c in range(NT):
                            last = pe.transpose(ps[4 + c // 4][:, (c % 4) * P:(c % 4 + 1) * P],
                                                act_row[0][:, c * P:(c + 1) * P], ident)
                        last.then_inc(lg_t, 1)

                each_tile(pe, step)

            @block.scalar
            def _(act):
                def split(j, pair, b, first):
                    act.wait_ge(w_in_sem[b], (pair + 1) * 16)
                    if not first:
                        act.wait_ge(projected, (j - 1) * NB)
                    act.activation(w_hi[b][:, :, :], w_raw[b][:, :, :], ACT.Copy).then_inc(hi_done, 1)

                def silu(j, pair, b, kind, first):
                    act.wait_ge(tap, (j + 1) * CONV_K)
                    if not first:
                        act.wait_ge(stored[b], pair * 16)
                    act.activation(act_row[b][:, :], acc[b][:, 0:SEQ], ACT.Silu).then_inc(silu_done, 1)
                    if kind == "qk":
                        act.wait_ge(silu_done, j + 1)
                        act.activation(acc[b][:, 0:SEQ], act_row[b][:, :], ACT.Square).then_inc(sq_done, 1)

                def step(j, pair, b, j0, kind, first):
                    if first and b == 0:
                        split(j, pair, b, True)
                    if not (isinstance(j, int) and j == J_END - 1):
                        split(j + 1, pair + b, 1 - b, first and b == 0)
                    for t in range(NB):
                        act.wait_ge(projected, j * NB + t + 1)
                        if t == 0:
                            if first:
                                pass
                            elif kind in ("qk", "v"):
                                act.wait_ge(tap, (j - 1) * CONV_K)
                            elif kind == "u":
                                if not (at(j, J_U) or at(j, J_U + 1)):
                                    act.wait_ge(row_free, j - J_U - 1)
                            else:
                                act.wait_ge(stored[b], pair * 16)
                        if kind in ("qk", "v", "u"):
                            dst = row[b][:, PAD + t * TB:PAD + (t + 1) * TB]
                        else:
                            dst = act_row[b][:, t * TB:(t + 1) * TB]
                        act.activation(dst, ps[t][:, :], ACT.Copy).then_inc(evacuated, 1)
                    if kind in ("qk", "v") and not at(j, 0) or at(j, J_U):
                        prev = "v" if at(j, J_U) or kind == "v" and not at(j, J_V) else "qk"
                        silu(j - 1, pair - 1 + b, 1 - b, prev, at(j, 1) or at(j, 2))
                    if kind == "lg":
                        act.wait_ge(lg_t, 1)
                        for n in range(4):
                            act.activation(sh.logits[:, 4 * n:4 * n + 4, :],
                                           ps[4 + n][:, :].rearrange("p (c n) -> p c n", n=P)[:, :, 96:128],
                                           ACT.Copy).then_inc(lg_out, 1)

                each_tile(act, step)

            @block.vector
            def _(dve):
                dve.wait_ge(padded, 4)

                def conv(j, b):
                    dve.wait_ge(evacuated, (j + 1) * NB)
                    for n in range(CONV_K):
                        src = row[b][:, PAD - CONV_K // 2 + n:PAD - CONV_K // 2 + n + SEQ]
                        w = sh.cols[:, bass.ds(j + 24 * n, 1)]
                        if n:
                            dve.wait_ge(tap, j * CONV_K + n)
                            dve.scalar_tensor_tensor(acc[b][:, 0:SEQ], src, w, acc[b][:, 0:SEQ], ALU.mult,
                                                     ALU.add).then_inc(tap, 1)
                        else:
                            dve.tensor_scalar(acc[b][:, 0:SEQ], src, w, None, ALU.mult).then_inc(tap, 1)

                def sums_out(j, b):
                    dve.wait_ge(ss_done, j + 1)
                    dve.tensor_copy(sh.sumsq[:, bass.ds(j, 1), :],
                                    ps[4 + b][:, 0:NT].unsqueeze(1)).then_inc(ss_out, 1)

                n_window = [0]

                def windows(j, b, g):
                    dve.wait_ge(evacuated, (j + 1) * NB)
                    if j > J_U:
                        dve.wait_ge(row_free, j - J_U)
                    w = WINDOWS[g]
                    src, dst, m = row[b], acc[0], 1
                    n = CW - 1

                    def chained(ins):
                        n_window[0] += 1
                        ins.then_inc(window, 1)
                        dve.wait_ge(window, n_window[0])

                    while m < w:
                        chained(dve.tensor_tensor(dst[:, 0:n], src[:, 0:n], src[:, m:m + n], ALU.add))
                        m *= 2
                        n -= m
                        src, dst = dst, acc[1] if dst is acc[0] else acc[0]
                    at = PAD - w // 2
                    for side, p0 in ((0, at), (1, at + SEQ - PAD)):
                        e0 = CL["edge"][0] + (g * 2 + side) * PAD
                        chained(dve.tensor_tensor(src[:, p0:p0 + PAD], src[:, p0:p0 + PAD],
                                                  sh.consts[:, e0:e0 + PAD], ALU.mult))
                    dve.wait_ge(stored[b], (j // 2) * 16)
                    dve.scalar_tensor_tensor(act_row[b][:, :], src[:, at:at + SEQ], 1.0 / w,
                                             row[b][:, PAD:PAD + SEQ], ALU.mult, ALU.subtract).then_inc(row_free, 1)

                def step(j, pair, b, j0, kind, first):
                    if kind == "v" and not isinstance(j, int):
                        dve.wait_ge(silu_done, j - 1)
                    elif not first:
                        dve.wait_ge(ss_done, j - 1)
                    conv(j, b)
                    if kind == "qk" and not at(j, 0) or at(j, J_V):
                        sums_out(j - 1, 1 - b)

                each_tile(dve, step, segments[:2])
                dve.wait_ge(silu_done, J_U)
                for j in range(J_U, J_LG):
                    windows(j, j % 2, (j - J_U) // 2)

FIELDS = ("neg_gc", "neg_eg", "e_last", "e_to_last", "w", "norm_k")
NF = len(FIELDS)
GROUPS = 2
HG = H // GROUPS


def stage_gates(nc, a, sh):
    with ExitStack() as es:
        sb = lambda name, shape, dt=F32: es.enter_context(nc.sbuf_tensor("gt_" + name, shape, dt))
        sem = lambda name: sh.es.enter_context(nc.semaphore("gt_" + name))
        rate = sb("rate", [P, 16])
        dt_b = sb("dt_b", [P, 16])
        half = [P, NT, 16]
        x, mag, z, z2, poly, soft, g = (sb(n, half) for n in ("x", "mag", "z", "z2", "poly", "soft", "g"))
        beta = sb("beta", half)
        nk2, nq2 = sb("nk2", [P, NT, H]), sb("nq2", [P, NT, H])
        nk, nq = sb("nk", [P, NT, H]), sb("nq", [P, NT, H])
        tmp = sb("tmp", [P, NT, H])
        gc_s, gl_s = sb("gc_s", [P, 2, NT, H]), sb("gl_s", [P, 2, NT, H])
        gct = sb("gct", [P, 2, P])
        params_in, more_in, gct_done, gc_stored = sem("params_in"), sem("consts_in"), sem("gct_done"), sem("gc_stored")
        v, s, mm = sem("vector_step"), sem("scalar_step"), sem("sums")
        ps = sh.ps

        def view(dr, field):
            f = FIELDS.index(field)
            return sh.tables[:, dr, :, :, f, :]

        def by_group(ap):
            return ap.rearrange("p c (g h) -> p c g h", g=GROUPS)

        with nc.Block() as block:
            @block.sync
            def _(sp):
                sp.dma_start(sh.consts_late[:, :], a["consts"][:, CN_EARLY:CN]).then_inc(more_in, 16)
                sp.dma_start(rate[:, :], a["a_log"].rearrange("o d h -> o (d h)").broadcast_to((P, 16))).then_inc(params_in, 16)
                sp.dma_start(dt_b[:, :], a["dt_bias"].rearrange("o d h -> o (d h)").broadcast_to((P, 16))).then_inc(params_in, 16)
                sp.wait_ge(gct_done, 2)
                sp.dma_start(sh.gc_rows.rearrange("d n t -> n d t"), gct[:, :, :]).then_inc(gc_stored, 16)
                sp.wait_ge(gc_stored, 16)

            @block.vector
            def _(dve):
                n = [0]

                def then(ins):
                    n[0] += 1
                    ins.then_inc(v, 1)
                    dve.wait_ge(v, n[0])

                tt, ts, stt = dve.tensor_tensor, dve.tensor_scalar, dve.scalar_tensor_tensor
                dve.wait_ge(params_in, 32)
                then(tt(x[:, :, :], sh.logits[:, :, 16:32], dt_b[:, :].unsqueeze(1).broadcast_to((P, NT, 16)), ALU.add))
                then(ts(z[:, :, :], x[:, :, :], -1.0, None, ALU.mult))
                then(tt(mag[:, :, :], x[:, :, :], z[:, :, :], ALU.max))
                then(ts(beta[:, :, :], sh.logits[:, :, 0:16], -80.0, None, ALU.max))
                dve.wait_ge(s, 2)
                then(ts(z[:, :, :], z2[:, :, :], 2.0, None, ALU.add))
                then(dve.reciprocal(z[:, :, :], z[:, :, :]))
                then(tt(z[:, :, :], z2[:, :, :], z[:, :, :], ALU.mult))
                then(tt(z2[:, :, :], z[:, :, :], z[:, :, :], ALU.mult))
                terms = [2.0 / (2 * k + 1) for k in range(8)]
                then(ts(poly[:, :, :], z2[:, :, :], terms[7], terms[6], ALU.mult, ALU.add))
                for k in range(5, -1, -1):
                    then(tt(poly[:, :, :], poly[:, :, :], z2[:, :, :], ALU.mult))
                    then(ts(poly[:, :, :], poly[:, :, :], terms[k], None, ALU.add))
                then(tt(poly[:, :, :], poly[:, :, :], z[:, :, :], ALU.mult))
                then(stt(soft[:, :, :], x[:, :, :], 0.0, poly[:, :, :], ALU.max, ALU.add))
                dve.wait_ge(s, 3)
                then(stt(g[:, :, :], soft[:, :, :], -1.0, rate[:, :].unsqueeze(1).broadcast_to((P, NT, 16)),
                         ALU.mult, ALU.mult))
                sh.g_ready = n[0]
                then(ts(beta[:, :, :], beta[:, :, :], 1.0, None, ALU.add))
                then(dve.reciprocal(beta[:, :, :], beta[:, :, :]))
                then(ts(nk2[:, :, :], sh.sumsq[:, 8:16, :].rearrange("p h c -> p c h"), EPS, None, ALU.add))
                then(ts(nq2[:, :, :], sh.sumsq[:, 0:8, :].rearrange("p h c -> p c h"), EPS, None, ALU.add))
                sh.norms_ready = n[0]
                then(dve.reciprocal(tmp[:, :, :], nk2[:, :, :]))
                for dr in range(2):
                    then(tt(view(dr, "w"), by_group(tmp[:, :, :]), by_group(beta[:, :, dr * H:dr * H + H]), ALU.mult))
                dve.wait_ge(s, 5)
                for dr in range(2):
                    then(dve.tensor_copy(view(dr, "norm_k"), by_group(nk[:, :, :])))
                then(dve.reciprocal(sh.rq[:, :, :], nq[:, :, :]))
                dve.wait_ge(mm, 4)
                for dr in range(2):
                    then(dve.tensor_copy(gc_s[:, dr, :, :], ps[dr][:, 0:P].rearrange("p (c h) -> p c h", h=H)))
                    then(tt(gl_s[:, dr, :, :], ps[2 + dr][:, 0:P].rearrange("p (c h) -> p c h", h=H),
                            gc_s[:, dr, :, :], ALU.subtract))
                    then(ts(view(dr, "neg_gc"), by_group(gc_s[:, dr, :, :]), -1.0, None, ALU.mult))
                sh.sums_ready = n[0]
                for dr in range(2):
                    dve.wait_ge(mm, 5 + dr)
                    dve.tensor_copy(gct[:, dr, :], ps[4 + dr][:, 0:P]).then_inc(gct_done, 1)
                dve.wait_ge(s, 11)
                for dr in range(2):
                    then(ts(view(dr, "neg_eg"), by_group(gc_s[:, dr, :, :]), -1.0, None, ALU.mult))
                    then(dve.tensor_copy(view(dr, "e_last"), by_group(gl_s[:, dr, :, :])))

            @block.scalar
            def _(act):
                act.wait_ge(v, 3)
                act.activation(z2[:, :, :], mag[:, :, :], ACT.Exp, scale=-1.0).then_inc(s, 1)
                act.wait_ge(v, 4)
                act.activation(beta[:, :, :], beta[:, :, :], ACT.Exp, scale=-1.0).then_inc(s, 1)
                act.activation(rate[:, :], rate[:, :], ACT.Exp).then_inc(s, 1)
                act.wait_ge(v, sh.norms_ready)
                act.activation(nk[:, :, :], nk2[:, :, :], ACT.Sqrt).then_inc(s, 1)
                act.activation(nq[:, :, :], nq2[:, :, :], ACT.Sqrt).then_inc(s, 1)
                act.wait_ge(v, sh.sums_ready)
                act.wait_ge(mm, 6)
                for dr in range(2):
                    act.activation(view(dr, "e_to_last"), by_group(gl_s[:, dr, :, :]), ACT.Exp).then_inc(s, 1)
                    act.wait_ge(s, 6 + 3 * dr)
                    act.activation(gc_s[:, dr, :, :], gc_s[:, dr, :, :], ACT.Exp).then_inc(s, 1)
                    act.activation(gl_s[:, dr, :, :], ps[2 + dr][:, 0:P].rearrange("p (c h) -> p c h", h=H),
                                   ACT.Exp).then_inc(s, 1)

            @block.tensor
            def _(pe):
                pe.wait_ge(v, sh.g_ready)
                pe.wait_ge(more_in, 16)
                for dr, tri in ((0, "tri_f"), (1, "tri_b")):
                    gd = g[:, :, dr * H:dr * H + H]
                    pe.matmul(ps[dr][:, 0:P], sh.late(tri), gd, start=True, stop=True).then_inc(mm, 1)
                    pe.matmul(ps[2 + dr][:, 0:P], sh.late("ones"), gd, start=True, stop=True).then_inc(mm, 1)
                pe.wait_ge(v, sh.sums_ready)
                for dr in range(2):
                    pe.transpose(ps[4 + dr][:, 0:P], gc_s[:, dr, :, :].rearrange("p c h -> p (c h)"),
                                 sh.const("ident")).then_inc(mm, 1)


def stage_delta(nc, a, sh):
    with ExitStack() as es:
        sb = lambda name, shape, dt=F32: es.enter_context(nc.sbuf_tensor("dl_" + name, shape, dt))
        sems = lambda name: [sh.es.enter_context(nc.semaphore(f"dl_{name}_{d}")) for d in "fb"]
        quad = [P, HG, P]
        pair = lambda name, shape=quad: [sb(f"{name}_{d}", shape) for d in "fb"]
        pairs = lambda name, shape=quad: [pair(f"{name}{g}", shape) for g in range(GROUPS)]
        qkv = pairs("qkv", [P, 3, HG, P])
        cur = pairs("cur", [P, NF, HG])
        dmat, eb, lt, tm, ost = pair("dmat"), pair("eb"), pair("lt"), pair("tm"), pair("ost")
        at_, xm, kd, vp, qs = pairs("at"), pairs("xm"), pairs("kd"), pairs("vp"), pairs("qs")
        state = pairs("state")
        m_half, m_last = pair("m_half", [P, HG, 64]), pair("m_last")
        r, zs = pair("r"), pair("zs")
        z_raw = sb("z_raw", [P, KT, TB])
        zx = [sb(f"zx_{part}", [P, KT, TB], F32R) for part in ("hi", "lo")]
        zw, zw_hi, zw_lo = ([sb(f"{nm}{i}", [P, KT, P], dt) for i in range(2)]
                            for nm, dt in (("zw", F32), ("zw_hi", F32R), ("zw_lo", F32R)))
        z_row = [sb(f"z_row{i}", [P, TB]) for i in range(2)]

        loaded = [sems(f"loaded{g}") for g in range(GROUPS)]
        stored = sems("stored")
        sem = lambda name: sh.es.enter_context(nc.semaphore("dl_" + name))
        zw_in = [sem(f"zw_in{i}") for i in range(2)]
        z_stored = [sem(f"z_stored{i}") for i in range(2)]
        z_raw_in, zx_hi, zx_lo, zx_ready = map(sem, ("z_raw_in", "zx_hi", "zx_lo", "zx_ready"))
        z_hi, z_lo, z_out, z_proj = map(sem, ("z_hi", "z_lo", "z_out", "z_proj"))
        cleared = sems("cleared")
        cur_ready, gc_in, arg_done, eb_done, d_done = map(sems, ("cur_ready", "gc_in", "arg_done", "eb_done", "d_done"))
        kk_ps, kq_ps, kv_ps = map(sems, ("kk_ps", "kq_ps", "kv_ps"))
        turn_ps, turned = sems("turn_ps"), sems("turned")
        x_steps, at_done = map(sems, ("x_steps", "at_done"))
        kv_out, qs_done = map(sems, ("kv_out", "qs_done"))
        m_ps, m_out, join_ps, joined = map(sems, ("m_ps", "m_out", "join_ps", "joined"))
        ks_ps, r_done, y_ps, zs_done, o_ps, s_ps, o_out, s_done = map(
            sems, ("ks_ps", "r_done", "y_ps", "zs_done", "o_ps", "s_ps", "o_out", "s_done"))
        NL = len(LEVELS)
        ident = sh.const("ident")
        A, B, E, Z = ([sh.ps[4 * d + n] for d in range(2)] for n in range(4))

        def field(g, d, name):
            return cur[g][d][:, FIELDS.index(name), :]

        def scalar(g, d, name, u):
            return cur[g][d][:, FIELDS.index(name), u:u + 1]

        def quads(bank):
            return bank[:, :].rearrange("p (u i) -> p u i", u=HG)

        def blocks(ap, s, odd):
            return ap.rearrange("p u (b two s) -> p u b two s", two=2, s=s)[:, :, :, odd, :]

        def each_step(eng, step, written=(0,)):
            for c0, c1 in zip(written, written[1:] + (NT,)):
                for g in range(GROUPS):
                    step(c0 * 2 + g, c0, g)
                if c1 > c0 + 1:
                    with eng.Fori(c0 + 1, c1) as c:
                        for g in range(GROUPS):
                            step(c * 2 + g, c, g)

        def chunks(eng, c):
            return c, held(eng, NT - 1 - c, NT - 2)

        last_step = lambda n: isinstance(n, int) and n == NT * GROUPS - 1
        early = lambda n: isinstance(n, int) and n < GROUPS

        CB = NT // NB
        ZX_HALVES = (slice(0, KT // 2), slice(KT // 2, KT))
        block_at = [0]

        with nc.Block() as block:
            @block.sync
            def _(sp):
                def load(n, at, g, d):
                    if not early(n):
                        sp.wait_ge(ks_ps[d], n - 1)
                        sp.wait_ge(qs_done[d], n - 1)
                    for kind in range(3):
                        sp.dma_start(qkv[g][d][:, kind, :, :],
                                     sh.rows[kind * H + g * HG:kind * H + (g + 1) * HG, :,
                                             bass.ds(at * P, P)].rearrange("h p t -> p h t")
                                     ).then_inc(loaded[g][d], 16)

                def load_gc(n, at, g, d):
                    if not (early(n) and n == 0):
                        sp.wait_ge(at_done[d], n)
                    sp.dma_start(dmat[d][:, :, :].rearrange("p u i -> p (u i)").unsqueeze(1),
                                 sh.gc_rows[d, bass.ds(at * H + g * HG, HG), :].rearrange("u i -> (u i)")
                                 .rearrange("(o q n) -> o q n", o=1, q=1).broadcast_to((P, 1, HG * P))
                                 ).then_inc(gc_in[d], 16)

                def store(n, at, g, d):
                    sp.wait_ge(o_out[d], n + 1)
                    sp.dma_start(sh.o_rows[d, bass.ds(at * P, P), g * HG * P:(g + 1) * HG * P],
                                 ost[d][:, :, :].rearrange("p u e -> p (u e)")).then_inc(stored[d], 16)

                def load_weights(n, c, g, i):
                    if not (early(n) and n == 0):
                        sp.wait_ge(z_lo, n * 2 + i - 1)
                    tile = (c - block_at[0] * CB) * GROUPS + g
                    col = (OFF_ZD, OFF_ZP)[i] + tile * P
                    sp.dma_start(zw[i][:, :, :], a["w_in"][0, :, bass.ds(col, P)].rearrange("(k p) n -> p k n", p=P)
                                 ).then_inc(zw_in[i], 16)

                def load_tokens(t):
                    for m in range(TB // P):
                        sp.dma_start(z_raw[:, :, m * P:(m + 1) * P], sh.h_tiles[t * (TB // P) + m, :, :, :]
                                     ).then_inc(z_raw_in, 16)

                def step(n, c, g):
                    if isinstance(c, int):
                        block_at[0] = c // CB
                    here = chunks(sp, c)
                    for d in range(2):
                        load(n, here[d], g, d)
                    for d in range(2):
                        load_gc(n, here[d], g, d)
                    for i in range(2):
                        load_weights(n, c, g, i)
                    if not early(n):
                        before = c - 1, here[1] + 1
                        for d in range(2):
                            store(n - 2, before[d], g, d)
                    if g == 0:
                        if isinstance(c, int):
                            sp.wait_ge(zx_lo, (c // CB + 1) * 2)
                            if c // CB + 1 < NB:
                                load_tokens(c // CB + 1)
                        sp.sem_inc(zx_ready, 1)

                load_tokens(0)
                each_step(sp, step, tuple(range(0, NT, CB)))
                for g in range(GROUPS):
                    for d in range(2):
                        store((NT - 1) * 2 + g, (NT - 1, 0)[d], g, d)
                for d in range(2):
                    sp.wait_ge(stored[d], NT * GROUPS * 16)

            @block.gpsimd
            def _(pool):
                for d in range(2):
                    for g in range(GROUPS):
                        pool.memset(state[g][d][:, :, :], 0.0)
                    pool.memset(m_last[d][:, :, :], 0.0).then_inc(cleared[d], 1)

                def step(n, c, g):
                    for d in range(2):
                        pool.wait_ge(eb_done[d], n + 1)
                        pool.wait_ge(loaded[g][d], (c + 1) * 48)
                        if not early(n):
                            pool.wait_ge(o_ps[d], n - 1)
                        pool.tensor_tensor(qs[g][d][:, :, :], qkv[g][d][:, 0, :, :], eb[d][:, :, :],
                                           ALU.mult).then_inc(qs_done[d], 1)
                    if not last_step(n):
                        for i in range(2):
                            split(n + 1, i)

                def split(n, i):
                    pool.wait_ge(z_hi, n * 2 + i + 1)
                    pool.tensor_tensor(zw_lo[i][:, :, :], zw[i][:, :, :], zw_hi[i][:, :, :].bitcast(F32),
                                       ALU.subtract).then_inc(z_lo, 1)

                for i in range(2):
                    split(0, i)
                each_step(pool, step, (0, NT - 1))

            @block.tensor
            def _(pe):
                fill_at = [0]

                def fill(n, c, count):
                    for m in range(fill_at[0], fill_at[0] + count):
                        i, k, p = m // (3 * KT), m % (3 * KT) // 3, m % 3
                        if k == 0 and p == 0:
                            pe.wait_ge(zx_ready, c + 1)
                            pe.wait_ge(z_lo, n * 2 + i + 1)
                            if not (early(n) and n == 0):
                                pe.wait_ge(z_out, n * 2 + i - 1)
                        w, x = ((zw_hi, zx[0]), (zw_hi, zx[1]), (zw_lo, zx[0]))[p]
                        last = pe.matmul(Z[i][:, :], w[i][:, k, :], x[:, k, :],
                                         start=(k == 0 and p == 0), stop=(k == KT - 1 and p == 2))
                        if k == KT - 1 and p == 2:
                            last.then_inc(z_proj, 1)
                    fill_at[0] = (fill_at[0] + count) % (6 * KT)

                def prepare(n, c, g):
                    for d in range(2):
                        pe.wait_ge(loaded[g][d], (c + 1) * 48)
                        if not (early(n) and n == 0):
                            pe.wait_ge(joined[d], n * NL)
                        for u in range(HG):
                            k = qkv[g][d][:, 1, u, :]
                            last = pe.matmul(quads(B[d])[:, u, :], k, k, start=True, stop=True)
                        last.then_inc(kk_ps[d], 1)
                    fill(n, c, 4)
                    for d in range(2):
                        if not early(n):
                            pe.wait_ge(s_done[d], n - 1)
                        for u in range(HG):
                            last = pe.transpose(quads(E[d])[:, u, :], qkv[g][d][:, 1, u, :], ident)
                        last.then_inc(kv_ps[d], 1)
                    fill(n, c, 4)
                    for d in range(2):
                        if not (early(n) and n == 0):
                            pe.wait_ge(m_out[d], n * NL)
                        for u in range(HG):
                            last = pe.matmul(quads(A[d])[:, u, :], qkv[g][d][:, 1, u, :], qkv[g][d][:, 0, u, :],
                                             start=True, stop=True)
                        last.then_inc(kq_ps[d], 1)
                    fill(n, c, 4)
                    for d in range(2):
                        pe.wait_ge(kv_out[d], n * 2 + 1)
                        for u in range(HG):
                            last = pe.transpose(quads(E[d])[:, u, :], qkv[g][d][:, 2, u, :], ident)
                        last.then_inc(kv_ps[d], 1)
                    fill(n, c, 4)
                    for d in range(2):
                        pe.wait_ge(x_steps[d], n * 3 + 3)
                        for u in range(HG):
                            last = pe.transpose(quads(B[d])[:, u, :], xm[g][d][:, u, :], ident)
                        last.then_inc(turn_ps[d], 1)

                def level_m(n, g, l):
                    s = LEVELS[l]
                    for d in range(2):
                        if l == 0:
                            pe.wait_ge(turned[d], n * NL + 1)
                            pe.wait_ge(at_done[d], n + 1)
                        else:
                            pe.wait_ge(joined[d], n * NL + l)
                        for u in range(HG):
                            last = pe.matmul(A[d][:, u * 64:(u + 1) * 64], lt[d][:, u, :],
                                             blocks(tm[d][:, :, :], s, d)[:, u], start=True, stop=True)
                        last.then_inc(m_ps[d], 1)

                def level_turn(n, g, l):
                    for d in range(2):
                        pe.wait_ge(joined[d], n * NL + l + 1)
                        for u in range(HG):
                            last = pe.transpose(quads(B[d])[:, u, :], tm[d][:, u, :], ident)
                        last.then_inc(turn_ps[d], 1)

                def level_join(n, g, l):
                    s = LEVELS[l]
                    for d in range(2):
                        pe.wait_ge(m_out[d], n * NL + l + 1)
                        pe.wait_ge(turned[d], n * NL + l + 1)
                        for u in range(HG):
                            if l < NL - 1:
                                last = pe.matmul(B[d][:, u * 64:(u + 1) * 64], xm[g][d][:, u, :],
                                                 m_half[d][:, u, :], start=True, stop=True)
                            else:
                                last = pe.matmul(B[d][:, u * 64:(u + 1) * 64], m_last[d][:, u, :],
                                                 blocks(xm[g][d][:, :, :], s, 1 - d)[:, u], start=True, stop=True)
                        last.then_inc(join_ps[d], 1)

                def scan_ks(n, g, final):
                    for d in range(2):
                        if early(n):
                            pe.wait_ge(cleared[d], 1)
                        else:
                            pe.wait_ge(s_done[d], n - 1)
                        if final:
                            pe.wait_ge(s_done[d], n)
                        else:
                            pe.wait_ge(kv_out[d], n * 2 + 4)
                        for u in range(HG):
                            last = pe.matmul(quads(E[d])[:, u, :], qkv[g][d][:, 1, u, :], state[g][d][:, u, :],
                                             start=True, stop=True)
                        last.then_inc(ks_ps[d], 1)

                def scan_y(n, g, final):
                    for d in range(2):
                        pe.wait_ge(r_done[d], n + 1)
                        if final:
                            pe.wait_ge(joined[d], (n + 1) * NL)
                        for u in range(HG):
                            last = pe.matmul(quads(E[d])[:, u, :], xm[g][d][:, u, :], r[d][:, u, :],
                                             start=True, stop=True)
                        last.then_inc(y_ps[d], 1)

                def scan_o(n, g):
                    for d in range(2):
                        pe.wait_ge(zs_done[d], n + 1)
                        pe.wait_ge(qs_done[d], n + 1)
                        for u in range(HG):
                            pe.matmul(quads(E[d])[:, u, :], qs[g][d][:, u, :], state[g][d][:, u, :],
                                      start=True, stop=False)
                            last = pe.matmul(quads(E[d])[:, u, :], at_[g][d][:, u, :], zs[d][:, u, :],
                                             start=False, stop=True)
                        last.then_inc(o_ps[d], 1)

                def scan_s(n, g):
                    for d in range(2):
                        pe.wait_ge(o_out[d], n + 1)
                        for u in range(HG):
                            last = pe.matmul(quads(E[d])[:, u, :], kd[g][d][:, u, :], zs[d][:, u, :],
                                             start=True, stop=True)
                        last.then_inc(s_ps[d], 1)

                def step(n, c, g):
                    scan = not (early(n) and n == 0)
                    prepare(n, c, g)
                    for l in range(NL):
                        level_m(n, g, l)
                        if l:
                            level_turn(n, g, l - 1)
                        fill(n, c, (3, 3, 3, 3, 3, 3)[l])
                        if scan and l == 0:
                            scan_ks(n - 1, 1 - g, False)
                        if scan and l == 1:
                            scan_y(n - 1, 1 - g, False)
                        if scan and l == 2:
                            scan_o(n - 1, 1 - g)
                        if scan and l == 3:
                            scan_s(n - 1, 1 - g)
                        level_join(n, g, l)
                        fill(n, c, (3, 3, 2, 2, 2, 2)[l])

                each_step(pe, step)
                n = NT * GROUPS - 1
                scan_ks(n, 1, True)
                scan_y(n, 1, True)
                scan_o(n, 1)
                scan_s(n, 1)

            @block.scalar
            def _(act):
                def prepare(n, c, g):
                    for d in range(2):
                        act.wait_ge(gc_in[d], (n + 1) * 16)
                        if not (early(n) and n == 0):
                            act.wait_ge(qs_done[d], n)
                        act.activation(eb[d][:, :, :], dmat[d][:, :, :], ACT.Exp).then_inc(eb_done[d], 1)
                    for d in range(2):
                        act.wait_ge(cur_ready[d], n + 1)
                        act.wait_ge(arg_done[d], n + 1)
                        for u in range(HG):
                            last = act.activation(dmat[d][:, u, :], dmat[d][:, u, :], ACT.Exp,
                                                  bias=scalar(g, d, "neg_gc", u))
                        last.then_inc(d_done[d], 1)
                    for d in range(2):
                        act.wait_ge(kv_ps[d], n * 2 + 1)
                        if not early(n):
                            act.wait_ge(s_ps[d], n - 1)
                        for u in range(HG):
                            last = act.activation(kd[g][d][:, u, :], quads(E[d])[:, u, :], ACT.Copy,
                                                  scale=scalar(g, d, "e_to_last", u))
                        last.then_inc(kv_out[d], 1)
                    for d in range(2):
                        act.wait_ge(kv_ps[d], n * 2 + 2)
                        if not early(n):
                            act.wait_ge(r_done[d], n - 1)
                        for u in range(HG):
                            last = act.activation(vp[g][d][:, u, :], quads(E[d])[:, u, :], ACT.Copy,
                                                  scale=scalar(g, d, "norm_k", u))
                        last.then_inc(kv_out[d], 1)
                    for d in range(2):
                        act.wait_ge(turn_ps[d], n * NL + 1)
                        act.activation(tm[d][:, :, :], quads(B[d]), ACT.Copy).then_inc(turned[d], 1)

                def level_turn(n, g, l):
                    for d in range(2):
                        act.wait_ge(turn_ps[d], n * NL + l + 2)
                        act.activation(xm[g][d][:, :, :], quads(B[d]), ACT.Copy).then_inc(turned[d], 1)

                def scan_z(n, g):
                    for d in range(2):
                        act.wait_ge(y_ps[d], n + 1)
                        if not (early(n) and n == 0):
                            act.wait_ge(s_ps[d], n)
                        for u in range(HG):
                            last = act.activation(zs[d][:, u, :], quads(E[d])[:, u, :], ACT.Copy,
                                                  scale=scalar(g, d, "w", u))
                        last.then_inc(zs_done[d], 1)

                def scan_out(n, g):
                    for d in range(2):
                        act.wait_ge(o_ps[d], n + 1)
                        if not (early(n) and n == 0):
                            act.wait_ge(stored[d], n * 16)
                        act.activation(ost[d][:, :, :], quads(E[d]), ACT.Copy).then_inc(o_out[d], 1)

                def split_tokens(c):
                    act.wait_ge(z_raw_in, (c // CB + 1) * (TB // P) * 16)
                    if c:
                        act.wait_ge(z_proj, c * 2 * GROUPS)
                    for part in ZX_HALVES:
                        act.activation(zx[0][:, part, :], z_raw[:, part, :], ACT.Copy).then_inc(zx_hi, 1)

                def split(n, i):
                    act.wait_ge(zw_in[i], (n + 1) * 16)
                    if not (early(n) and n == 0):
                        act.wait_ge(z_proj, n * 2 + i - 1)
                    act.activation(zw_hi[i][:, :, :], zw[i][:, :, :], ACT.Copy).then_inc(z_hi, 1)

                def gate(n, c, g, i):
                    act.wait_ge(z_proj, n * 2 + i + 1)
                    if not (early(n) and n == 0):
                        act.wait_ge(z_stored[i], n * 16)
                    act.activation(z_row[i][:, :], Z[i][:, :], ACT.Copy).then_inc(z_out, 1)
                    if not last_step(n):
                        split(n + 1, i)
                    act.wait_ge(z_out, n * 2 + i + 1)
                    row = (R_ZD, R_ZP)[i] + (c - block_at[0] * CB) * GROUPS + g
                    act.dma_start(sh.rows[bass.ds(row, 1), :, block_at[0] * TB:(block_at[0] + 1) * TB]
                                  .rearrange("o p t -> (o p) t"), z_row[i][:, :]).then_inc(z_stored[i], 16)

                def step(n, c, g):
                    if isinstance(c, int):
                        block_at[0] = c // CB
                        if g == 0 and c % CB == 0:
                            split_tokens(c)
                    scan = not (early(n) and n == 0)
                    prepare(n, c, g)
                    level_turn(n, g, 0)
                    if scan:
                        scan_z(n - 1, 1 - g)
                    level_turn(n, g, 1)
                    gate(n, c, g, 0)
                    if scan:
                        scan_out(n - 1, 1 - g)
                    for l in range(2, NL - 1):
                        level_turn(n, g, l)
                    gate(n, c, g, 1)

                for i in range(2):
                    split(0, i)
                each_step(act, step, tuple(sorted({*range(0, NT, CB), NT - 1})))
                scan_z(NT * GROUPS - 1, 1)
                scan_out(NT * GROUPS - 1, 1)
                for i in range(2):
                    act.wait_ge(z_stored[i], NT * GROUPS * 16)

            @block.vector
            def _(dve):
                def prepare(n, c, g):
                    here = chunks(dve, c)
                    for d in range(2):
                        if not early(n):
                            dve.wait_ge(zs_done[d], n - 1)
                            dve.wait_ge(s_done[d], n - 1)
                        dve.tensor_copy(cur[g][d][:, :, :].unsqueeze(1),
                                        sh.tables[:, d, bass.ds(here[d], 1), g, :, :]).then_inc(cur_ready[d], 1)
                    for d in range(2):
                        dve.wait_ge(gc_in[d], (n + 1) * 16)
                        dve.wait_ge(eb_done[d], n + 1)
                        mask = sh.late(("mask_f", "mask_b")[d]).unsqueeze(1).broadcast_to((P, HG, P))
                        dve.tensor_tensor(dmat[d][:, :, :], dmat[d][:, :, :], mask, ALU.add).then_inc(arg_done[d], 1)
                    for d in range(2):
                        dve.wait_ge(cur_ready[d], n + 1)
                        dve.wait_ge(d_done[d], n + 1)
                        dve.wait_ge(kk_ps[d], n + 1)
                        for u in range(HG):
                            last = dve.scalar_tensor_tensor(lt[d][:, u, :], quads(B[d])[:, u, :], scalar(g, d, "w", u),
                                                            dmat[d][:, u, :], ALU.mult, ALU.mult)
                        last.then_inc(x_steps[d], 1)
                    for d in range(2):
                        dve.wait_ge(x_steps[d], n * 3 + 1)
                        if not early(n):
                            dve.wait_ge(y_ps[d], n - 1)
                        neg1 = sh.late(("neg1_f", "neg1_b")[d]).unsqueeze(1).broadcast_to((P, HG, P))
                        dve.tensor_tensor(xm[g][d][:, :, :], lt[d][:, :, :], neg1, ALU.mult).then_inc(x_steps[d], 1)
                    for d in range(2):
                        dve.wait_ge(x_steps[d], n * 3 + 2)
                        dve.tensor_tensor(xm[g][d][:, :, :], xm[g][d][:, :, :],
                                          ident.unsqueeze(1).broadcast_to((P, HG, P)), ALU.add).then_inc(x_steps[d], 1)
                    for d in range(2):
                        dve.wait_ge(kq_ps[d], n + 1)
                        if not early(n):
                            dve.wait_ge(o_ps[d], n - 1)
                        dve.tensor_tensor(at_[g][d][:, :, :], quads(A[d]), dmat[d][:, :, :],
                                          ALU.mult).then_inc(at_done[d], 1)

                def level_mask(n, g, l):
                    s = LEVELS[l]
                    for d in range(2):
                        dve.wait_ge(m_ps[d], n * NL + l + 1)
                        c0 = CL[("level_f", "level_b")[d]][0] - CN_EARLY + l * 64
                        mask = sh.consts_late[:, c0:c0 + 64].rearrange("p (b s) -> p b s", s=s)
                        if l < NL - 1:
                            m = m_half[d][:, :, :].rearrange("p u (b s) -> p u b s", s=s)
                        else:
                            if early(n) and n == 0:
                                dve.wait_ge(cleared[d], 1)
                            m = blocks(m_last[d][:, :, :], s, d)
                        dve.tensor_tensor(m, A[d][:, 0:256].rearrange("p (u b s) -> p u b s", u=HG, s=s),
                                          mask.unsqueeze(1).broadcast_to((P, HG, 64 // s, s)),
                                          ALU.mult).then_inc(m_out[d], 1)

                def level_update(n, g, l):
                    s = LEVELS[l]
                    for d in range(2):
                        dve.wait_ge(join_ps[d], n * NL + l + 1)
                        if l < NL - 1:
                            old = blocks(tm[d][:, :, :], s, d)
                        else:
                            old = blocks(xm[g][d][:, :, :], s, 1 - d)
                        dve.tensor_tensor(old, old, B[d][:, 0:256].rearrange("p (u b s) -> p u b s", u=HG, s=s),
                                          ALU.subtract).then_inc(joined[d], 1)

                def scan_r(n, g):
                    for d in range(2):
                        dve.wait_ge(ks_ps[d], n + 1)
                        if not (early(n) and n == 0):
                            dve.wait_ge(y_ps[d], n)
                        for u in range(HG):
                            last = dve.scalar_tensor_tensor(r[d][:, u, :], quads(E[d])[:, u, :],
                                                            scalar(g, d, "neg_eg", u), vp[g][d][:, u, :],
                                                            ALU.mult, ALU.add)
                        last.then_inc(r_done[d], 1)

                def scan_state(n, g):
                    for d in range(2):
                        dve.wait_ge(s_ps[d], n + 1)
                        for u in range(HG):
                            last = dve.scalar_tensor_tensor(state[g][d][:, u, :], state[g][d][:, u, :],
                                                            scalar(g, d, "e_last", u), quads(E[d])[:, u, :],
                                                            ALU.mult, ALU.add)
                        last.then_inc(s_done[d], 1)

                def split_tokens(c):
                    for half, part in enumerate(ZX_HALVES):
                        dve.wait_ge(zx_hi, c // CB * 2 + half + 1)
                        dve.tensor_tensor(zx[1][:, part, :], z_raw[:, part, :], zx[0][:, part, :].bitcast(F32),
                                          ALU.subtract).then_inc(zx_lo, 1)

                def step(n, c, g):
                    if g == 0 and isinstance(c, int):
                        split_tokens(c)
                    scan = not (early(n) and n == 0)
                    prepare(n, c, g)
                    for l in range(NL):
                        level_mask(n, g, l)
                        level_update(n, g, l)
                        if scan and l == 0:
                            scan_r(n - 1, 1 - g)
                        if scan and l == 3:
                            scan_state(n - 1, 1 - g)

                each_step(dve, step, tuple(range(0, NT, CB)))
                scan_r(NT * GROUPS - 1, 1)
                scan_state(NT * GROUPS - 1, 1)

N_POOL = len(WINDOWS)
PK = POOL_W // N_POOL // P


def stage_pool(nc, a, sh):
    with ExitStack() as es:
        sb = lambda name, shape, dt=F32: es.enter_context(nc.sbuf_tensor("po_" + name, shape, dt))
        sem = lambda name: sh.es.enter_context(nc.semaphore("po_" + name))
        two = lambda name, shape, dt=F32: [sb(f"{name}{b}", shape, dt) for b in range(2)]
        m, m_hi, m_lo = two("m", [P, PK, SEQ]), two("m_hi", [P, PK, SEQ], F32R), two("m_lo", [P, PK, SEQ], F32R)
        w, w_hi, w_lo = (two("w", [P, PK, PK * P]), two("w_hi", [P, PK, PK * P], F32R),
                         two("w_lo", [P, PK, PK * P], F32R))
        gate, y = two("gate", [P, PK, SEQ]), two("y", [P, SEQ])
        loaded = [sem(f"loaded{b}") for b in range(2)]
        stored = [sem(f"stored{b}") for b in range(2)]
        hi, lo, silu, mapped, gated = sem("hi"), sem("lo"), sem("silu"), sem("mapped"), sem("gated")
        ps = sh.ps

        with nc.Block() as block:
            @block.sync
            def _(sp):
                for g in range(N_POOL):
                    b = g % 2
                    if g >= 2:
                        sp.wait_ge(gated, (g - 1) * PK * NB)
                    for dst, row in ((m[b], J_U + PK * g), (gate[b], R_ZP + PK * g)):
                        sp.dma_start(dst[:, :, :], sh.rows[row:row + PK, :, :].rearrange("k p t -> p k t")
                                     ).then_inc(loaded[b], 16)
                    sp.dma_start(w[b][:, :, :], a["pool_w"][0, g].rearrange("(k p) n -> p k n", p=P)
                                 ).then_inc(loaded[b], 16)
                for b in range(2):
                    sp.wait_ge(stored[b], N_POOL * PK // 2 * 16)

            @block.scalar
            def _(act):
                for g in range(N_POOL):
                    b = g % 2
                    act.wait_ge(loaded[b], (g // 2 + 1) * 48)
                    if g >= 2:
                        act.wait_ge(mapped, (g - 1) * PK * NB)
                    act.activation(w_hi[b][:, :, :], w[b][:, :, :], ACT.Copy).then_inc(hi, 1)
                    for k in range(PK):
                        act.activation(m_hi[b][:, k, :], m[b][:, k, :], ACT.Copy).then_inc(hi, 1)
                    for k in range(PK):
                        act.activation(gate[b][:, k, :], gate[b][:, k, :], ACT.Silu).then_inc(silu, 1)

            @block.gpsimd
            def _(pool):
                for g in range(N_POOL):
                    for o in range(PK):
                        n = g * PK + o
                        pool.wait_ge(gated, (n + 1) * NB)
                        pool.dma_start(sh.yp_rows[n, :, :], y[o][:, :]).then_inc(stored[o], 16)

            @block.vector
            def _(dve):
                def split(g):
                    b = g % 2
                    dve.wait_ge(hi, g * (PK + 1) + 1)
                    dve.tensor_tensor(w_lo[b][:, :, :], w[b][:, :, :], w_hi[b][:, :, :].bitcast(F32),
                                      ALU.subtract).then_inc(lo, 1)
                    for k in range(PK):
                        dve.wait_ge(hi, g * (PK + 1) + k + 2)
                        dve.tensor_tensor(m_lo[b][:, k, :], m[b][:, k, :], m_hi[b][:, k, :].bitcast(F32),
                                          ALU.subtract).then_inc(lo, 1)

                split(0)
                for g in range(N_POOL):
                    if g + 1 < N_POOL:
                        split(g + 1)
                    for o in range(PK):
                        n = g * PK + o
                        dve.wait_ge(silu, n + 1)
                        if g:
                            dve.wait_ge(stored[o], g * 16)
                        for t in range(NB):
                            dve.wait_ge(mapped, n * NB + t + 1)
                            dve.scalar_tensor_tensor(y[o][:, t * TB:(t + 1) * TB], ps[o * NB + t][:, :],
                                                     sh.cols[:, P + n:P + n + 1],
                                                     gate[g % 2][:, o, t * TB:(t + 1) * TB],
                                                     ALU.mult, ALU.mult).then_inc(gated, 1)

            @block.tensor
            def _(pe):
                for g in range(N_POOL):
                    b = g % 2
                    pe.wait_ge(lo, (g + 1) * (PK + 1))
                    for o in range(PK):
                        for t in range(NB):
                            if g:
                                pe.wait_ge(gated, ((g - 1) * PK + o) * NB + t + 1)
                            for k in range(PK):
                                for wp, mp in ((w_hi, m_hi), (w_hi, m_lo), (w_lo, m_hi)):
                                    last = pe.matmul(ps[o * NB + t][:, :], wp[b][:, k, o * P:(o + 1) * P],
                                                     mp[b][:, k, t * TB:(t + 1) * TB],
                                                     start=(k == 0 and mp is m_hi and wp is w_hi),
                                                     stop=(k == PK - 1 and wp is w_lo))
                            last.then_inc(mapped, 1)


EK = MIX_W // P


def stage_output(nc, a, sh, out):
    with ExitStack() as es:
        sb = lambda name, shape, dt=F32: es.enter_context(nc.sbuf_tensor("ou_" + name, shape, dt))
        sem = lambda name: sh.es.enter_context(nc.semaphore("ou_" + name))
        two = lambda name, shape, dt=F32: [sb(f"{name}{b}", shape, dt) for b in range(2)]
        w_hi, w_lo = sb("w_hi", [P, EK, D], F32R), sb("w_lo", [P, EK, D], F32R)
        o_f, o_b, x = two("o_f", [P, D]), two("o_b", [P, D]), two("x", [P, D])
        y, y_hi, y_lo = sb("y", [P, EK, P]), two("y_hi", [P, EK, P], F32R), two("y_lo", [P, EK, P], F32R)
        gate = sb("gate", [P, H, P])
        done = sb("done", [P, D])
        w_raw = [done, x[1], o_f[1], o_b[1]]
        fnw = sb("fnw", [P, D])
        qf, qf2 = sb("qf", [P, NT, H]), sb("qf2", [P, NT, H])
        st = two("st", [P, 4, H])
        minus_half = sb("minus_half", [P, H])
        w_loaded = [sem(f"w_loaded{i}") for i in range(len(w_raw))]
        w_split_hi, w_split = sem("w_split_hi"), sem("w_split")
        o_loaded = [sem(f"o_loaded{b}") for b in range(2)]
        x_loaded = [sem(f"x_loaded{b}") for b in range(2)]
        gate_in, gate_on, res_arg = sem("gate_in"), sem("gate_on"), sem("res_arg")
        stored = sem("stored")
        const_in, const_set = sem("const_in"), sem("const_set")
        o_sum, o_sq, o_rstd, o_norm = map(sem, ("o_sum", "o_sq", "o_rstd", "o_norm"))
        o_stat = sem("o_stat")
        turned, gated, hi_p, hi_d, lo_p, lo_d = map(sem, ("turned", "gated", "hi_p", "hi_d", "lo_p", "lo_d"))
        out_ps, res, res_sq, res_rstd, final = map(
            sem, ("out_ps", "res", "res_sq", "res_rstd", "final"))
        ps, ident = sh.ps, sh.const("ident")
        heads = lambda ap: ap.rearrange("p (h e) -> p h e", h=H)

        def each_tile(eng, step, peel_last=False):
            for b in range(2):
                step(b, 0, b, True)
            with eng.Fori(1, NT // 2 - peel_last) as n:
                for b in range(2):
                    step(n * 2 + b, n, b, False)
            if peel_last:
                for b in range(2):
                    step(NT - 2 + b, NT // 2 - 1, b, False)

        is0 = lambda t: isinstance(t, int) and t == 0

        with nc.Block() as block:
            @block.sync
            def _(sp):
                sp.dma_start(fnw[:, :], a["final_norm_w"].rearrange("(o n) -> o n", o=1).broadcast_to((P, D))
                             ).then_inc(const_in, 16)

                def load_o(b, row):
                    for dst, d in ((o_f[b], 0), (o_b[b], 1)):
                        sp.dma_start(dst[:, :], sh.o_rows[d, bass.ds(row, P), :]).then_inc(o_loaded[b], 16)

                def load_x(b, row):
                    sp.dma_start(x[b][:, :], a["x"][0, bass.ds(row, P), :]).then_inc(x_loaded[b], 16)

                def store(t):
                    sp.wait_ge(final, t + 1)
                    sp.dma_start(out[0, bass.ds(t * P, P), :], done[:, :]).then_inc(stored, 16)

                load_o(0, 0)
                for i in range(EK):
                    if i >= len(w_raw):
                        sp.wait_ge(w_split, i - len(w_raw) + 1)
                    sp.dma_start(w_raw[i % len(w_raw)][:, :], a["w_out"][0, i * P:(i + 1) * P, :]
                                 ).then_inc(w_loaded[i % len(w_raw)], 16)
                load_x(0, 0)
                sp.wait_ge(w_split, EK)
                load_o(1, P)
                load_x(1, P)
                with sp.Fori(1, NT // 2) as n:
                    for b in range(2):
                        t = n * 2 + b
                        row, turned_before = held(sp, t * P, SEQ - P), held(sp, t - 1, NT)
                        before = held(sp, t - 2, NT - 3)
                        sp.wait_ge(turned, turned_before)
                        load_o(b, row)
                        store(before)
                        load_x(b, row)
                for b in range(2):
                    store(NT - 2 + b)
                sp.wait_ge(stored, NT * 16)

            @block.gpsimd
            def _(pool):
                def load(t):
                    pool.dma_start(y[:, 0:H, :], sh.yp_rows[:, :, bass.ds(t * P, P)].rearrange("k p t -> p k t")
                                   ).then_inc(gate_in, 16)
                    pool.dma_start(gate[:, :, :], sh.rows[R_ZD:R_ZP, :, bass.ds(t * P, P)].rearrange("k p t -> p k t")
                                   ).then_inc(gate_in, 16)

                def step(t, n, b, first):
                    pool.wait_ge(o_stat, t * 4 + 3)
                    pool.tensor_tensor(st[b][:, 0, :], st[b][:, 1, :], minus_half[:, :], ALU.pow).then_inc(o_rstd, 1)
                    pool.wait_ge(hi_p, t + 1)
                    pool.tensor_tensor(y_lo[b][:, 0:H, :], y[:, 0:H, :], y_hi[b][:, 0:H, :].bitcast(F32),
                                       ALU.subtract).then_inc(lo_p, 1)
                    if not (isinstance(t, int) and t == NT - 1):
                        following, split_after = held(pool, t + 1, NT - 1), held(pool, t + 1, NT)
                        pool.wait_ge(lo_p, split_after)
                        pool.wait_ge(lo_d, split_after)
                        load(following)
                    if not is0(t):
                        last_norm(t - 1, 1 - b)

                def last_norm(t, b):
                    pool.wait_ge(res_arg, t + 1)
                    pool.tensor_tensor(st[b][:, 2, 2:3], st[b][:, 2, 1:2], minus_half[:, 0:1],
                                       ALU.pow).then_inc(res_rstd, 1)

                pool.wait_ge(const_set, 1)
                load(0)
                each_tile(pool, step, True)
                last_norm(NT - 1, 1)

            @block.scalar
            def _(act):
                def front(t, n, b, first):
                    act.wait_ge(o_sum, t + 1)
                    act.activation(o_b[b][:, :], o_f[b][:, :], ACT.Square).then_inc(o_sq, 1)
                    act.wait_ge(gate_in, (t + 1) * 32)
                    if not first:
                        act.wait_ge(out_ps, (t - 1) * 2)
                    act.activation(y_hi[b][:, 0:H, :], y[:, 0:H, :], ACT.Copy).then_inc(hi_p, 1)
                    act.activation(gate[:, :, :], gate[:, :, :], ACT.Silu).then_inc(gate_on, 1)
                    act.wait_ge(gated, (t + 1) * 2)
                    act.activation(y_hi[b][:, H:EK, :], y[:, H:EK, :], ACT.Copy).then_inc(hi_d, 1)

                def back(t, b):
                    act.wait_ge(res, (t + 1) * 2)
                    if not is0(t):
                        act.wait_ge(stored, t * 16)
                    act.activation(done[:, :], x[b][:, :], ACT.Square,
                                   accum_out=st[b][:, 2, 0:1]).then_inc(res_sq, 1)

                for i in range(EK):
                    act.wait_ge(w_loaded[i % len(w_raw)], (i // len(w_raw) + 1) * 16)
                    act.activation(w_hi[:, i, :], w_raw[i % len(w_raw)][:, :], ACT.Copy).then_inc(w_split_hi, 1)

                def step(t, n, b, first):
                    front(t, n, b, first)
                    if not is0(t):
                        back(t - 1, 1 - b)

                each_tile(act, step)
                back(NT - 1, 1)

            @block.vector
            def _(dve):
                dve.memset(minus_half[:, :], -0.5).then_inc(const_set, 1)
                dve.tensor_scalar(qf[:, :, :], sh.rq[:, :, :], float(P) ** -0.5, None, ALU.mult).then_inc(const_set, 1)
                dve.wait_ge(const_set, 2)
                dve.scalar_tensor_tensor(qf2[:, :, :], qf[:, :, :], 1.0 / P, qf[:, :, :], ALU.mult,
                                         ALU.mult).then_inc(const_set, 1)
                dve.wait_ge(const_set, 3)
                dve.wait_ge(const_in, 16)

                def front(t, n, b, first):
                    dve.wait_ge(o_loaded[b], (n + 1) * 32)
                    dve.tensor_tensor(o_f[b][:, :], o_f[b][:, :], o_b[b][:, :], ALU.add).then_inc(o_sum, 1)
                    dve.wait_ge(o_sq, t + 1)
                    dve.tensor_reduce(st[b][:, 3, :], heads(o_b[b][:, :]), AX.X, ALU.add).then_inc(o_stat, 1)
                    dve.wait_ge(o_stat, t * 4 + 1)
                    dve.tensor_tensor(st[b][:, 0, :].unsqueeze(1), st[b][:, 3, :].unsqueeze(1), qf2[:, bass.ds(t, 1), :],
                                      ALU.mult).then_inc(o_stat, 1)
                    dve.wait_ge(o_stat, t * 4 + 2)
                    dve.tensor_scalar(st[b][:, 1, :], st[b][:, 0, :], EPS, None, ALU.add).then_inc(o_stat, 1)
                    dve.wait_ge(o_rstd, t + 1)
                    dve.tensor_tensor(st[b][:, 3, :].unsqueeze(1), st[b][:, 0, :].unsqueeze(1), qf[:, bass.ds(t, 1), :],
                                      ALU.mult).then_inc(o_stat, 1)
                    dve.wait_ge(o_stat, t * 4 + 4)
                    dve.tensor_tensor(heads(o_f[b][:, :]), heads(o_f[b][:, :]),
                                      st[b][:, 3, :].unsqueeze(2).broadcast_to((P, H, P)), ALU.mult).then_inc(o_norm, 1)
                    dve.wait_ge(turned, t + 1)
                    dve.wait_ge(gate_on, t + 1)
                    for n2 in range(2):
                        h = slice(n2 * 4, n2 * 4 + 4)
                        dve.scalar_tensor_tensor(y[:, H + n2 * 4:H + n2 * 4 + 4, :],
                                                 ps[n2][:, :].rearrange("p (h t) -> p h t", h=4),
                                                 sh.cols[:, P + 8:P + 9], gate[:, h, :],
                                                 ALU.mult, ALU.mult).then_inc(gated, 1)
                    dve.wait_ge(hi_d, t + 1)
                    dve.tensor_tensor(y_lo[b][:, H:EK, :], y[:, H:EK, :], y_hi[b][:, H:EK, :].bitcast(F32),
                                      ALU.subtract).then_inc(lo_d, 1)

                def back(t, n, b):
                    dve.wait_ge(x_loaded[b], (n + 1) * 16)
                    for n2 in range(2):
                        dve.wait_ge(out_ps, t * 2 + n2 + 1)
                        c = slice(n2 * TB, (n2 + 1) * TB)
                        dve.tensor_tensor(x[b][:, c], ps[2 + 2 * b + n2][:, :], x[b][:, c], ALU.add).then_inc(res, 1)
                    dve.wait_ge(res_sq, t + 1)
                    dve.tensor_scalar(st[b][:, 2, 1:2], st[b][:, 2, 0:1], 1.0 / D, EPS, ALU.mult,
                                      ALU.add).then_inc(res_arg, 1)
                    dve.wait_ge(res_rstd, t + 1)
                    dve.scalar_tensor_tensor(done[:, :], x[b][:, :], st[b][:, 2, 2:3], fnw[:, :],
                                             ALU.mult, ALU.mult).then_inc(final, 1)

                for i in range(EK):
                    dve.wait_ge(w_split_hi, i + 1)
                    dve.tensor_tensor(w_lo[:, i, :], w_raw[i % len(w_raw)][:, :], w_hi[:, i, :].bitcast(F32),
                                      ALU.subtract).then_inc(w_split, 1)

                def step(t, n, b, first):
                    front(t, n, b, first)
                    if not is0(t):
                        back(t - 1, n - 1 + b, 1 - b)

                each_tile(dve, step)
                back(NT - 1, NT // 2 - 1, 1)

            @block.tensor
            def _(pe):
                def turn(t, b):
                    pe.wait_ge(o_norm, t + 1)
                    if not is0(t):
                        pe.wait_ge(gated, t * 2)
                    for h in range(H):
                        last = pe.transpose(ps[h // 4][:, (h % 4) * P:(h % 4 + 1) * P],
                                            o_f[b][:, h * P:(h + 1) * P], ident)
                    last.then_inc(turned, 1)

                def multiply(t, b, half, early):
                    if half == 0:
                        pe.wait_ge(lo_p, t + 1)
                        pe.wait_ge(lo_d, t + 1)
                        if not early:
                            pe.wait_ge(res, (t - 1) * 2)
                    for k in range(EK):
                        if is0(t) and half == 0:
                            pe.wait_ge(w_split, k + 1)
                        for yp, wp in ((y_hi, w_hi), (y_lo, w_hi), (y_hi, w_lo)):
                            last = pe.matmul(ps[2 + 2 * b + half][:, :], yp[b][:, k, :],
                                             wp[:, k, half * TB:(half + 1) * TB],
                                             start=(k == 0 and yp is y_hi and wp is w_hi),
                                             stop=(k == EK - 1 and wp is w_lo))
                    last.then_inc(out_ps, 1)

                def step(t, n, b, first):
                    if not is0(t):
                        early = first or b == 0 and isinstance(t, int)
                        multiply(t - 1, 1 - b, 0, early)
                    turn(t, b)
                    if not is0(t):
                        multiply(t - 1, 1 - b, 1, True)

                step(0, 0, 0, True)
                step(1, 0, 1, True)
                step(2, 1, 0, False)
                step(3, 1, 1, False)
                with pe.Fori(2, NT // 2) as n:
                    for b in range(2):
                        step(n * 2 + b, n, b, False)
                multiply(NT - 1, 1, 0, False)
                multiply(NT - 1, 1, 1, True)


class Shared:

    def const(self, name):
        return self.consts[:, CL[name][0]:CL[name][1]]

    def late(self, name):
        return self.consts_late[:, CL[name][0] - CN_EARLY:CL[name][1] - CN_EARLY]


def build(nc, a, out):
    with ExitStack() as es:
        sh = Shared()
        sh.es = es
        sb = lambda name, shape, dt=F32: es.enter_context(nc.sbuf_tensor(name, shape, dt))
        sh.ps = [es.enter_context(nc.psum_tensor(f"bank{n}", [P, TB], F32)) for n in range(8)]
        sh.consts = sb("consts_sb", [P, CN_EARLY])
        sh.cols = sb("cols", [P, P + 16])
        sh.ones = sb("ones_col", [P, 1])
        sh.rows = nc.dram_tensor("rows", (R_END, P, SEQ), F32, kind="Internal").ap()
        sh.h_tiles = nc.dram_tensor("h_tiles", (NT, P, KT, P), F32, kind="Internal").ap()
        sh.gc_rows = nc.dram_tensor("gc_rows", (2, NT * H, P), F32, kind="Internal").ap()
        sh.rq = sb("rq", [P, NT, H])
        sh.o_rows = nc.dram_tensor("o_rows", (2, SEQ, H * P), F32, kind="Internal").ap()
        sh.yp_rows = nc.dram_tensor("yp_rows", (POOL_W // P, P, SEQ), F32, kind="Internal").ap()
        with ExitStack() as scope:
            sh.sumsq = scope.enter_context(nc.sbuf_tensor("sumsq", [P, J_V, NT], F32))
            sh.logits = scope.enter_context(nc.sbuf_tensor("logits", [P, NT, 32], F32))
            with ExitStack() as early:
                sh.xh = early.enter_context(nc.sbuf_tensor("xh", [P, KT, SEQ], F32R))
                sh.xl = early.enter_context(nc.sbuf_tensor("xl", [P, KT, SEQ], F32R))
                stage_prepare(nc, a, sh)
                stage_project(nc, a, sh)
            sh.consts_late = scope.enter_context(nc.sbuf_tensor("consts_late", [P, CN - CN_EARLY], F32))
            sh.tables = scope.enter_context(nc.sbuf_tensor("tables", [P, 2, NT, GROUPS, NF, HG], F32))
            stage_gates(nc, a, sh)
            stage_delta(nc, a, sh)
        stage_pool(nc, a, sh)
        stage_output(nc, a, sh, out)


_INS = ["x", "norm_w", "w_in", "pool_w", "pool_scale", "conv_w", "a_log", "dt_bias", "head_norm_w", "w_out",
        "final_norm_w"]


def kernel(**inputs):
    import concourse.bacc as bacc
    from concourse.bass_utils import run_bass_kernel_spmd

    nc = bacc.Bacc("TRN2", target_bir_lowering=False, num_devices=1)
    arrays = {"in_" + name: np.ascontiguousarray(inputs[name]) for name in _INS}
    arrays["in_consts"] = constant_table()
    args = {name[3:]: nc.dram_tensor(name, v.shape, mybir.dt.from_np(v.dtype), kind="ExternalInput").ap()
            for name, v in arrays.items()}
    out = nc.dram_tensor("out_0", (1, SEQ, D), F32, kind="ExternalOutput").ap()
    build(nc, args, out)
    r = run_bass_kernel_spmd(nc, [arrays], core_ids=[0])
    return r.results[0]["out_0"]
```

```python
from contextlib import ExitStack

import numpy as np
import concourse.bass as bass
import concourse.mybir as mybir

F32 = mybir.dt.float32
F32R = mybir.dt.float32r
ACT = mybir.ActivationFunctionType
ALU = mybir.AluOpType
AX = mybir.AxisListType

P = 128
D = 1024
SEQ = 2048
KT = D // P
NT = SEQ // P
TB = 512
NB = SEQ // TB
POOL_W = 1024
H = 8
CONV_K = 5
EPS = 1e-6
OFF_ZP = 1024
OFF_QKV = 2048
OFF_LOGITS = 6144
IN_W = 6176
MIX_W = 2048
WINDOWS = (2, 4, 8, 16)

J_QK, J_V, J_U, J_LG, J_END = 0, 16, 24, 32, 33
R_ZD, R_END = 32, 40
OFF_ZD = 5120
PAD = 8
CW = SEQ + 2 * PAD

LEVELS = (2, 4, 8, 16, 32, 64)
BIG = -1.0e30


def constant_layout():
    at, out = 0, {}
    for name, n in (("ident", P), ("edge", 4 * 2 * PAD), ("tri_f", P), ("tri_b", P), ("ones", P), ("mask_f", P), ("mask_b", P),
                    ("neg1_f", P), ("neg1_b", P), ("level_f", 64 * 2), ("level_b", 64 * 2), ("level_c", 64 * (len(LEVELS) - 2))):
        out[name] = (at, at + n)
        at += n
    return out, at


CL, CN = constant_layout()
CN_EARLY = CL["edge"][1]


def constant_table():
    t = np.zeros((P, CN), np.float32)

    def put(name, a):
        t[:, CL[name][0]:CL[name][1]] = a

    r, c = np.arange(P)[:, None], np.arange(P)[None, :]
    put("ident", r == c)
    put("tri_f", r <= c)
    put("tri_b", r >= c)
    put("ones", 1.0)
    put("mask_f", np.where(c >= r, 0.0, BIG))
    put("mask_b", np.where(c <= r, 0.0, BIG))
    put("neg1_f", -((r % 2 == 0) & (c == r + 1)).astype(np.float32))
    put("neg1_b", -((r % 2 == 1) & (c == r - 1)).astype(np.float32))
    f, b = [], []
    for s in (LEVELS[0], LEVELS[-1]):
        even = np.array([x for x in range(P) if (x // s) % 2 == 0])[None, :]
        odd = np.array([x for x in range(P) if (x // s) % 2 == 1])[None, :]
        f.append(r // s == even // s + 1)
        b.append(r // s == odd // s - 1)
    put("level_f", np.concatenate(f, 1))
    put("level_b", np.concatenate(b, 1))
    c = np.zeros((P, 64 * (len(LEVELS) - 2)), np.float32)
    for n, s in enumerate(LEVELS[1:-1]):
        half = np.arange(64)
        c[0:64, n * 64:(n + 1) * 64] = half[:, None] // s == half[None, :] // s
    put("level_c", c)
    e = np.ones((4, 2, PAD), np.float32)
    for g, w in enumerate(WINDOWS):
        for n in range(PAD):
            for side, tok in ((0, n), (1, SEQ - PAD + n)):
                lo, hi = max(tok - w // 2, 0), min(tok + w // 2 - 1, SEQ - 1)
                e[g, side, n] = w / (hi - lo + 1)
    put("edge", e.reshape(1, -1))
    return t


def stage_prepare(nc, a, sh):
    with ExitStack() as es:
        sb = lambda name, shape, dt=F32: es.enter_context(nc.sbuf_tensor("pr_" + name, shape, dt))
        sem = lambda name: sh.es.enter_context(nc.semaphore("pr_" + name))
        xin = [sb(f"xin{q}", [P, D]) for q in range(4)]
        xs = [sb(f"xs{b}", [P, D]) for b in range(2)]
        ht = [sb(f"ht{b}", [P, KT, P]) for b in range(2)]
        junk = sb("junk", [P, D])
        stat = sb("stat", [P, 2, 4])
        rows = sb("rows", [P, P])
        rows2 = sb("rows2", [16, P])
        eps = sb("eps", [P, 1])
        params_in = sem("params_in")
        x_in = [sem(f"x_in{q}") for q in range(4)]
        h_out = [sem(f"h_out{b}") for b in range(2)]
        x_scaled, norms, rstd = sem("x_scaled"), sem("norms"), sem("rstd")
        x_t, ht_half, hi, lo, cols_t, cols = sem("x_t"), sem("ht_half"), sem("hi"), sem("lo"), sem("cols_t"), sem("cols")
        ps = sh.ps
        ident = sh.const("ident")
        is0 = lambda t: isinstance(t, int) and t == 0

        with nc.Block() as block:
            @block.sync
            def _(sp):
                sp.dma_start(sh.consts[:, :], a["consts"][:, 0:CN_EARLY]).then_inc(params_in, 16)
                sp.dma_start(rows[0:120, :], a["conv_w"].rearrange("o k (t p) -> (o k t) p", p=P)).then_inc(params_in, 16)
                sp.dma_start(rows[120:128, :], a["norm_w"].rearrange("o (t p) -> (o t) p", p=P)).then_inc(params_in, 16)
                sp.dma_start(rows2[0:8, :], a["pool_scale"].rearrange("o (t p) -> (o t) p", p=P)).then_inc(params_in, 16)
                sp.dma_start(rows2[8:9, :], a["head_norm_w"]).then_inc(params_in, 16)

                def store(t, b):
                    sp.wait_ge(ht_half, t * 2 + 2)
                    sp.dma_start(sh.h_tiles[bass.ds(t, 1), :, :, :].rearrange("o p k n -> (o p) k n"),
                                 ht[b][:, :, :]).then_inc(h_out[b], 16)

                for t in range(4):
                    sp.dma_start(xin[t][:, :], a["x"][0, t * P:(t + 1) * P, :]).then_inc(x_in[t], 16)
                with sp.Fori(1, NT // 4) as i:
                    for q in range(4):
                        t = i * 4 + q
                        row, scaled = held(sp, t * P, SEQ - P), held(sp, t - 3, NT)
                        sp.wait_ge(x_scaled, scaled)
                        sp.dma_start(xin[q][:, :], a["x"][0, bass.ds(row, P), :]).then_inc(x_in[q], 16)
                        store(held(sp, t - 4, NT - 5), q % 2)
                for j in range(2):
                    sp.dma_start(sh.w_raw[j][:, :, :], a["w_in"][0, :, OFF_QKV + j * P:OFF_QKV + (j + 1) * P]
                                 .rearrange("(k p) n -> p k n", p=P)).then_inc(sh.w_in_sem[j], 16)
                for t in range(NT - 4, NT):
                    store(t, t % 2)
                for b in range(2):
                    sp.wait_ge(h_out[b], NT // 2 * 16)

            @block.scalar
            def _(act):
                act.wait_ge(cols, 1)

                def front(t, i, q):
                    b = q % 2
                    act.wait_ge(x_in[q], (i + 1) * 16)
                    if not is0(t):
                        act.wait_ge(norms, t * 2)
                    act.activation(junk[:, :], xin[q][:, :], ACT.Square,
                                   accum_out=stat[:, b, 0:1]).then_inc(norms, 1)
                    act.wait_ge(norms, t * 2 + 1)
                    act.activation(stat[:, b, 1:2], stat[:, b, 0:1], ACT.Sqrt, bias=eps[:, :],
                                   scale=1.0 / D).then_inc(norms, 1)

                def scale(t, q, first):
                    act.wait_ge(rstd, t + 1)
                    if not first:
                        act.wait_ge(x_t, t - 1)
                    act.activation(xs[q % 2][:, :], xin[q][:, :], ACT.Copy,
                                   scale=stat[:, q % 2, 2:3]).then_inc(x_scaled, 1)

                def high(t, q):
                    act.wait_ge(ht_half, t * 2 + 2)
                    act.activation(sh.xh[:, :, bass.ds(t * P, P)], ht[q % 2][:, :, :], ACT.Copy).then_inc(hi, 1)

                for t in range(4):
                    front(t, 0, t)
                    if t >= 1:
                        scale(t - 1, t - 1, t < 3)
                    if t >= 2:
                        high(t - 2, t - 2)
                with act.Fori(1, NT // 4) as i:
                    for q in range(4):
                        front(i * 4 + q, i, q)
                        scale(i * 4 + q - 1, (q - 1) % 4, False)
                        high(i * 4 + q - 2, (q - 2) % 4)
                scale(NT - 1, 3, False)
                high(NT - 2, 2)
                high(NT - 1, 3)

            @block.tensor
            def _(pe):
                pe.wait_ge(params_in, 80)
                pe.transpose(ps[4][:, 0:P], rows[:, :], ident).then_inc(cols_t, 1)
                pe.transpose(ps[5][:, 0:9], rows2[0:9, :], ident[0:9, 0:9]).then_inc(cols_t, 1)

                def tile(t, b, first):
                    pe.wait_ge(x_scaled, t + 1)
                    if not first:
                        pe.wait_ge(ht_half, t * 2 - 2)
                    for k in range(KT):
                        last = pe.transpose(ps[2 * b + k // 4][:, (k % 4) * P:(k % 4 + 1) * P],
                                            xs[b][:, k * P:(k + 1) * P], ident)
                    last.then_inc(x_t, 1)

                tile(0, 0, True)
                tile(1, 1, True)
                with pe.Fori(1, NT // 2) as i:
                    tile(i * 2, 0, False)
                    tile(i * 2 + 1, 1, False)

            @block.vector
            def _(dve):
                dve.memset(eps[:, :], EPS).then_inc(cols, 1)
                dve.wait_ge(cols_t, 2)
                dve.tensor_copy(sh.cols[:, 0:P], ps[4][:, 0:P]).then_inc(cols, 1)
                dve.tensor_copy(sh.cols[:, P:P + 9], ps[5][:, 0:9]).then_inc(cols, 1)
                dve.wait_ge(cols, 3)

                def root(t, b):
                    dve.wait_ge(norms, t * 2 + 2)
                    dve.reciprocal(stat[:, b, 2:3], stat[:, b, 1:2]).then_inc(rstd, 1)

                def tile(t, i, b, first):
                    dve.wait_ge(x_t, t + 1)
                    if not first:
                        dve.wait_ge(lo, t - 1)
                        dve.wait_ge(h_out[b], i * 16)
                    for half in range(2):
                        nw = sh.cols[:, 120 + 4 * half:124 + 4 * half].unsqueeze(2).broadcast_to((P, 4, P))
                        dve.tensor_tensor(ht[b][:, 4 * half:4 * half + 4, :],
                                          ps[2 * b + half][:, :].rearrange("p (k t) -> p k t", t=P),
                                          nw, ALU.mult).then_inc(ht_half, 1)

                root(0, 0)
                root(1, 1)
                tile(0, 0, 0, True)
                root(2, 0)
                tile(1, 0, 1, True)
                with dve.Fori(1, NT // 2 - 1) as i:
                    root(i * 2 + 1, 1)
                    tile(i * 2, i, 0, False)
                    root(i * 2 + 2, 0)
                    tile(i * 2 + 1, i, 1, False)
                root(NT - 1, 1)
                tile(NT - 2, NT // 2 - 1, 0, False)
                tile(NT - 1, NT // 2 - 1, 1, False)

            @block.gpsimd
            def _(pool):
                def tile(t, b):
                    pool.wait_ge(hi, t + 1)
                    pool.tensor_tensor(sh.xl[:, :, bass.ds(t * P, P)], ht[b][:, :, :],
                                       sh.xh[:, :, bass.ds(t * P, P)].bitcast(F32), ALU.subtract).then_inc(lo, 1)

                with pool.Fori(0, NT // 2) as i:
                    tile(i * 2, 0)
                    tile(i * 2 + 1, 1)


def held(eng, v, most):
    if isinstance(v, int):
        return v
    reg = eng.alloc_register()
    eng.reg_mov(reg, v)
    return eng.snap(reg, min_val=0, max_val=most)


def tile_columns(j):
    if isinstance(j, int):
        if j >= J_LG:
            return IN_W - P
        if j >= J_U:
            return (j - J_U) * P
        return OFF_QKV + j * P
    raise TypeError(j)


def stage_project(nc, a, sh):
    with ExitStack() as es:
        sb = lambda name, shape, dt=F32: es.enter_context(nc.sbuf_tensor("pj_" + name, shape, dt))
        sem = lambda name: sh.es.enter_context(nc.semaphore("pj_" + name))
        w_raw, w_in_sem = sh.w_raw, sh.w_in_sem
        w_hi = [sb(f"w_hi{b}", [P, KT, P], F32R) for b in range(2)]
        w_lo = [sb(f"w_lo{b}", [P, KT, P], F32R) for b in range(2)]
        row = [sb(f"row{b}", [P, CW]) for b in range(2)]
        acc = [sb(f"acc{b}", [P, CW]) for b in range(2)]
        act_row = [sb(f"act_row{b}", [P, SEQ]) for b in range(2)]
        stored = [sem(f"stored{b}") for b in range(2)]
        hi_done, lo_done, projected, evacuated = sem("hi_done"), sem("lo_done"), sem("projected"), sem("evacuated")
        padded, tap, row_free, silu_done, sq_done = sem("padded"), sem("tap"), sem("row_free"), sem("silu_done"), sem("sq_done")
        ss_done, ss_out = sem("ss_done"), sem("ss_out")
        window = sem("window")
        lg_t = sem("lg_t")
        ps, ident = sh.ps, sh.const("ident")

        segments = [(J_QK, J_V, "qk", 4), (J_V, J_U, "v", 2), (J_U, J_LG, "u", 2), (J_LG, J_END, "lg", 1)]

        def each_tile(eng, step, parts=segments):
            for j0, j1, kind, peel in parts:
                for j in range(j0, j0 + peel):
                    step(j, j // 2, j % 2, j0, kind, j < 2)
                if j1 - j0 > peel:
                    with eng.Fori((j0 + peel) // 2, j1 // 2) as n:
                        step(n * 2, n, 0, j0, kind, False)
                        step(n * 2 + 1, n, 1, j0, kind, False)

        def at(j, n):
            return isinstance(j, int) and j == n

        def columns(j, j0):
            return tile_columns(j0) + (j - j0) * P

        with nc.Block() as block:
            @block.sync
            def _(sp):
                def load(j, pair, b, j0, first):
                    if first:
                        return
                    sp.wait_ge(lo_done, j - 1)
                    w = a["w_in"][0, :, bass.ds(columns(j, j0), P)].rearrange("(k p) n -> p k n", p=P)
                    sp.dma_start(w_raw[b][:, :, :], w).then_inc(w_in_sem[b], 16)

                def store(j, b, kind):
                    if kind in ("qk", "v"):
                        sp.wait_ge(silu_done, j + 1)
                    else:
                        sp.wait_ge(row_free, j - J_U + 1)
                    sp.dma_start(sh.rows[bass.ds(j, 1), :, :].rearrange("o p t -> (o p) t"),
                                 act_row[b][:, :]).then_inc(stored[b], 16)

                def step(j, pair, b, j0, kind, first):
                    load(j, pair, b, j0, first)
                    if not first:
                        before = [s[2] for s in segments if s[0] < j0][-1:] if at(j, j0) or at(j, j0 + 1) else [kind]
                        store(j - 2, b, before[0])

                each_tile(sp, step)
                store(J_LG - 1, 1, "u")
                for b in range(2):
                    sp.wait_ge(stored[b], J_LG // 2 * 16)

            @block.gpsimd
            def _(pool):
                for b in range(2):
                    pool.memset(row[b][:, 0:PAD], 0.0).then_inc(padded, 1)
                    pool.memset(row[b][:, PAD + SEQ:CW], 0.0).then_inc(padded, 1)
                pool.memset(sh.ones[:, :], 1.0).then_inc(padded, 1)

                def step(j, pair, b, j0, kind, first):
                    pool.wait_ge(hi_done, j + 1)
                    pool.tensor_tensor(w_lo[b][:, :, :], w_raw[b][:, :, :], w_hi[b][:, :, :].bitcast(F32),
                                       ALU.subtract).then_inc(lo_done, 1)

                each_tile(pool, step)

            @block.tensor
            def _(pe):
                pe.wait_ge(padded, 5)

                def sums(j, b):
                    pe.wait_ge(sq_done, j + 1)
                    if not (at(j, 0) or at(j, 1)):
                        pe.wait_ge(ss_out, j - 1)
                    for c in range(NT):
                        last = pe.matmul(ps[4 + b][:, c:c + 1], acc[b][:, c * P:(c + 1) * P], sh.ones[:, 0:1],
                                         start=True, stop=True)
                    last.then_inc(ss_done, 1)

                def step(j, pair, b, j0, kind, first):
                    pe.wait_ge(lo_done, j + 1)
                    for t in range(NB):
                        if not at(j, 0):
                            pe.wait_ge(evacuated, j * NB + (t - NB + 1))
                        for k in range(KT):
                            for w, x in ((w_hi, sh.xh), (w_hi, sh.xl), (w_lo, sh.xh)):
                                last = pe.matmul(ps[t][:, :], w[b][:, k, :], x[:, k, t * TB:(t + 1) * TB],
                                                 start=(k == 0 and x is sh.xh and w is w_hi),
                                                 stop=(k == KT - 1 and w is w_lo))
                        last.then_inc(projected, 1)
                        if t == 1:
                            if kind == "qk" and not first:
                                sums(j - 2, b)
                            if kind == "v" and isinstance(j, int):
                                sums(j - 2, b)
                    if kind == "lg":
                        pe.wait_ge(evacuated, (j + 1) * NB)
                        pe.wait_ge(ss_out, J_V)
                        for c in range(NT):
                            last = pe.transpose(ps[4 + c // 4][:, (c % 4) * P:(c % 4 + 1) * P],
                                                act_row[0][:, c * P:(c + 1) * P], ident)
                        last.then_inc(lg_t, 1)

                each_tile(pe, step)

            @block.scalar
            def _(act):
                def split(j, pair, b, first):
                    act.wait_ge(w_in_sem[b], (pair + 1) * 16)
                    if not first:
                        act.wait_ge(projected, (j - 1) * NB)
                    act.activation(w_hi[b][:, :, :], w_raw[b][:, :, :], ACT.Copy).then_inc(hi_done, 1)

                def silu(j, pair, b, kind, first):
                    act.wait_ge(tap, (j + 1) * CONV_K)
                    if not first:
                        act.wait_ge(stored[b], pair * 16)
                    act.activation(act_row[b][:, :], acc[b][:, 0:SEQ], ACT.Silu).then_inc(silu_done, 1)
                    if kind == "qk":
                        act.wait_ge(silu_done, j + 1)
                        act.activation(acc[b][:, 0:SEQ], act_row[b][:, :], ACT.Square).then_inc(sq_done, 1)

                def step(j, pair, b, j0, kind, first):
                    if first and b == 0:
                        split(j, pair, b, True)
                    if not (isinstance(j, int) and j == J_END - 1):
                        split(j + 1, pair + b, 1 - b, first and b == 0)
                    for t in range(NB):
                        act.wait_ge(projected, j * NB + t + 1)
                        if t == 0:
                            if first:
                                pass
                            elif kind in ("qk", "v"):
                                act.wait_ge(tap, (j - 1) * CONV_K)
                            elif kind == "u":
                                if not (at(j, J_U) or at(j, J_U + 1)):
                                    act.wait_ge(row_free, j - J_U - 1)
                            else:
                                act.wait_ge(stored[b], pair * 16)
                        if kind in ("qk", "v", "u"):
                            dst = row[b][:, PAD + t * TB:PAD + (t + 1) * TB]
                        else:
                            dst = act_row[b][:, t * TB:(t + 1) * TB]
                        act.activation(dst, ps[t][:, :], ACT.Copy).then_inc(evacuated, 1)
                    if kind in ("qk", "v") and not at(j, 0) or at(j, J_U):
                        prev = "v" if at(j, J_U) or kind == "v" and not at(j, J_V) else "qk"
                        silu(j - 1, pair - 1 + b, 1 - b, prev, at(j, 1) or at(j, 2))
                    if kind == "lg":
                        act.wait_ge(lg_t, 1)
                        for n in range(4):
                            act.activation(sh.logits[:, 4 * n:4 * n + 4, :],
                                           ps[4 + n][:, :].rearrange("p (c n) -> p c n", n=P)[:, :, 96:128],
                                           ACT.Copy)

                each_tile(act, step)

            @block.vector
            def _(dve):
                dve.wait_ge(padded, 4)

                def conv(j, b):
                    dve.wait_ge(evacuated, (j + 1) * NB)
                    for n in range(CONV_K):
                        src = row[b][:, PAD - CONV_K // 2 + n:PAD - CONV_K // 2 + n + SEQ]
                        w = sh.cols[:, bass.ds(j + 24 * n, 1)]
                        if n:
                            dve.wait_ge(tap, j * CONV_K + n)
                            dve.scalar_tensor_tensor(acc[b][:, 0:SEQ], src, w, acc[b][:, 0:SEQ], ALU.mult,
                                                     ALU.add).then_inc(tap, 1)
                        else:
                            dve.tensor_scalar(acc[b][:, 0:SEQ], src, w, None, ALU.mult).then_inc(tap, 1)

                def sums_out(j, b):
                    dve.wait_ge(ss_done, j + 1)
                    dve.tensor_copy(sh.sumsq[:, bass.ds(j, 1), :],
                                    ps[4 + b][:, 0:NT].unsqueeze(1)).then_inc(ss_out, 1)

                n_window = [0]

                def windows(j, b, g):
                    dve.wait_ge(evacuated, (j + 1) * NB)
                    if j > J_U:
                        dve.wait_ge(row_free, j - J_U)
                    w = WINDOWS[g]
                    src, dst, m = row[b], acc[0], 1
                    n = CW - 1

                    def chained(ins):
                        n_window[0] += 1
                        ins.then_inc(window, 1)
                        dve.wait_ge(window, n_window[0])

                    while m < w:
                        chained(dve.tensor_tensor(dst[:, 0:n], src[:, 0:n], src[:, m:m + n], ALU.add))
                        m *= 2
                        n -= m
                        src, dst = dst, acc[1] if dst is acc[0] else acc[0]
                    at = PAD - w // 2
                    for side, p0 in ((0, at), (1, at + SEQ - PAD)):
                        e0 = CL["edge"][0] + (g * 2 + side) * PAD
                        chained(dve.tensor_tensor(src[:, p0:p0 + PAD], src[:, p0:p0 + PAD],
                                                  sh.consts[:, e0:e0 + PAD], ALU.mult))
                    dve.wait_ge(stored[b], (j // 2) * 16)
                    dve.scalar_tensor_tensor(act_row[b][:, :], src[:, at:at + SEQ], 1.0 / w,
                                             row[b][:, PAD:PAD + SEQ], ALU.mult, ALU.subtract).then_inc(row_free, 1)

                def step(j, pair, b, j0, kind, first):
                    if kind == "v" and not isinstance(j, int):
                        dve.wait_ge(silu_done, j - 1)
                    elif not first:
                        dve.wait_ge(ss_done, j - 1)
                    conv(j, b)
                    if kind == "qk" and not at(j, 0) or at(j, J_V):
                        sums_out(j - 1, 1 - b)

                each_tile(dve, step, segments[:2])
                dve.wait_ge(silu_done, J_U)
                for j in range(J_U, J_LG):
                    windows(j, j % 2, (j - J_U) // 2)

FIELDS = ("neg_gc", "neg_eg", "e_last", "e_to_last", "w", "norm_k")
NF = len(FIELDS)
N_POOL = len(WINDOWS)
PK = POOL_W // N_POOL // P
GROUPS = 2
HG = H // GROUPS


def prefetch_buffers(nc, sh, scope):
    sb = lambda name, shape: scope.enter_context(nc.sbuf_tensor(name, shape, F32))
    sem = lambda name: sh.es.enter_context(nc.semaphore(name))
    sh.qkv = [[sb(f"dl_qkv0_{d}", [P, 3, HG, P]) for d in "fb"]]
    sh.z_raw = sb("dl_z_raw", [P, KT // 2, TB])
    sh.zw = [sb(f"dl_zw{i}", [P, KT, P]) for i in range(2)]
    sh.loaded0 = [sem(f"dl_loaded0_{d}") for d in "fb"]
    sh.zw_in = [sem(f"dl_zw_in{i}") for i in range(2)]
    sh.z_raw_in = sem("dl_z_raw_in")


def prefetch(sp, a, sh):
    for d, at in ((0, 0), (1, NT - 1)):
        for kind in (1, 0, 2):
            sp.dma_start(sh.qkv[0][d][:, kind, :, :],
                         sh.rows[kind * H:kind * H + HG, :, at * P:(at + 1) * P].rearrange("h p t -> p h t")
                         ).then_inc(sh.loaded0[d], 16)
    for i, col in enumerate((OFF_ZP, OFF_ZD)):
        sp.dma_start(sh.zw[i][:, :, :], a["w_in"][0, :, col:col + P].rearrange("(k p) n -> p k n", p=P)
                     ).then_inc(sh.zw_in[i], 16)
    for m in range(TB // P):
        sp.dma_start(sh.z_raw[:, :, m * P:(m + 1) * P], sh.h_tiles[m, :, 0:KT // 2, :]).then_inc(sh.z_raw_in, 16)


def stage_gates(nc, a, sh):
    with ExitStack() as es:
        sb = lambda name, shape, dt=F32: es.enter_context(nc.sbuf_tensor("gt_" + name, shape, dt))
        sem = lambda name: sh.es.enter_context(nc.semaphore("gt_" + name))
        rate = sb("rate", [P, 16])
        dt_b = sb("dt_b", [P, 16])
        half = [P, NT, 16]
        x, mag, z, z2, poly, soft, g = (sb(n, half) for n in ("x", "mag", "z", "z2", "poly", "soft", "g"))
        beta = sb("beta", half)
        nk2, nq2 = sb("nk2", [P, NT, H]), sb("nq2", [P, NT, H])
        nk, nq = sb("nk", [P, NT, H]), sb("nq", [P, NT, H])
        tmp = sb("tmp", [P, NT, H])
        gc_s, gl_s = sb("gc_s", [P, 2, NT, H]), sb("gl_s", [P, 2, NT, H])
        gct = sb("gct", [P, 2, P])
        params_in, more_in, gct_done, gc_stored = sem("params_in"), sem("consts_in"), sem("gct_done"), sem("gc_stored")
        v, s, mm = sem("vector_step"), sem("scalar_step"), sem("sums")
        ps = sh.ps

        def view(dr, field):
            f = FIELDS.index(field)
            return sh.tables[:, dr, :, :, f, :]

        def by_group(ap):
            return ap.rearrange("p c (g h) -> p c g h", g=GROUPS)

        with nc.Block() as block:
            @block.sync
            def _(sp):
                sp.dma_start(sh.consts_late[:, :], a["consts"][:, CN_EARLY:CN]).then_inc(more_in, 16)
                sp.dma_start(rate[:, :], a["a_log"].rearrange("o d h -> o (d h)").broadcast_to((P, 16))).then_inc(params_in, 16)
                sp.dma_start(dt_b[:, :], a["dt_bias"].rearrange("o d h -> o (d h)").broadcast_to((P, 16))).then_inc(params_in, 16)
                prefetch(sp, a, sh)
                sp.wait_ge(gct_done, 2)
                sp.dma_start(sh.gc_rows.rearrange("d n t -> n d t"), gct[:, :, :]).then_inc(gc_stored, 16)
                sp.wait_ge(gc_stored, 16)

            @block.vector
            def _(dve):
                n = [0]

                def then(ins):
                    n[0] += 1
                    ins.then_inc(v, 1)
                    dve.wait_ge(v, n[0])

                tt, ts, stt = dve.tensor_tensor, dve.tensor_scalar, dve.scalar_tensor_tensor
                dve.wait_ge(params_in, 32)
                then(tt(x[:, :, :], sh.logits[:, :, 16:32], dt_b[:, :].unsqueeze(1).broadcast_to((P, NT, 16)), ALU.add))
                then(ts(z[:, :, :], x[:, :, :], -1.0, None, ALU.mult))
                then(tt(mag[:, :, :], x[:, :, :], z[:, :, :], ALU.max))
                then(ts(beta[:, :, :], sh.logits[:, :, 0:16], -80.0, None, ALU.max))
                dve.wait_ge(s, 2)
                then(ts(z[:, :, :], z2[:, :, :], 2.0, None, ALU.add))
                then(dve.reciprocal(z[:, :, :], z[:, :, :]))
                then(tt(z[:, :, :], z2[:, :, :], z[:, :, :], ALU.mult))
                then(tt(z2[:, :, :], z[:, :, :], z[:, :, :], ALU.mult))
                terms = [2.0 / (2 * k + 1) for k in range(8)]
                then(ts(poly[:, :, :], z2[:, :, :], terms[7], terms[6], ALU.mult, ALU.add))
                for k in range(5, -1, -1):
                    then(tt(poly[:, :, :], poly[:, :, :], z2[:, :, :], ALU.mult))
                    then(ts(poly[:, :, :], poly[:, :, :], terms[k], None, ALU.add))
                then(tt(poly[:, :, :], poly[:, :, :], z[:, :, :], ALU.mult))
                then(stt(soft[:, :, :], x[:, :, :], 0.0, poly[:, :, :], ALU.max, ALU.add))
                dve.wait_ge(s, 3)
                then(stt(g[:, :, :], soft[:, :, :], -1.0, rate[:, :].unsqueeze(1).broadcast_to((P, NT, 16)),
                         ALU.mult, ALU.mult))
                sh.g_ready = n[0]
                then(ts(beta[:, :, :], beta[:, :, :], 1.0, None, ALU.add))
                then(dve.reciprocal(beta[:, :, :], beta[:, :, :]))
                then(ts(nk2[:, :, :], sh.sumsq[:, 8:16, :].rearrange("p h c -> p c h"), EPS, None, ALU.add))
                then(ts(nq2[:, :, :], sh.sumsq[:, 0:8, :].rearrange("p h c -> p c h"), EPS, None, ALU.add))
                sh.norms_ready = n[0]
                then(dve.reciprocal(tmp[:, :, :], nk2[:, :, :]))
                for dr in range(2):
                    then(tt(view(dr, "w"), by_group(tmp[:, :, :]), by_group(beta[:, :, dr * H:dr * H + H]), ALU.mult))
                dve.wait_ge(s, 5)
                for dr in range(2):
                    then(dve.tensor_copy(view(dr, "norm_k"), by_group(nk[:, :, :])))
                then(dve.reciprocal(sh.rq[:, :, :], nq[:, :, :]))
                dve.wait_ge(mm, 4)
                for dr in range(2):
                    then(dve.tensor_copy(gc_s[:, dr, :, :], ps[dr][:, 0:P].rearrange("p (c h) -> p c h", h=H)))
                    then(tt(gl_s[:, dr, :, :], ps[2 + dr][:, 0:P].rearrange("p (c h) -> p c h", h=H),
                            gc_s[:, dr, :, :], ALU.subtract))
                    then(ts(view(dr, "neg_gc"), by_group(gc_s[:, dr, :, :]), -1.0, None, ALU.mult))
                sh.sums_ready = n[0]
                for dr in range(2):
                    dve.wait_ge(mm, 5 + dr)
                    dve.tensor_copy(gct[:, dr, :], ps[4 + dr][:, 0:P]).then_inc(gct_done, 1)
                dve.wait_ge(s, 11)
                for dr in range(2):
                    then(ts(view(dr, "neg_eg"), by_group(gc_s[:, dr, :, :]), -1.0, None, ALU.mult))
                    then(dve.tensor_copy(view(dr, "e_last"), by_group(gl_s[:, dr, :, :])))

            @block.scalar
            def _(act):
                act.wait_ge(v, 3)
                act.activation(z2[:, :, :], mag[:, :, :], ACT.Exp, scale=-1.0).then_inc(s, 1)
                act.wait_ge(v, 4)
                act.activation(beta[:, :, :], beta[:, :, :], ACT.Exp, scale=-1.0).then_inc(s, 1)
                act.activation(rate[:, :], rate[:, :], ACT.Exp).then_inc(s, 1)
                act.wait_ge(v, sh.norms_ready)
                act.activation(nk[:, :, :], nk2[:, :, :], ACT.Sqrt).then_inc(s, 1)
                act.activation(nq[:, :, :], nq2[:, :, :], ACT.Sqrt).then_inc(s, 1)
                act.wait_ge(v, sh.sums_ready)
                act.wait_ge(mm, 6)
                for dr in range(2):
                    act.activation(view(dr, "e_to_last"), by_group(gl_s[:, dr, :, :]), ACT.Exp).then_inc(s, 1)
                    act.wait_ge(s, 6 + 3 * dr)
                    act.activation(gc_s[:, dr, :, :], gc_s[:, dr, :, :], ACT.Exp).then_inc(s, 1)
                    act.activation(gl_s[:, dr, :, :], ps[2 + dr][:, 0:P].rearrange("p (c h) -> p c h", h=H),
                                   ACT.Exp).then_inc(s, 1)

            @block.tensor
            def _(pe):
                pe.wait_ge(v, sh.g_ready)
                pe.wait_ge(more_in, 16)
                for dr, tri in ((0, "tri_f"), (1, "tri_b")):
                    gd = g[:, :, dr * H:dr * H + H]
                    pe.matmul(ps[dr][:, 0:P], sh.late(tri), gd, start=True, stop=True).then_inc(mm, 1)
                    pe.matmul(ps[2 + dr][:, 0:P], sh.late("ones"), gd, start=True, stop=True).then_inc(mm, 1)
                pe.wait_ge(v, sh.sums_ready)
                for dr in range(2):
                    pe.transpose(ps[4 + dr][:, 0:P], gc_s[:, dr, :, :].rearrange("p c h -> p (c h)"),
                                 sh.const("ident")).then_inc(mm, 1)


def stage_delta(nc, a, sh):
    with ExitStack() as es:
        sb = lambda name, shape, dt=F32: es.enter_context(nc.sbuf_tensor("dl_" + name, shape, dt))
        sems = lambda name: [sh.es.enter_context(nc.semaphore(f"dl_{name}_{d}")) for d in "fb"]
        quad = [P, HG, P]
        pair = lambda name, shape=quad: [sb(f"{name}_{d}", shape) for d in "fb"]
        pairs = lambda name, shape=quad: [pair(f"{name}{g}", shape) for g in range(GROUPS)]
        qkv = sh.qkv + [pair("qkv1", [P, 3, HG, P])]
        cur = pairs("cur", [P, NF, HG])
        dmat, eb, lt, tm, ost = pair("dmat"), pair("eb"), pair("lt"), pair("tm"), pair("ost")
        at_, xm, kd, vp, qs = pairs("at"), pairs("xm"), pairs("kd"), pairs("vp"), pairs("qs")
        state = pairs("state")
        m_half, m_last = pair("m_half", [P, HG, 64]), pair("m_last")
        t_pack, lt_pack = m_half, pair("lt_pack", [P, HG, 64])
        r, zs = pair("r"), pair("zs")
        z_raw, zw = sh.z_raw, sh.zw
        m_raw, m_hi, m_lo = sb("m_raw", [P, PK, TB]), sb("m_hi", [P, PK, TB], F32R), sb("m_lo", [P, PK, TB], F32R)
        pw_hi, pw_lo = sb("pw_hi", [P, PK, P], F32R), sb("pw_lo", [P, PK, P], F32R)
        pw_raw = sh.sumsq[:, :, :].rearrange("p (k a) b -> p k (a b)", k=PK)
        e_zp = sh.logits[:, :, :].rearrange("p c n -> p (c n)")
        zx = [sb(f"zx_{part}", [P, KT, TB], F32R) for part in ("hi", "lo")]
        zw_hi, zw_lo = ([sb(f"{nm}{i}", [P, KT, P], F32R) for i in range(2)] for nm in ("zw_hi", "zw_lo"))
        z_row = [sb(f"z_row{i}", [P, TB]) for i in range(2)]

        loaded = [sh.loaded0, sems("loaded1")]
        stored = sems("stored")
        sem = lambda name: sh.es.enter_context(nc.semaphore("dl_" + name))
        zw_in = sh.zw_in
        z_stored = [sem(f"z_stored{i}") for i in range(2)]
        z_raw_in = sh.z_raw_in
        zx_hi, zx_lo, zx_ready = map(sem, ("zx_hi", "zx_lo", "zx_ready"))
        m_in, pw_in, pool_hi, pool_lo = map(sem, ("m_in", "pw_in", "pool_hi", "pool_lo"))
        map_ps, e_done, gate_steps, y_done = map(sem, ("map_ps", "e_done", "gate_steps", "y_done"))
        z_hi, z_lo, z_out, z_proj = map(sem, ("z_hi", "z_lo", "z_out", "z_proj"))
        cleared = sems("cleared")
        cur_ready, gc_in, arg_done, eb_done, d_done = map(sems, ("cur_ready", "gc_in", "arg_done", "eb_done", "d_done"))
        kk_ps, kq_ps, kv_ps = map(sems, ("kk_ps", "kq_ps", "kv_ps"))
        t_packed, lt_packed = sems("t_packed"), sems("lt_packed")
        turn_ps, turned = sems("turn_ps"), sems("turned")
        x_steps, at_done = map(sems, ("x_steps", "at_done"))
        kv_out, qs_done = map(sems, ("kv_out", "qs_done"))
        m_ps, m_out, join_ps, joined = map(sems, ("m_ps", "m_out", "join_ps", "joined"))
        ks_ps, r_done, y_ps, zs_done, o_ps, s_ps, o_out, s_done = map(
            sems, ("ks_ps", "r_done", "y_ps", "zs_done", "o_ps", "s_ps", "o_out", "s_done"))
        NL = len(LEVELS)
        ident = sh.const("ident")
        A, B, E, Z = ([sh.ps[4 * d + n] for d in range(2)] for n in range(4))

        def field(g, d, name):
            return cur[g][d][:, FIELDS.index(name), :]

        def scalar(g, d, name, u):
            return cur[g][d][:, FIELDS.index(name), u:u + 1]

        def quads(bank):
            return bank[:, :].rearrange("p (u i) -> p u i", u=HG)

        def blocks(ap, s, odd):
            return ap.rearrange("p u (b two s) -> p u b two s", two=2, s=s)[:, :, :, odd, :]

        def each_step(eng, step, written=(0,)):
            for c0, c1 in zip(written, written[1:] + (NT,)):
                for g in range(GROUPS):
                    step(c0 * 2 + g, c0, g)
                if c1 > c0 + 1:
                    with eng.Fori(c0 + 1, c1) as c:
                        for g in range(GROUPS):
                            step(c * 2 + g, c, g)

        def chunks(eng, c):
            return c, held(eng, NT - 1 - c, NT - 2)

        last_step = lambda n: isinstance(n, int) and n == NT * GROUPS - 1
        early = lambda n: isinstance(n, int) and n < GROUPS

        CB = NT // NB
        HALF = slice(0, P // 2)
        packed = lambda l: 0 < l < NL - 1
        m_rows = lambda l, d: HALF if packed(l) or l == NL - 1 and d == 1 else slice(0, P)
        FILL_PREPARE, FILL_M, FILL_JOIN = (0, 4, 7, 3, 2), (1, 0, 2, 0, 1, 2), (4, 4, 3, 2, 5, 0)
        assert sum(FILL_PREPARE + FILL_M + FILL_JOIN) + 2 * (NL - 2) == 6 * KT
        ZX_HALVES = (slice(0, KT // 2), slice(KT // 2, KT))
        block_at = [0]

        with nc.Block() as block:
            @block.sync
            def _(sp):
                def load(n, at, g, d):
                    if not early(n):
                        sp.wait_ge(ks_ps[d], n - 1)
                        sp.wait_ge(qs_done[d], n - 1)
                    for kind in range(3):
                        sp.dma_start(qkv[g][d][:, kind, :, :],
                                     sh.rows[kind * H + g * HG:kind * H + (g + 1) * HG, :,
                                             bass.ds(at * P, P)].rearrange("h p t -> p h t")
                                     ).then_inc(loaded[g][d], 16)

                def load_gc(n, at, g, d):
                    if not (early(n) and n == 0):
                        sp.wait_ge(at_done[d], n)
                    sp.dma_start(dmat[d][:, :, :].rearrange("p u i -> p (u i)").unsqueeze(1),
                                 sh.gc_rows[d, bass.ds(at * H + g * HG, HG), :].rearrange("u i -> (u i)")
                                 .rearrange("(o q n) -> o q n", o=1, q=1).broadcast_to((P, 1, HG * P))
                                 ).then_inc(gc_in[d], 16)

                def store(n, at, g, d):
                    sp.wait_ge(o_out[d], n + 1)
                    sp.dma_start(sh.o_rows[d, bass.ds(at * P, P), g * HG * P:(g + 1) * HG * P],
                                 ost[d][:, :, :].rearrange("p u e -> p (u e)")).then_inc(stored[d], 16)

                def load_weights(n, c, g, i):
                    sp.wait_ge(z_lo, n * 2 + i - 1)
                    tile = (c - block_at[0] * CB) * GROUPS + g
                    col = (OFF_ZP, OFF_ZD)[i] + tile * P
                    sp.dma_start(zw[i][:, :, :], a["w_in"][0, :, bass.ds(col, P)].rearrange("(k p) n -> p k n", p=P)
                                 ).then_inc(zw_in[i], 16)

                def load_tokens(t, half):
                    for m in range(TB // P):
                        sp.dma_start(z_raw[:, :, m * P:(m + 1) * P],
                                     sh.h_tiles[t * (TB // P) + m, :, half * KT // 2:(half + 1) * KT // 2, :]
                                     ).then_inc(z_raw_in, 16)

                def load_pooled(n, c, g):
                    if not (early(n) and n == 0):
                        sp.wait_ge(pool_lo, c * 3 + 2 * g)
                    group = c - block_at[0] * CB
                    if g == 0:
                        sp.dma_start(m_raw[:, :, :], sh.rows[bass.ds(J_U + group * PK, PK), :,
                                                             block_at[0] * TB:(block_at[0] + 1) * TB]
                                     .rearrange("k p t -> p k t")).then_inc(m_in, 16)
                    sp.dma_start(pw_raw, a["pool_w"][0, bass.ds(group, 1), :, g * P:(g + 1) * P]
                                 .rearrange("o (k p) n -> p (o k) n", p=P)).then_inc(pw_in, 16)

                def step(n, c, g):
                    if isinstance(c, int):
                        block_at[0] = c // CB
                    here = chunks(sp, c)
                    prefetched = early(n) and n == 0
                    for d in range(2):
                        if not prefetched:
                            load(n, here[d], g, d)
                    for d in range(2):
                        load_gc(n, here[d], g, d)
                    for i in range(2):
                        if not prefetched:
                            load_weights(n, c, g, i)
                    load_pooled(n, c, g)
                    if not early(n):
                        before = c - 1, here[1] + 1
                        for d in range(2):
                            store(n - 2, before[d], g, d)
                    if g == 0:
                        if isinstance(c, int):
                            sp.wait_ge(zx_lo, c // CB * 2 + 1)
                            sp.sem_inc(zx_ready, 1)
                            load_tokens(c // CB, 1)
                            sp.wait_ge(zx_lo, c // CB * 2 + 2)
                            sp.sem_inc(zx_ready, 1)
                            if c // CB + 1 < NB:
                                load_tokens(c // CB + 1, 0)
                        else:
                            sp.sem_inc(zx_ready, 2)

                each_step(sp, step, tuple(range(0, NT, CB)))
                for g in range(GROUPS):
                    for d in range(2):
                        store((NT - 1) * 2 + g, (NT - 1, 0)[d], g, d)
                for d in range(2):
                    sp.wait_ge(stored[d], NT * GROUPS * 16)

            @block.gpsimd
            def _(pool):
                for d in range(2):
                    for g in range(GROUPS):
                        pool.memset(state[g][d][:, :, :], 0.0)
                    pool.memset(m_last[d][:, :, :], 0.0).then_inc(cleared[d], 1)

                def step(n, c, g):
                    for d in range(2):
                        pool.wait_ge(eb_done[d], n + 1)
                        pool.wait_ge(loaded[g][d], (c + 1) * 48)
                        if not early(n):
                            pool.wait_ge(o_ps[d], n - 1)
                        pool.tensor_tensor(qs[g][d][:, :, :], qkv[g][d][:, 0, :, :], eb[d][:, :, :],
                                           ALU.mult).then_inc(qs_done[d], 1)
                    split_pooled(c, g)
                    if not last_step(n):
                        split(n + 1, 0)
                    pool.wait_ge(gate_steps, n * 4 + 4)
                    pool.tensor_tensor(z_row[0][:, :], z_row[0][:, :], e_zp, ALU.mult).then_inc(y_done, 1)
                    if not last_step(n):
                        split(n + 1, 1)

                def split_pooled(c, g):
                    if g == 0:
                        pool.wait_ge(pool_hi, c * 3 + 1)
                        pool.tensor_tensor(m_lo[:, :, :], m_raw[:, :, :], m_hi[:, :, :].bitcast(F32),
                                           ALU.subtract).then_inc(pool_lo, 1)
                    pool.wait_ge(pool_hi, c * 3 + 2 + g)
                    pool.tensor_tensor(pw_lo[:, :, :], pw_raw, pw_hi[:, :, :].bitcast(F32),
                                       ALU.subtract).then_inc(pool_lo, 1)

                def split(n, i):
                    pool.wait_ge(z_hi, n * 2 + i + 1)
                    pool.tensor_tensor(zw_lo[i][:, :, :], zw[i][:, :, :], zw_hi[i][:, :, :].bitcast(F32),
                                       ALU.subtract).then_inc(z_lo, 1)

                for i in range(2):
                    split(0, i)
                each_step(pool, step, (0, NT - 1))

            @block.tensor
            def _(pe):
                fill_at = [0]

                def fill(n, c, count):
                    for m in range(fill_at[0], fill_at[0] + count):
                        i, k, p = m // (3 * KT), m % (3 * KT) // 3, m % 3
                        if k == 0 and p == 0:
                            pe.wait_ge(zx_ready, c * 2 + 1)
                            pe.wait_ge(z_lo, n * 2 + i + 1)
                            if not (early(n) and n == 0):
                                if i == 0:
                                    pe.wait_ge(gate_steps, n * 4)
                                else:
                                    pe.wait_ge(z_out, n * 2)
                        if i == 0 and k == KT // 2 and p == 0:
                            pe.wait_ge(zx_ready, c * 2 + 2)
                        w, x = ((zw_hi, zx[0]), (zw_hi, zx[1]), (zw_lo, zx[0]))[p]
                        last = pe.matmul(Z[i][:, :], w[i][:, k, :], x[:, k, :],
                                         start=(k == 0 and p == 0), stop=(k == KT - 1 and p == 2))
                        if k == KT - 1 and p == 2:
                            last.then_inc(z_proj, 1)
                    fill_at[0] = (fill_at[0] + count) % (6 * KT)

                def pool_map(n, c, g):
                    pe.wait_ge(pool_lo, c * 3 + 2 + g)
                    pe.wait_ge(z_out, n * 2 + 1)
                    for k in range(PK):
                        for w, x in ((pw_hi, m_hi), (pw_hi, m_lo), (pw_lo, m_hi)):
                            last = pe.matmul(Z[0][:, :], w[:, k, :], x[:, k, :],
                                             start=(k == 0 and w is pw_hi and x is m_hi),
                                             stop=(k == PK - 1 and w is pw_lo))
                    last.then_inc(map_ps, 1)

                def prepare(n, c, g):
                    for d in range(2):
                        pe.wait_ge(loaded[g][d], (c + 1) * 48)
                        if not (early(n) and n == 0):
                            pe.wait_ge(joined[d], n * NL)
                        for u in range(HG):
                            k = qkv[g][d][:, 1, u, :]
                            last = pe.matmul(quads(B[d])[:, u, :], k, k, start=True, stop=True)
                        last.then_inc(kk_ps[d], 1)
                    fill(n, c, FILL_PREPARE[0])
                    for d in range(2):
                        if not early(n):
                            pe.wait_ge(s_done[d], n - 1)
                        for u in range(HG):
                            last = pe.transpose(quads(E[d])[:, u, :], qkv[g][d][:, 1, u, :], ident)
                        last.then_inc(kv_ps[d], 1)
                    fill(n, c, FILL_PREPARE[1])
                    for d in range(2):
                        if not (early(n) and n == 0):
                            pe.wait_ge(m_out[d], n * NL)
                        for u in range(HG):
                            last = pe.matmul(quads(A[d])[:, u, :], qkv[g][d][:, 1, u, :], qkv[g][d][:, 0, u, :],
                                             start=True, stop=True)
                        last.then_inc(kq_ps[d], 1)
                    fill(n, c, FILL_PREPARE[2])
                    for d in range(2):
                        pe.wait_ge(kv_out[d], n * 2 + 1)
                        for u in range(HG):
                            last = pe.transpose(quads(E[d])[:, u, :], qkv[g][d][:, 2, u, :], ident)
                        last.then_inc(kv_ps[d], 1)
                    fill(n, c, FILL_PREPARE[3])
                    for d in range(2):
                        pe.wait_ge(x_steps[d], n * 3 + 3)
                        for u in range(HG):
                            last = pe.transpose(quads(B[d])[:, u, :], xm[g][d][:, u, :], ident)
                        last.then_inc(turn_ps[d], 1)
                    fill(n, c, FILL_PREPARE[4])

                def level_m(n, g, l):
                    s = LEVELS[l]
                    for d in range(2):
                        if l == 0:
                            pe.wait_ge(turned[d], n * NL + 1)
                            pe.wait_ge(at_done[d], n + 1)
                        else:
                            pe.wait_ge(joined[d], n * NL + l)
                        if packed(l):
                            pe.wait_ge(lt_packed[d], n * (NL - 2) + l)
                        rows = m_rows(l, d)
                        for u in range(HG):
                            n_t = lt_pack[d][:, u, :] if packed(l) else lt[d][:, u, rows]
                            last = pe.matmul(A[d][rows, u * 64:(u + 1) * 64], n_t,
                                             blocks(tm[d][:, :, :], s, d)[:, u], start=True, stop=True)
                        last.then_inc(m_ps[d], 1)

                def level_turn(n, c, l):
                    for d in range(2):
                        pe.wait_ge(joined[d], n * NL + l + 1)
                        if packed(l + 1):
                            pe.wait_ge(t_packed[d], n * (NL - 2) + l + 1)
                            fill(n, c, 1)
                            for u in range(HG):
                                last = pe.transpose(quads(B[d])[HALF, u, :], t_pack[d][:, u, :], ident)
                        else:
                            for u in range(HG):
                                last = pe.transpose(quads(B[d])[:, u, :], tm[d][:, u, :], ident)
                        last.then_inc(turn_ps[d], 1)

                def level_join(n, g, l):
                    s = LEVELS[l]
                    for d in range(2):
                        pe.wait_ge(m_out[d], n * NL + l + 1)
                        pe.wait_ge(turned[d], n * NL + l + 1)
                        rows = HALF if d == 0 else slice(0, P)
                        for u in range(HG):
                            if l < NL - 1:
                                k = m_rows(l, d)
                                last = pe.matmul(B[d][:, u * 64:(u + 1) * 64], xm[g][d][k, u, :],
                                                 m_half[d][k, u, :], start=True, stop=True)
                            else:
                                last = pe.matmul(B[d][rows, u * 64:(u + 1) * 64], m_last[d][:, u, rows],
                                                 blocks(xm[g][d][:, :, :], s, 1 - d)[:, u], start=True, stop=True)
                        last.then_inc(join_ps[d], 1)

                def scan_ks(n, g, final):
                    for d in range(2):
                        if early(n):
                            pe.wait_ge(cleared[d], 1)
                        else:
                            pe.wait_ge(s_done[d], n - 1)
                        if final:
                            pe.wait_ge(s_done[d], n)
                        else:
                            pe.wait_ge(kv_out[d], n * 2 + 4)
                        for u in range(HG):
                            last = pe.matmul(quads(E[d])[:, u, :], qkv[g][d][:, 1, u, :], state[g][d][:, u, :],
                                             start=True, stop=True)
                        last.then_inc(ks_ps[d], 1)

                def scan_y(n, g, final):
                    for d in range(2):
                        pe.wait_ge(r_done[d], n + 1)
                        if final:
                            pe.wait_ge(joined[d], (n + 1) * NL)
                        for u in range(HG):
                            last = pe.matmul(quads(E[d])[:, u, :], xm[g][d][:, u, :], r[d][:, u, :],
                                             start=True, stop=True)
                        last.then_inc(y_ps[d], 1)

                def scan_o(n, g):
                    for d in range(2):
                        pe.wait_ge(zs_done[d], n + 1)
                        pe.wait_ge(qs_done[d], n + 1)
                        for u in range(HG):
                            pe.matmul(quads(E[d])[:, u, :], qs[g][d][:, u, :], state[g][d][:, u, :],
                                      start=True, stop=False)
                            last = pe.matmul(quads(E[d])[:, u, :], at_[g][d][:, u, :], zs[d][:, u, :],
                                             start=False, stop=True)
                        last.then_inc(o_ps[d], 1)

                def scan_s(n, g):
                    for d in range(2):
                        pe.wait_ge(o_out[d], n + 1)
                        for u in range(HG):
                            last = pe.matmul(quads(E[d])[:, u, :], kd[g][d][:, u, :], zs[d][:, u, :],
                                             start=True, stop=True)
                        last.then_inc(s_ps[d], 1)

                def step(n, c, g):
                    scan = not (early(n) and n == 0)
                    prepare(n, c, g)
                    for l in range(NL):
                        level_m(n, g, l)
                        if l:
                            level_turn(n, c, l - 1)
                        if l == 3:
                            pool_map(n, c, g)
                        fill(n, c, FILL_M[l])
                        if scan and l == 0:
                            scan_ks(n - 1, 1 - g, False)
                        if scan and l == 1:
                            scan_y(n - 1, 1 - g, False)
                        if scan and l == 2:
                            scan_o(n - 1, 1 - g)
                        if scan and l == 3:
                            scan_s(n - 1, 1 - g)
                        level_join(n, g, l)
                        fill(n, c, FILL_JOIN[l])

                each_step(pe, step)
                n = NT * GROUPS - 1
                scan_ks(n, 1, True)
                scan_y(n, 1, True)
                scan_o(n, 1)
                scan_s(n, 1)

            @block.scalar
            def _(act):
                def prepare(n, c, g):
                    for d in range(2):
                        act.wait_ge(gc_in[d], (n + 1) * 16)
                        if not (early(n) and n == 0):
                            act.wait_ge(qs_done[d], n)
                        act.activation(eb[d][:, :, :], dmat[d][:, :, :], ACT.Exp).then_inc(eb_done[d], 1)
                    for d in range(2):
                        act.wait_ge(cur_ready[d], n + 1)
                        act.wait_ge(arg_done[d], n + 1)
                        for u in range(HG):
                            last = act.activation(dmat[d][:, u, :], dmat[d][:, u, :], ACT.Exp,
                                                  bias=scalar(g, d, "neg_gc", u))
                        last.then_inc(d_done[d], 1)
                    if g == 0 and isinstance(c, int) and c % CB == 0:
                        split_tokens(c, 1)
                    for d in range(2):
                        act.wait_ge(kv_ps[d], n * 2 + 1)
                        if not early(n):
                            act.wait_ge(s_ps[d], n - 1)
                        for u in range(HG):
                            last = act.activation(kd[g][d][:, u, :], quads(E[d])[:, u, :], ACT.Copy,
                                                  scale=scalar(g, d, "e_to_last", u))
                        last.then_inc(kv_out[d], 1)
                    for d in range(2):
                        act.wait_ge(kv_ps[d], n * 2 + 2)
                        if not early(n):
                            act.wait_ge(r_done[d], n - 1)
                        for u in range(HG):
                            last = act.activation(vp[g][d][:, u, :], quads(E[d])[:, u, :], ACT.Copy,
                                                  scale=scalar(g, d, "norm_k", u))
                        last.then_inc(kv_out[d], 1)
                    for d in range(2):
                        act.wait_ge(turn_ps[d], n * NL + 1)
                        act.activation(tm[d][:, :, :], quads(B[d]), ACT.Copy).then_inc(turned[d], 1)

                def level_turn(n, g, l):
                    if packed(l + 1):
                        for d in range(2):
                            act.wait_ge(joined[d], n * NL + l + 1)
                            s = LEVELS[l + 1]
                            act.activation(t_pack[d][:, :, :].rearrange("p u (b s) -> p u b s", s=s),
                                           blocks(tm[d][:, :, :], s, 1 - d), ACT.Copy).then_inc(t_packed[d], 1)
                    for d in range(2):
                        act.wait_ge(turn_ps[d], n * NL + l + 2)
                        rows = HALF if packed(l + 1) else slice(0, P)
                        act.activation(xm[g][d][rows, :, :], quads(B[d])[rows, :, :], ACT.Copy).then_inc(turned[d], 1)

                def scan_z(n, g):
                    for d in range(2):
                        act.wait_ge(y_ps[d], n + 1)
                        if not (early(n) and n == 0):
                            act.wait_ge(s_ps[d], n)
                        for u in range(HG):
                            last = act.activation(zs[d][:, u, :], quads(E[d])[:, u, :], ACT.Copy,
                                                  scale=scalar(g, d, "w", u))
                        last.then_inc(zs_done[d], 1)

                def scan_out(n, g):
                    for d in range(2):
                        act.wait_ge(o_ps[d], n + 1)
                        if not (early(n) and n == 0):
                            act.wait_ge(stored[d], n * 16)
                        act.activation(ost[d][:, :, :], quads(E[d]), ACT.Copy).then_inc(o_out[d], 1)

                def split_tokens(c, half):
                    act.wait_ge(z_raw_in, (c // CB * 2 + half + 1) * (TB // P) * 16)
                    if c:
                        act.wait_ge(z_proj, c * 2 * GROUPS)
                    act.activation(zx[0][:, ZX_HALVES[half], :], z_raw[:, :, :], ACT.Copy).then_inc(zx_hi, 1)

                def split_pooled(n, c, g):
                    if not (early(n) and n == 0):
                        act.wait_ge(map_ps, n)
                    if g == 0:
                        act.wait_ge(m_in, (c + 1) * 16)
                        act.activation(m_hi[:, :, :], m_raw[:, :, :], ACT.Copy).then_inc(pool_hi, 1)
                    act.wait_ge(pw_in, (n + 1) * 16)
                    act.activation(pw_hi[:, :, :], pw_raw, ACT.Copy).then_inc(pool_hi, 1)

                def split(n, i):
                    act.wait_ge(zw_in[i], (n + 1) * 16)
                    if not (early(n) and n == 0):
                        act.wait_ge(z_proj, n * 2 + i - 1)
                    act.activation(zw_hi[i][:, :, :], zw[i][:, :, :], ACT.Copy).then_inc(z_hi, 1)

                def gate(n, c, g, i):
                    act.wait_ge(z_proj, n * 2 + i + 1)
                    if not (early(n) and n == 0):
                        act.wait_ge(z_stored[i], n * 16)
                    act.activation(z_row[i][:, :], Z[i][:, :], ACT.Copy).then_inc(z_out, 1)
                    if i == 0:
                        act.wait_ge(z_out, n * 2 + 1)
                        if not (early(n) and n == 0):
                            act.wait_ge(y_done, n)
                        act.activation(e_zp, z_row[0][:, :], ACT.Exp, scale=-1.0).then_inc(e_done, 1)
                    if not last_step(n):
                        split(n + 1, i)
                    if i == 1:
                        tokens = slice(block_at[0] * TB, (block_at[0] + 1) * TB)
                        tile = (c - block_at[0] * CB) * GROUPS + g
                        act.wait_ge(z_out, n * 2 + 2)
                        act.dma_start(sh.rows[bass.ds(R_ZD + tile, 1), :, tokens].rearrange("o p t -> (o p) t"),
                                      z_row[1][:, :]).then_inc(z_stored[1], 16)
                        act.wait_ge(y_done, n + 1)
                        act.dma_start(sh.yp_rows[bass.ds(tile, 1), :, tokens].rearrange("o p t -> (o p) t"),
                                      z_row[0][:, :]).then_inc(z_stored[0], 16)

                def step(n, c, g):
                    if isinstance(c, int):
                        block_at[0] = c // CB
                        if g == 0 and c % CB == 0:
                            split_tokens(c, 0)
                    scan = not (early(n) and n == 0)
                    prepare(n, c, g)
                    split_pooled(n, c, g)
                    level_turn(n, g, 0)
                    if scan:
                        scan_z(n - 1, 1 - g)
                    level_turn(n, g, 1)
                    gate(n, c, g, 0)
                    if scan:
                        scan_out(n - 1, 1 - g)
                    for l in range(2, NL - 1):
                        level_turn(n, g, l)
                    gate(n, c, g, 1)

                for i in range(2):
                    split(0, i)
                each_step(act, step, tuple(sorted({*range(0, NT, CB), NT - 1})))
                scan_z(NT * GROUPS - 1, 1)
                scan_out(NT * GROUPS - 1, 1)
                for i in range(2):
                    act.wait_ge(z_stored[i], NT * GROUPS * 16)

            @block.vector
            def _(dve):
                def prepare(n, c, g):
                    here = chunks(dve, c)
                    for d in range(2):
                        if not early(n):
                            dve.wait_ge(zs_done[d], n - 1)
                            dve.wait_ge(s_done[d], n - 1)
                        dve.tensor_copy(cur[g][d][:, :, :].unsqueeze(1),
                                        sh.tables[:, d, bass.ds(here[d], 1), g, :, :]).then_inc(cur_ready[d], 1)
                    for d in range(2):
                        dve.wait_ge(gc_in[d], (n + 1) * 16)
                        dve.wait_ge(eb_done[d], n + 1)
                        mask = sh.late(("mask_f", "mask_b")[d]).unsqueeze(1).broadcast_to((P, HG, P))
                        dve.tensor_tensor(dmat[d][:, :, :], dmat[d][:, :, :], mask, ALU.add).then_inc(arg_done[d], 1)
                    if g == 0 and isinstance(c, int) and c % CB == 0:
                        split_tokens(c, 1)
                    for d in range(2):
                        dve.wait_ge(cur_ready[d], n + 1)
                        dve.wait_ge(d_done[d], n + 1)
                        dve.wait_ge(kk_ps[d], n + 1)
                        for u in range(HG):
                            last = dve.scalar_tensor_tensor(lt[d][:, u, :], quads(B[d])[:, u, :], scalar(g, d, "w", u),
                                                            dmat[d][:, u, :], ALU.mult, ALU.mult)
                        last.then_inc(x_steps[d], 1)
                    for d in range(2):
                        dve.wait_ge(x_steps[d], n * 3 + 1)
                        if not early(n):
                            dve.wait_ge(y_ps[d], n - 1)
                        neg1 = sh.late(("neg1_f", "neg1_b")[d]).unsqueeze(1).broadcast_to((P, HG, P))
                        dve.tensor_tensor(xm[g][d][:, :, :], lt[d][:, :, :], neg1, ALU.mult).then_inc(x_steps[d], 1)
                    for d in range(2):
                        dve.wait_ge(x_steps[d], n * 3 + 2)
                        dve.tensor_tensor(xm[g][d][:, :, :], xm[g][d][:, :, :],
                                          ident.unsqueeze(1).broadcast_to((P, HG, P)), ALU.add).then_inc(x_steps[d], 1)
                    for d in range(2):
                        dve.wait_ge(kq_ps[d], n + 1)
                        if not early(n):
                            dve.wait_ge(o_ps[d], n - 1)
                        dve.tensor_tensor(at_[g][d][:, :, :], quads(A[d]), dmat[d][:, :, :],
                                          ALU.mult).then_inc(at_done[d], 1)

                def level_mask(n, g, l):
                    s = LEVELS[l]
                    for d in range(2):
                        dve.wait_ge(m_ps[d], n * NL + l + 1)
                        if packed(l):
                            dve.wait_ge(turn_ps[d], n * NL + l + 1)
                        rows = m_rows(l, d)
                        if packed(l):
                            c0 = CL["level_c"][0] + (l - 1) * 64
                        else:
                            c0 = CL[("level_f", "level_b")[d]][0] + (0 if l == 0 else 64)
                        c0 -= CN_EARLY
                        mask = sh.consts_late[rows, c0:c0 + 64].rearrange("p (b s) -> p b s", s=s)
                        if l < NL - 1:
                            m = m_half[d][rows, :, :].rearrange("p u (b s) -> p u b s", s=s)
                        else:
                            if early(n) and n == 0:
                                dve.wait_ge(cleared[d], 1)
                            m = blocks(m_last[d][rows, :, :], s, d)
                        dve.tensor_tensor(m, A[d][rows, 0:256].rearrange("p (u b s) -> p u b s", u=HG, s=s),
                                          mask.unsqueeze(1).broadcast_to((rows.stop, HG, 64 // s, s)),
                                          ALU.mult).then_inc(m_out[d], 1)

                def pack(n, l):
                    s = LEVELS[l]
                    for d in range(2):
                        dve.tensor_copy(lt_pack[d][:, :, :].rearrange("p u (b s) -> p u b s", s=s),
                                        blocks(lt[d][:, :, :], s, 1 - d)).then_inc(lt_packed[d], 1)

                def level_update(n, g, l):
                    s = LEVELS[l]
                    for d in range(2):
                        dve.wait_ge(join_ps[d], n * NL + l + 1)
                        rows = slice(0, P)
                        if l < NL - 1:
                            old = blocks(tm[d][:, :, :], s, d)
                        else:
                            rows = HALF if d == 0 else slice(0, P)
                            old = blocks(xm[g][d][rows, :, :], s, 1 - d)
                        dve.tensor_tensor(old, old, B[d][rows, 0:256].rearrange("p (u b s) -> p u b s", u=HG, s=s),
                                          ALU.subtract).then_inc(joined[d], 1)

                def scan_r(n, g):
                    for d in range(2):
                        dve.wait_ge(ks_ps[d], n + 1)
                        if not (early(n) and n == 0):
                            dve.wait_ge(y_ps[d], n)
                        for u in range(HG):
                            last = dve.scalar_tensor_tensor(r[d][:, u, :], quads(E[d])[:, u, :],
                                                            scalar(g, d, "neg_eg", u), vp[g][d][:, u, :],
                                                            ALU.mult, ALU.add)
                        last.then_inc(r_done[d], 1)

                def scan_state(n, g):
                    for d in range(2):
                        dve.wait_ge(s_ps[d], n + 1)
                        for u in range(HG):
                            last = dve.scalar_tensor_tensor(state[g][d][:, u, :], state[g][d][:, u, :],
                                                            scalar(g, d, "e_last", u), quads(E[d])[:, u, :],
                                                            ALU.mult, ALU.add)
                        last.then_inc(s_done[d], 1)

                def split_tokens(c, half):
                    dve.wait_ge(zx_hi, c // CB * 2 + half + 1)
                    part = ZX_HALVES[half]
                    dve.tensor_tensor(zx[1][:, part, :], z_raw[:, :, :], zx[0][:, part, :].bitcast(F32),
                                      ALU.subtract).then_inc(zx_lo, 1)

                def sigmoid(n, half):
                    if half == 0:
                        dve.wait_ge(e_done, n + 1)
                        dve.tensor_scalar(e_zp, e_zp, -BIG, 1.0, ALU.min, ALU.add).then_inc(gate_steps, 1)
                        dve.wait_ge(gate_steps, n * 4 + 1)
                    part = e_zp[:, half * TB // 2:(half + 1) * TB // 2]
                    dve.reciprocal(part, part).then_inc(gate_steps, 1)

                def pooled(n, c, g):
                    tile = (c - block_at[0] * CB) * GROUPS + g
                    dve.wait_ge(map_ps, n + 1)
                    dve.scalar_tensor_tensor(z_row[0][:, :], Z[0][:, :], sh.cols[:, bass.ds(P + tile, 1)], z_row[0][:, :],
                                             ALU.mult, ALU.mult).then_inc(gate_steps, 1)

                def step(n, c, g):
                    if isinstance(c, int):
                        block_at[0] = c // CB
                        if g == 0 and c % CB == 0:
                            split_tokens(c, 0)
                    scan = not (early(n) and n == 0)
                    prepare(n, c, g)
                    for l in range(NL):
                        level_mask(n, g, l)
                        if packed(l + 1):
                            pack(n, l + 1)
                        if l in (2, 3):
                            sigmoid(n, l - 2)
                        if l == 3:
                            pooled(n, c, g)
                        if scan and l == 4:
                            scan_state(n - 1, 1 - g)
                        level_update(n, g, l)
                        if scan and l == 0:
                            scan_r(n - 1, 1 - g)

                each_step(dve, step, tuple(range(0, NT, CB)))
                scan_r(NT * GROUPS - 1, 1)
                scan_state(NT * GROUPS - 1, 1)

EK = MIX_W // P


def stage_output(nc, a, sh, out):
    with ExitStack() as es:
        sb = lambda name, shape, dt=F32: es.enter_context(nc.sbuf_tensor("ou_" + name, shape, dt))
        sem = lambda name: sh.es.enter_context(nc.semaphore("ou_" + name))
        two = lambda name, shape, dt=F32: [sb(f"{name}{b}", shape, dt) for b in range(2)]
        w_hi, w_lo = sb("w_hi", [P, EK, D], F32R), sb("w_lo", [P, EK, D], F32R)
        o_f, o_b, x = two("o_f", [P, D]), two("o_b", [P, D]), two("x", [P, D])
        y, y_hi, y_lo = sb("y", [P, EK, P]), two("y_hi", [P, EK, P], F32R), two("y_lo", [P, EK, P], F32R)
        gate = sb("gate", [P, H, P])
        done = sb("done", [P, D])
        w_raw = [done, x[1], o_f[1], o_b[1]]
        fnw = sb("fnw", [P, D])
        qf, qf2 = sb("qf", [P, NT, H]), sb("qf2", [P, NT, H])
        st = two("st", [P, 4, H])
        minus_half = sb("minus_half", [P, H])
        w_loaded = [sem(f"w_loaded{i}") for i in range(len(w_raw))]
        w_split_hi, w_split = sem("w_split_hi"), sem("w_split")
        o_loaded = [sem(f"o_loaded{b}") for b in range(2)]
        x_loaded = [sem(f"x_loaded{b}") for b in range(2)]
        gate_in, res_arg = sem("gate_in"), sem("res_arg")
        stored = sem("stored")
        const_in, const_set = sem("const_in"), sem("const_set")
        o_sum, o_sq, o_rstd, o_norm = map(sem, ("o_sum", "o_sq", "o_rstd", "o_norm"))
        o_stat = sem("o_stat")
        turned, gated, lo_p, lo_d = map(sem, ("turned", "gated", "lo_p", "lo_d"))
        y_act = sem("y_act")
        out_ps, res, res_sq, res_rstd, final = map(
            sem, ("out_ps", "res", "res_sq", "res_rstd", "final"))
        ps, ident = sh.ps, sh.const("ident")
        heads = lambda ap: ap.rearrange("p (h e) -> p h e", h=H)

        def each_tile(eng, step, peel_last=False):
            for b in range(2):
                step(b, 0, b, True)
            with eng.Fori(1, NT // 2 - peel_last) as n:
                for b in range(2):
                    step(n * 2 + b, n, b, False)
            if peel_last:
                for b in range(2):
                    step(NT - 2 + b, NT // 2 - 1, b, False)

        is0 = lambda t: isinstance(t, int) and t == 0

        with nc.Block() as block:
            @block.sync
            def _(sp):
                sp.dma_start(fnw[:, :], a["final_norm_w"].rearrange("(o n) -> o n", o=1).broadcast_to((P, D))
                             ).then_inc(const_in, 16)

                def load_o(b, row):
                    for dst, d in ((o_f[b], 0), (o_b[b], 1)):
                        sp.dma_start(dst[:, :], sh.o_rows[d, bass.ds(row, P), :]).then_inc(o_loaded[b], 16)

                def load_x(b, row):
                    sp.dma_start(x[b][:, :], a["x"][0, bass.ds(row, P), :]).then_inc(x_loaded[b], 16)

                def store(t):
                    sp.wait_ge(final, t + 1)
                    sp.dma_start(out[0, bass.ds(t * P, P), :], done[:, :]).then_inc(stored, 16)

                load_o(0, 0)
                for i in range(EK):
                    if i >= len(w_raw):
                        sp.wait_ge(w_split, i - len(w_raw) + 1)
                    sp.dma_start(w_raw[i % len(w_raw)][:, :], a["w_out"][0, i * P:(i + 1) * P, :]
                                 ).then_inc(w_loaded[i % len(w_raw)], 16)
                load_x(0, 0)
                sp.wait_ge(w_split, EK)
                load_o(1, P)
                load_x(1, P)
                with sp.Fori(1, NT // 2) as n:
                    for b in range(2):
                        t = n * 2 + b
                        row, turned_before = held(sp, t * P, SEQ - P), held(sp, t - 1, NT)
                        before = held(sp, t - 2, NT - 3)
                        sp.wait_ge(turned, turned_before)
                        load_o(b, row)
                        store(before)
                        load_x(b, row)
                for b in range(2):
                    store(NT - 2 + b)
                sp.wait_ge(stored, NT * 16)

            @block.gpsimd
            def _(pool):
                def load(t):
                    pool.dma_start(y[:, 0:H, :], sh.yp_rows[:, :, bass.ds(t * P, P)].rearrange("k p t -> p k t")
                                   ).then_inc(gate_in, 16)
                    pool.dma_start(gate[:, :, :], sh.rows[R_ZD:R_END, :, bass.ds(t * P, P)].rearrange("k p t -> p k t")
                                   ).then_inc(gate_in, 16)

                def step(t, n, b, first):
                    pool.wait_ge(o_stat, t * 4 + 3)
                    pool.tensor_tensor(st[b][:, 0, :], st[b][:, 1, :], minus_half[:, :], ALU.pow).then_inc(o_rstd, 1)
                    pool.wait_ge(y_act, t * 3 + 1)
                    pool.tensor_tensor(y_lo[b][:, 0:H, :], y[:, 0:H, :], y_hi[b][:, 0:H, :].bitcast(F32),
                                       ALU.subtract).then_inc(lo_p, 1)
                    if not (isinstance(t, int) and t == NT - 1):
                        following, split_after = held(pool, t + 1, NT - 1), held(pool, t + 1, NT)
                        pool.wait_ge(lo_p, split_after)
                        pool.wait_ge(lo_d, split_after)
                        load(following)
                    if not is0(t):
                        last_norm(t - 1, 1 - b)

                def last_norm(t, b):
                    pool.wait_ge(res_arg, t + 1)
                    pool.tensor_tensor(st[b][:, 2, 2:3], st[b][:, 2, 1:2], minus_half[:, 0:1],
                                       ALU.pow).then_inc(res_rstd, 1)

                pool.wait_ge(const_set, 1)
                load(0)
                each_tile(pool, step, True)
                last_norm(NT - 1, 1)

            @block.scalar
            def _(act):
                def front(t, n, b, first):
                    act.wait_ge(o_sum, t + 1)
                    act.activation(o_b[b][:, :], o_f[b][:, :], ACT.Square).then_inc(o_sq, 1)
                    act.wait_ge(gate_in, (t + 1) * 32)
                    if not first:
                        act.wait_ge(out_ps, (t - 1) * 2)
                    act.activation(y_hi[b][:, 0:H, :], y[:, 0:H, :], ACT.Copy).then_inc(y_act, 1)
                    act.activation(gate[:, :, :], gate[:, :, :], ACT.Silu).then_inc(y_act, 1)
                    act.wait_ge(gated, (t + 1) * 2)
                    act.activation(y_hi[b][:, H:EK, :], y[:, H:EK, :], ACT.Copy).then_inc(y_act, 1)

                def back(t, b):
                    act.wait_ge(res, (t + 1) * 2)
                    if not is0(t):
                        act.wait_ge(stored, t * 16)
                    act.activation(done[:, :], x[b][:, :], ACT.Square,
                                   accum_out=st[b][:, 2, 0:1]).then_inc(res_sq, 1)

                def split_w():
                    for i in range(EK):
                        act.wait_ge(w_loaded[i % len(w_raw)], (i // len(w_raw) + 1) * 16)
                        act.activation(w_hi[:, i, :], w_raw[i % len(w_raw)][:, :], ACT.Copy).then_inc(w_split_hi, 1)

                def step(t, n, b, first):
                    front(t, n, b, first)
                    if is0(t):
                        split_w()
                    else:
                        back(t - 1, 1 - b)

                each_tile(act, step)
                back(NT - 1, 1)

            @block.vector
            def _(dve):
                dve.memset(minus_half[:, :], -0.5).then_inc(const_set, 1)
                dve.tensor_scalar(qf[:, :, :], sh.rq[:, :, :], float(P) ** -0.5, None, ALU.mult).then_inc(const_set, 1)
                dve.wait_ge(const_set, 2)
                dve.scalar_tensor_tensor(qf2[:, :, :], qf[:, :, :], 1.0 / P, qf[:, :, :], ALU.mult,
                                         ALU.mult).then_inc(const_set, 1)
                dve.wait_ge(const_set, 3)
                dve.wait_ge(const_in, 16)

                def front(t, n, b, first):
                    dve.wait_ge(o_loaded[b], (n + 1) * 32)
                    dve.tensor_tensor(o_f[b][:, :], o_f[b][:, :], o_b[b][:, :], ALU.add).then_inc(o_sum, 1)
                    dve.wait_ge(o_sq, t + 1)
                    dve.tensor_reduce(st[b][:, 3, :], heads(o_b[b][:, :]), AX.X, ALU.add).then_inc(o_stat, 1)
                    dve.wait_ge(o_stat, t * 4 + 1)
                    dve.tensor_tensor(st[b][:, 0, :].unsqueeze(1), st[b][:, 3, :].unsqueeze(1), qf2[:, bass.ds(t, 1), :],
                                      ALU.mult).then_inc(o_stat, 1)
                    dve.wait_ge(o_stat, t * 4 + 2)
                    dve.tensor_scalar(st[b][:, 1, :], st[b][:, 0, :], EPS, None, ALU.add).then_inc(o_stat, 1)
                    dve.wait_ge(o_rstd, t + 1)
                    dve.tensor_tensor(st[b][:, 3, :].unsqueeze(1), st[b][:, 0, :].unsqueeze(1), qf[:, bass.ds(t, 1), :],
                                      ALU.mult).then_inc(o_stat, 1)
                    dve.wait_ge(o_stat, t * 4 + 4)
                    dve.tensor_tensor(heads(o_f[b][:, :]), heads(o_f[b][:, :]),
                                      st[b][:, 3, :].unsqueeze(2).broadcast_to((P, H, P)), ALU.mult).then_inc(o_norm, 1)
                    dve.wait_ge(turned, t + 1)
                    dve.wait_ge(y_act, t * 3 + 2)
                    for n2 in range(2):
                        h = slice(n2 * 4, n2 * 4 + 4)
                        dve.scalar_tensor_tensor(y[:, H + n2 * 4:H + n2 * 4 + 4, :],
                                                 ps[n2][:, :].rearrange("p (h t) -> p h t", h=4),
                                                 sh.cols[:, P + 8:P + 9], gate[:, h, :],
                                                 ALU.mult, ALU.mult).then_inc(gated, 1)
                    dve.wait_ge(y_act, t * 3 + 3)
                    dve.tensor_tensor(y_lo[b][:, H:EK, :], y[:, H:EK, :], y_hi[b][:, H:EK, :].bitcast(F32),
                                      ALU.subtract).then_inc(lo_d, 1)

                def back(t, n, b):
                    dve.wait_ge(x_loaded[b], (n + 1) * 16)
                    for n2 in range(2):
                        dve.wait_ge(out_ps, t * 2 + n2 + 1)
                        c = slice(n2 * TB, (n2 + 1) * TB)
                        dve.tensor_tensor(x[b][:, c], ps[2 + 2 * b + n2][:, :], x[b][:, c], ALU.add).then_inc(res, 1)
                    dve.wait_ge(res_sq, t + 1)
                    dve.tensor_scalar(st[b][:, 2, 1:2], st[b][:, 2, 0:1], 1.0 / D, EPS, ALU.mult,
                                      ALU.add).then_inc(res_arg, 1)
                    dve.wait_ge(res_rstd, t + 1)
                    dve.scalar_tensor_tensor(done[:, :], x[b][:, :], st[b][:, 2, 2:3], fnw[:, :],
                                             ALU.mult, ALU.mult).then_inc(final, 1)

                def split_w():
                    for i in range(EK):
                        dve.wait_ge(w_split_hi, i + 1)
                        dve.tensor_tensor(w_lo[:, i, :], w_raw[i % len(w_raw)][:, :], w_hi[:, i, :].bitcast(F32),
                                          ALU.subtract).then_inc(w_split, 1)

                def step(t, n, b, first):
                    front(t, n, b, first)
                    if is0(t):
                        split_w()
                    else:
                        back(t - 1, n - 1 + b, 1 - b)

                each_tile(dve, step)
                back(NT - 1, NT // 2 - 1, 1)

            @block.tensor
            def _(pe):
                def turn(t, b):
                    pe.wait_ge(o_norm, t + 1)
                    if not is0(t):
                        pe.wait_ge(gated, t * 2)
                    for h in range(H):
                        last = pe.transpose(ps[h // 4][:, (h % 4) * P:(h % 4 + 1) * P],
                                            o_f[b][:, h * P:(h + 1) * P], ident)
                    last.then_inc(turned, 1)

                def multiply(t, b, half, early, steps=range(EK)):
                    if half == 0:
                        pe.wait_ge(lo_p, t + 1)
                        pe.wait_ge(lo_d, t + 1)
                        if not early:
                            pe.wait_ge(res, (t - 1) * 2)
                    for k in steps:
                        if is0(t) and half == 0:
                            pe.wait_ge(w_split, k + 1)
                        for yp, wp in ((y_hi, w_hi), (y_lo, w_hi), (y_hi, w_lo)):
                            last = pe.matmul(ps[2 + 2 * b + half][:, :], yp[b][:, k, :],
                                             wp[:, k, half * TB:(half + 1) * TB],
                                             start=(k == 0 and yp is y_hi and wp is w_hi),
                                             stop=(k == EK - 1 and wp is w_lo))
                    if EK - 1 in steps:
                        last.then_inc(out_ps, 1)

                def step(t, n, b, first):
                    if not is0(t):
                        early = first or b == 0 and isinstance(t, int)
                        multiply(t - 1, 1 - b, 0, early)
                        cut = 3 * EK // 4 if isinstance(t, int) and t == 1 else EK // 4
                        multiply(t - 1, 1 - b, 1, True, range(0, cut))
                    turn(t, b)
                    if not is0(t):
                        multiply(t - 1, 1 - b, 1, True, range(cut, EK))

                step(0, 0, 0, True)
                step(1, 0, 1, True)
                step(2, 1, 0, False)
                step(3, 1, 1, False)
                with pe.Fori(2, NT // 2) as n:
                    for b in range(2):
                        step(n * 2 + b, n, b, False)
                multiply(NT - 1, 1, 0, False)
                multiply(NT - 1, 1, 1, True)


class Shared:

    def const(self, name):
        return self.consts[:, CL[name][0]:CL[name][1]]

    def late(self, name):
        return self.consts_late[:, CL[name][0] - CN_EARLY:CL[name][1] - CN_EARLY]


def build(nc, a, out):
    with ExitStack() as es:
        sh = Shared()
        sh.es = es
        sb = lambda name, shape, dt=F32: es.enter_context(nc.sbuf_tensor(name, shape, dt))
        sh.ps = [es.enter_context(nc.psum_tensor(f"bank{n}", [P, TB], F32)) for n in range(8)]
        sh.consts = sb("consts_sb", [P, CN_EARLY])
        sh.cols = sb("cols", [P, P + 16])
        sh.ones = sb("ones_col", [P, 1])
        sh.rows = nc.dram_tensor("rows", (R_END, P, SEQ), F32, kind="Internal").ap()
        sh.h_tiles = nc.dram_tensor("h_tiles", (NT, P, KT, P), F32, kind="Internal").ap()
        sh.gc_rows = nc.dram_tensor("gc_rows", (2, NT * H, P), F32, kind="Internal").ap()
        sh.rq = sb("rq", [P, NT, H])
        sh.o_rows = nc.dram_tensor("o_rows", (2, SEQ, H * P), F32, kind="Internal").ap()
        sh.yp_rows = nc.dram_tensor("yp_rows", (POOL_W // P, P, SEQ), F32, kind="Internal").ap()
        with ExitStack() as scope:
            sh.sumsq = scope.enter_context(nc.sbuf_tensor("sumsq", [P, J_V, NT], F32))
            sh.logits = scope.enter_context(nc.sbuf_tensor("logits", [P, NT, 32], F32))
            with ExitStack() as early:
                sh.xh = early.enter_context(nc.sbuf_tensor("xh", [P, KT, SEQ], F32R))
                sh.xl = early.enter_context(nc.sbuf_tensor("xl", [P, KT, SEQ], F32R))
                sh.w_raw = [early.enter_context(nc.sbuf_tensor(f"w_raw{b}", [P, KT, P], F32)) for b in range(2)]
                sh.w_in_sem = [es.enter_context(nc.semaphore(f"w_loaded{b}")) for b in range(2)]
                stage_prepare(nc, a, sh)
                stage_project(nc, a, sh)
            sh.consts_late = scope.enter_context(nc.sbuf_tensor("consts_late", [P, CN - CN_EARLY], F32))
            sh.tables = scope.enter_context(nc.sbuf_tensor("tables", [P, 2, NT, GROUPS, NF, HG], F32))
            prefetch_buffers(nc, sh, scope)
            stage_gates(nc, a, sh)
            stage_delta(nc, a, sh)
        stage_output(nc, a, sh, out)


_INS = ["x", "norm_w", "w_in", "pool_w", "pool_scale", "conv_w", "a_log", "dt_bias", "head_norm_w", "w_out",
        "final_norm_w"]


def kernel(**inputs):
    import concourse.bacc as bacc
    from concourse.bass_utils import run_bass_kernel_spmd

    nc = bacc.Bacc("TRN2", target_bir_lowering=False, num_devices=1)
    arrays = {"in_" + name: np.ascontiguousarray(inputs[name]) for name in _INS}
    arrays["in_consts"] = constant_table()
    args = {name[3:]: nc.dram_tensor(name, v.shape, mybir.dt.from_np(v.dtype), kind="ExternalInput").ap()
            for name, v in arrays.items()}
    out = nc.dram_tensor("out_0", (1, SEQ, D), F32, kind="ExternalOutput").ap()
    build(nc, args, out)
    r = run_bass_kernel_spmd(nc, [arrays], core_ids=[0])
    return r.results[0]["out_0"]
```
